# Optimizing a Trainium2 kernel written in Bass

```python
import math
import jax, jax.numpy as jnp
from jax import lax
import numpy as np

D_MODEL = 1024
BATCH = 1
SEQ = 256
DEPTH = 2

CHUNK = 64
HEAD_DIM = 64
N_SELF_HEADS = 12
N_DIFF_HEADS = 6
N_MEM_HEADS = 4
N_MEM = 256
SELF_WIDTH = N_SELF_HEADS * HEAD_DIM
MEM_WIDTH = N_MEM_HEADS * HEAD_DIM
IN_WIDTH = 3 * SELF_WIDTH + MEM_WIDTH
LEFT_CHUNKS = 8
BAND = (LEFT_CHUNKS + 1) * CHUNK
REL_CLIP = 128
N_REL = 2 * REL_CLIP + 1
Q_BLOCK = 128
D_FF = 2816
ROPE_THETA = 10000.0
EPS = 1e-6
NEG_INF = -1e30
N_MIXERS = 2
N_A_LAYERS = (DEPTH + 1) // 2
N_B_LAYERS = DEPTH // 2


def rmsnorm(x, g):
    x32 = x.astype(jnp.float32)
    y = x32 * lax.rsqrt(jnp.mean(x32 * x32, axis=-1, keepdims=True) + EPS)
    return (y * g.astype(jnp.float32)).astype(x.dtype)

def swiglu(h, w_gate, w_up, w_down):
    return (jax.nn.silu(h @ w_gate) * (h @ w_up)) @ w_down

def rope_tables(positions):
    inv_freq = 1.0 / (ROPE_THETA ** (jnp.arange(0, HEAD_DIM, 2, dtype=jnp.float32) / HEAD_DIM))
    ang = positions.astype(jnp.float32)[..., None] * inv_freq
    return jnp.cos(ang), jnp.sin(ang)

def apply_rope(x, cos, sin):
    x32 = x.astype(jnp.float32)
    x1, x2 = jnp.split(x32, 2, axis=-1)
    return jnp.concatenate([x1 * cos - x2 * sin, x2 * cos + x1 * sin], axis=-1).astype(x.dtype)

def chunked_rel_attention(q, k, v, rel_bias):
    B, S, H, D = q.shape
    n_chunks = S // CHUNK
    pad = ((0, 0), (LEFT_CHUNKS * CHUNK, 0), (0, 0), (0, 0))
    kp = jnp.pad(k, pad)
    vp = jnp.pad(v, pad)
    qi = jnp.arange(CHUNK)[:, None]
    ks = jnp.arange(BAND)[None, :]
    rel = LEFT_CHUNKS * CHUNK + qi - ks
    bias = rel_bias[:, jnp.clip(rel, -REL_CLIP, REL_CLIP) + REL_CLIP].astype(jnp.float32)
    scale = HEAD_DIM ** -0.5
    slot = jnp.arange(BAND)

    def one_chunk(c):
        start = c * CHUNK
        qc = lax.dynamic_slice_in_dim(q, start, CHUNK, axis=1)
        kc = lax.dynamic_slice_in_dim(kp, start, BAND, axis=1)
        vc = lax.dynamic_slice_in_dim(vp, start, BAND, axis=1)
        s = jnp.einsum('bqhd,bkhd->bhqk', qc, kc).astype(jnp.float32) * scale + bias
        valid = slot >= (LEFT_CHUNKS - c) * CHUNK
        s = jnp.where(valid, s, NEG_INF)
        p = jax.nn.softmax(s, axis=-1).astype(v.dtype)
        return jnp.einsum('bhqk,bkhd->bqhd', p, vc)

    out = lax.map(one_chunk, jnp.arange(n_chunks))
    return out.transpose(1, 0, 2, 3, 4).reshape(B, S, H, D)

def diff_attention(q, k, v, lam):
    B, S, H, _, D = q.shape
    n_blocks = S // Q_BLOCK
    scale = D ** -0.5
    k_chunk = jnp.arange(S) // CHUNK
    qb = q.reshape(B, n_blocks, Q_BLOCK, H, 2, D).transpose(1, 0, 2, 3, 4, 5)

    def one_block(args):
        q_blk, b = args
        s = jnp.einsum('bqhcd,bkhcd->bhcqk', q_blk, k).astype(jnp.float32) * scale
        q_chunk = (b * Q_BLOCK + jnp.arange(Q_BLOCK)) // CHUNK
        allowed = k_chunk[None, :] <= q_chunk[:, None]
        s = jnp.where(allowed, s, NEG_INF)
        p = jax.nn.softmax(s, axis=-1)
        a = (p[:, :, 0] - lam * p[:, :, 1]).astype(v.dtype)
        return jnp.einsum('bhqk,bkhe->bqhe', a, v)

    out = lax.map(one_block, (qb, jnp.arange(n_blocks)))
    return out.transpose(1, 0, 2, 3, 4).reshape(B, S, H, v.shape[-1])

def memory_attention(q, k, v):
    s = jnp.einsum('bshd,bnhd->bhsn', q, k).astype(jnp.float32) * (HEAD_DIM ** -0.5)
    p = jax.nn.softmax(s, axis=-1).astype(v.dtype)
    return jnp.einsum('bhsn,bnhd->bshd', p, v)

def first_inputs(seed: int = 0) -> dict:
    key = jax.random.key(seed)
    ks = iter(jax.random.split(key, 40))
    f32 = jnp.float32

    def nrm(shape, scale):
        return jax.random.normal(next(ks), shape, f32) * scale

    def gain(shape):
        return 1.0 + 0.02 * jax.random.normal(next(ks), shape, f32)

    x = nrm((BATCH, SEQ, D_MODEL), 1.0)
    mem = nrm((BATCH, N_MEM, D_MODEL), 1.0)
    offset = jax.random.randint(next(ks), (BATCH, 1), 0, SEQ, dtype=jnp.int32)
    positions = offset + jnp.arange(SEQ, dtype=jnp.int32)[None, :]
    return {
        'x': x,
        'mem': mem,
        'positions': positions,
        'ffn1_norm': gain((DEPTH, D_MODEL)),
        'ffn1_w_gate': nrm((DEPTH, D_MODEL, D_FF), D_MODEL ** -0.5),
        'ffn1_w_up': nrm((DEPTH, D_MODEL, D_FF), D_MODEL ** -0.5),
        'ffn1_w_down': nrm((DEPTH, D_FF, D_MODEL), D_FF ** -0.5),
        'mix_norm': gain((DEPTH, D_MODEL)),
        'mem_norm': gain((DEPTH, D_MODEL)),
        'w_in': nrm((DEPTH, D_MODEL, IN_WIDTH), D_MODEL ** -0.5),
        'w_mem_kv': nrm((DEPTH, D_MODEL, 2 * MEM_WIDTH), D_MODEL ** -0.5),
        'mem_q_norm': gain((DEPTH, HEAD_DIM)),
        'mem_k_norm': gain((DEPTH, HEAD_DIM)),
        'w_out': nrm((DEPTH, SELF_WIDTH + MEM_WIDTH, D_MODEL), (SELF_WIDTH + MEM_WIDTH) ** -0.5),
        'a_q_norm': gain((N_A_LAYERS, HEAD_DIM)),
        'a_k_norm': gain((N_A_LAYERS, HEAD_DIM)),
        'a_rel_bias': nrm((N_A_LAYERS, N_SELF_HEADS, N_REL), 0.1),
        'b_q_norm': gain((N_B_LAYERS, HEAD_DIM)),
        'b_k_norm': gain((N_B_LAYERS, HEAD_DIM)),
        'b_lambda_q1': nrm((N_B_LAYERS, HEAD_DIM), 0.1),
        'b_lambda_k1': nrm((N_B_LAYERS, HEAD_DIM), 0.1),
        'b_lambda_q2': nrm((N_B_LAYERS, HEAD_DIM), 0.1),
        'b_lambda_k2': nrm((N_B_LAYERS, HEAD_DIM), 0.1),
        'b_subln': gain((N_B_LAYERS, 2 * HEAD_DIM)),
        'ffn2_norm': gain((DEPTH, D_MODEL)),
        'ffn2_w_gate': nrm((DEPTH, D_MODEL, D_FF), D_MODEL ** -0.5),
        'ffn2_w_up': nrm((DEPTH, D_MODEL, D_FF), D_MODEL ** -0.5),
        'ffn2_w_down': nrm((DEPTH, D_FF, D_MODEL), D_FF ** -0.5),
    }

def first_block(x, mem, positions, ffn1_norm, ffn1_w_gate, ffn1_w_up, ffn1_w_down,
              mix_norm, mem_norm, w_in, w_mem_kv, mem_q_norm, mem_k_norm, w_out,
              a_q_norm, a_k_norm, a_rel_bias, b_q_norm, b_k_norm,
              b_lambda_q1, b_lambda_k1, b_lambda_q2, b_lambda_k2, b_subln,
              ffn2_norm, ffn2_w_gate, ffn2_w_up, ffn2_w_down):
    B, S, _ = x.shape
    cos, sin = rope_tables(positions)
    cos = cos[:, :, None, None, :]
    sin = sin[:, :, None, None, :]

    for i in range(DEPTH):
        h = rmsnorm(x, ffn1_norm[i])
        x = x + 0.5 * swiglu(h, ffn1_w_gate[i], ffn1_w_up[i], ffn1_w_down[i])

        h = rmsnorm(x, mix_norm[i])
        proj = h @ w_in[i]
        q_s, k_s, v_s, q_m = jnp.split(proj, [SELF_WIDTH, 2 * SELF_WIDTH, 3 * SELF_WIDTH], axis=-1)

        mkv = rmsnorm(mem, mem_norm[i]) @ w_mem_kv[i]
        k_m, v_m = jnp.split(mkv, 2, axis=-1)
        q_m = rmsnorm(q_m.reshape(B, S, N_MEM_HEADS, HEAD_DIM), mem_q_norm[i])
        k_m = rmsnorm(k_m.reshape(B, N_MEM, N_MEM_HEADS, HEAD_DIM), mem_k_norm[i])
        v_m = v_m.reshape(B, N_MEM, N_MEM_HEADS, HEAD_DIM)
        o_m = memory_attention(q_m, k_m, v_m).reshape(B, S, MEM_WIDTH)

        j = i // N_MIXERS
        if i % N_MIXERS == 0:
            q = rmsnorm(q_s.reshape(B, S, N_SELF_HEADS, HEAD_DIM), a_q_norm[j])
            k = rmsnorm(k_s.reshape(B, S, N_SELF_HEADS, HEAD_DIM), a_k_norm[j])
            v = v_s.reshape(B, S, N_SELF_HEADS, HEAD_DIM)
            o_s = chunked_rel_attention(q, k, v, a_rel_bias[j]).reshape(B, S, SELF_WIDTH)
        else:
            lambda_init = 0.8 - 0.6 * math.exp(-0.3 * i)
            q = rmsnorm(q_s.reshape(B, S, N_DIFF_HEADS, 2, HEAD_DIM), b_q_norm[j])
            k = rmsnorm(k_s.reshape(B, S, N_DIFF_HEADS, 2, HEAD_DIM), b_k_norm[j])
            q = apply_rope(q, cos, sin)
            k = apply_rope(k, cos, sin)
            v = v_s.reshape(B, S, N_DIFF_HEADS, 2 * HEAD_DIM)
            lam = (jnp.exp(jnp.sum(b_lambda_q1[j].astype(jnp.float32) * b_lambda_k1[j].astype(jnp.float32)))
                   - jnp.exp(jnp.sum(b_lambda_q2[j].astype(jnp.float32) * b_lambda_k2[j].astype(jnp.float32)))
                   + lambda_init)
            o = diff_attention(q, k, v, lam)
            o = rmsnorm(o, b_subln[j]) * (1.0 - lambda_init)
            o_s = o.reshape(B, S, SELF_WIDTH)

        x = x + jnp.concatenate([o_s, o_m], axis=-1) @ w_out[i]

        h = rmsnorm(x, ffn2_norm[i])
        x = x + 0.5 * swiglu(h, ffn2_w_gate[i], ffn2_w_up[i], ffn2_w_down[i])
    return x


DEPTH_2 = 1

N_MIXERS_2 = 3
N_LAYERS_A = len(range(0, DEPTH_2, N_MIXERS_2))
N_LAYERS_B = len(range(1, DEPTH_2, N_MIXERS_2))
N_LAYERS_C = len(range(2, DEPTH_2, N_MIXERS_2))

DEEPNORM_ALPHA = (2.0 * DEPTH_2) ** 0.25
DEEPNORM_BETA = (8.0 * DEPTH_2) ** -0.25
LN_EPS = 1e-5

A_HEADS = 8
A_HEAD_DIM = D_MODEL // A_HEADS
MOBA_BLOCK = 256
MOBA_TOPK = 3
MOBA_Q_CHUNK = 16
REL_BUCKETS = 32
REL_MAX_DIST = 128

B_GROUPS = 8
B_WIDTH = 2 * D_MODEL
B_CHUNK = 128

C_HEADS = 4
C_KEY_DIM = D_MODEL // 2
C_VAL_DIM = D_MODEL
C_DK = C_KEY_DIM // C_HEADS
C_DV = C_VAL_DIM // C_HEADS
C_GATE_RANK = 16
C_GATE_NORMALIZER = 16.0
C_CHUNK = 64
C_IN_WIDTH = 2 * C_KEY_DIM + 2 * C_VAL_DIM + C_GATE_RANK

N_EXPERTS = 32
TOP_K = 4
D_EXPERT = D_MODEL
SWIGLU_LIMIT = 7.0
SWIGLU_ALPHA = 1.702
MOE_ROW_BLOCK = 128


def layer_norm(x, g, b):
    xf = x.astype(jnp.float32)
    mu = xf.mean(-1, keepdims=True)
    var = jnp.square(xf - mu).mean(-1, keepdims=True)
    y = (xf - mu) * lax.rsqrt(var + LN_EPS) * g.astype(jnp.float32) + b.astype(jnp.float32)
    return y.astype(x.dtype)

def rms_norm(x, g):
    xf = x.astype(jnp.float32)
    return xf * lax.rsqrt(jnp.mean(xf * xf, -1, keepdims=True) + LN_EPS) * g.astype(jnp.float32)

def t5_bucket(rel):
    n = jnp.maximum(rel, 0)
    max_exact = REL_BUCKETS // 2
    nf = jnp.maximum(n, 1).astype(jnp.float32)
    large = max_exact + (jnp.log(nf / max_exact) / math.log(REL_MAX_DIST / max_exact)
                         * (REL_BUCKETS - max_exact)).astype(jnp.int32)
    large = jnp.minimum(large, REL_BUCKETS - 1)
    return jnp.where(n < max_exact, n, large)

def moba_attention(x, w_in, w_out, rel_bias):
    B, S, _ = x.shape
    H, Dh, BLK, QC = A_HEADS, A_HEAD_DIM, MOBA_BLOCK, MOBA_Q_CHUNK
    qkv = (x @ w_in).reshape(B, S, 3, H, Dh)
    q = qkv[:, :, 0].transpose(0, 2, 1, 3)
    k = qkv[:, :, 1].transpose(0, 2, 1, 3)
    v = qkv[:, :, 2].transpose(0, 2, 1, 3)
    nb = -(-S // BLK)
    pad = nb * BLK - S
    kb = jnp.pad(k, ((0, 0), (0, 0), (0, pad), (0, 0))).reshape(B, H, nb, BLK, Dh)
    vb = jnp.pad(v, ((0, 0), (0, 0), (0, pad), (0, 0))).reshape(B, H, nb, BLK, Dh)
    k_mean = kb.astype(jnp.float32).mean(axis=3)
    gate = jnp.einsum('bhsd,bhnd->bhsn', q.astype(jnp.float32), k_mean)
    pos = jnp.arange(S)
    past = jnp.arange(nb)[None, :] < (pos // BLK)[:, None]
    gate = jnp.where(past, gate, -jnp.inf)
    k_sel = min(MOBA_TOPK, nb)
    sel_score, sel_idx = lax.top_k(gate, k_sel)
    sel_valid = jnp.isfinite(sel_score)

    rel_t = rel_bias.T
    bi = jnp.arange(B)[:, None, None, None]
    hi = jnp.arange(H)[None, :, None, None]
    scale = Dh ** -0.5
    offs = jnp.arange(BLK)

    def attend_chunk(t0):
        qc = lax.dynamic_slice_in_dim(q, t0, QC, axis=2)
        idx = lax.dynamic_slice_in_dim(sel_idx, t0, QC, axis=2)
        valid = lax.dynamic_slice_in_dim(sel_valid, t0, QC, axis=2)
        qpos = t0 + jnp.arange(QC)
        kg = kb[bi, hi, idx]
        vg = vb[bi, hi, idx]
        s_sel = jnp.einsum('bhqd,bhqnjd->bhqnj', qc, kg).astype(jnp.float32) * scale
        rel_sel = qpos[None, None, :, None, None] - (idx[..., None] * BLK + offs)
        s_sel = jnp.where(valid[..., None],
                          s_sel + rel_t[hi[..., None], t5_bucket(rel_sel)], -jnp.inf)
        own = t0 // BLK
        ko = lax.dynamic_index_in_dim(kb, own, axis=2, keepdims=False)
        vo = lax.dynamic_index_in_dim(vb, own, axis=2, keepdims=False)
        rel_own = qpos[:, None] - (own * BLK + offs)[None, :]
        s_own = (jnp.einsum('bhqd,bhjd->bhqj', qc, ko).astype(jnp.float32) * scale
                 + rel_t[:, t5_bucket(rel_own)])
        s_own = jnp.where(rel_own >= 0, s_own, -jnp.inf)
        logits = jnp.concatenate([s_sel.reshape(B, H, QC, k_sel * BLK), s_own], axis=-1)
        p = jax.nn.softmax(logits, axis=-1).astype(v.dtype)
        p_sel = p[..., :k_sel * BLK].reshape(B, H, QC, k_sel, BLK)
        p_own = p[..., k_sel * BLK:]
        return (jnp.einsum('bhqnj,bhqnjd->bhqd', p_sel, vg)
                + jnp.einsum('bhqj,bhjd->bhqd', p_own, vo))

    o = lax.map(attend_chunk, jnp.arange(0, S, QC))
    o = o.transpose(1, 0, 3, 2, 4).reshape(B, S, H * Dh)
    return o @ w_out

def gmlp_mixer(x, w_in, ln_g, ln_b, w_s, b_s, w_out):
    B, S, _ = x.shape
    z = jax.nn.gelu(x @ w_in, approximate=False)
    u, v = jnp.split(z, 2, axis=-1)
    v = layer_norm(v, ln_g, ln_b)
    gw = B_WIDTH // B_GROUPS
    vc = v.reshape(B, S // B_CHUNK, B_CHUNK, B_GROUPS, gw)
    ws = w_s * jnp.tril(jnp.ones((B_CHUNK, B_CHUNK), w_s.dtype))
    mixed = jnp.einsum('gts,bcsge->bctge', ws, vc) + b_s.T[None, None, :, :, None]
    y = u * mixed.reshape(B, S, B_WIDTH)
    return y @ w_out

def gla_mixer(x, w_in, w_gk_up, b_gk, norm_g, w_out):
    B, S, _ = x.shape
    proj = x @ w_in
    splits = [C_KEY_DIM, 2 * C_KEY_DIM, 2 * C_KEY_DIM + C_VAL_DIM, 2 * C_KEY_DIM + 2 * C_VAL_DIM]
    q, k, v, g, gk_low = jnp.split(proj, splits, axis=-1)
    log_a = jax.nn.log_sigmoid((gk_low @ w_gk_up + b_gk).astype(jnp.float32)) / C_GATE_NORMALIZER
    nc = S // C_CHUNK

    def heads(t, dh):
        return t.astype(jnp.float32).reshape(B, nc, C_CHUNK, C_HEADS, dh).transpose(1, 0, 3, 2, 4)

    qh = heads(q, C_DK) * (C_DK ** -0.5)
    kh = heads(k, C_DK)
    vh = heads(v, C_DV)
    ah = heads(log_a, C_DK)
    causal = jnp.tril(jnp.ones((C_CHUNK, C_CHUNK), bool))

    def step(state, inp):
        qc, kc, vc, ac = inp
        b = jnp.cumsum(ac, axis=2)
        o_inter = jnp.einsum('bhck,bhkv->bhcv', qc * jnp.exp(b), state)
        diff = b[:, :, :, None, :] - b[:, :, None, :, :]
        diff = jnp.where(causal[None, None, :, :, None], diff, -jnp.inf)
        att = jnp.einsum('bhik,bhjk,bhijk->bhij', qc, kc, jnp.exp(diff))
        o_intra = jnp.einsum('bhij,bhjv->bhiv', att, vc)
        b_last = b[:, :, -1:, :]
        new_state = (jnp.exp(b_last[:, :, 0, :])[..., None] * state
                     + jnp.einsum('bhck,bhcv->bhkv', kc * jnp.exp(b_last - b), vc))
        return new_state, o_inter + o_intra

    state0 = jnp.zeros((B, C_HEADS, C_DK, C_DV), jnp.float32)
    _, o = lax.scan(step, state0, (qh, kh, vh, ah))
    o = o.transpose(1, 0, 3, 2, 4).reshape(B, S, C_HEADS, C_DV)
    o = rms_norm(o, norm_g) * jax.nn.silu(g.reshape(B, S, C_HEADS, C_DV).astype(jnp.float32))
    return o.reshape(B, S, C_VAL_DIM).astype(x.dtype) @ w_out

def moe_ffn(x, w_router, b_router, w_gu, b_gu, w_down, b_down):
    B, S, D = x.shape
    T = B * S
    xt = x.reshape(T, D)
    logits = (xt @ w_router + b_router).astype(jnp.float32)
    top_logit, top_e = lax.top_k(logits, TOP_K)
    gate = jax.nn.softmax(top_logit, axis=-1)
    n_assign = T * TOP_K
    flat_e = top_e.reshape(-1)
    flat_tok = jnp.arange(n_assign) // TOP_K
    order = jnp.argsort(flat_e)
    e_sorted = flat_e[order]
    tok_sorted = flat_tok[order]
    gate_sorted = gate.reshape(-1)[order]
    counts = jnp.zeros((N_EXPERTS,), jnp.int32).at[flat_e].add(1)
    padded = (counts + MOE_ROW_BLOCK - 1) // MOE_ROW_BLOCK * MOE_ROW_BLOCK
    start = jnp.cumsum(counts) - counts
    pend = jnp.cumsum(padded)
    pstart = pend - padded
    dest = pstart[e_sorted] + (jnp.arange(n_assign) - start[e_sorted])
    n_blocks = -(-n_assign // MOE_ROW_BLOCK) + N_EXPERTS
    n_rows = n_blocks * MOE_ROW_BLOCK
    row_tok = jnp.full((n_rows,), T, jnp.int32).at[dest].set(tok_sorted)
    x_pad = jnp.concatenate([xt, jnp.zeros((1, D), xt.dtype)], axis=0)
    xs = x_pad[row_tok].reshape(n_blocks, MOE_ROW_BLOCK, D)
    block_e = jnp.minimum(
        jnp.searchsorted(pend, jnp.arange(n_blocks) * MOE_ROW_BLOCK, side='right'), N_EXPERTS - 1)

    def expert_block(args):
        xb, e = args
        h = xb @ w_gu[e] + b_gu[e]
        h_gate, h_up = jnp.split(h, 2, axis=-1)
        h_gate = jnp.minimum(h_gate, SWIGLU_LIMIT)
        h_up = jnp.clip(h_up, -SWIGLU_LIMIT, SWIGLU_LIMIT)
        act = h_gate * jax.nn.sigmoid(SWIGLU_ALPHA * h_gate) * (h_up + 1.0)
        return act @ w_down[e] + b_down[e]

    ys = lax.map(expert_block, (xs, block_e)).reshape(n_rows, D)
    y_assign = ys[dest] * gate_sorted[:, None].astype(ys.dtype)
    y = jax.ops.segment_sum(y_assign, tok_sorted, num_segments=T)
    return y.reshape(B, S, D)

def second_inputs(seed: int = 0) -> dict:
    key = jax.random.key(seed)
    ks = jax.random.split(key, 23)
    f32 = jnp.float32
    D = D_MODEL

    def nrm(k, shape, scale):
        return jax.random.normal(k, shape, f32) * scale

    return {
        "x": nrm(ks[0], (BATCH, SEQ, D), 1.0),
        "rel_bias": nrm(ks[1], (REL_BUCKETS, A_HEADS), 0.5),
        "a_w_in": nrm(ks[2], (N_LAYERS_A, D, 3 * D), D ** -0.5),
        "a_w_out": nrm(ks[3], (N_LAYERS_A, D, D), D ** -0.5 * DEEPNORM_BETA),
        "b_w_in": nrm(ks[4], (N_LAYERS_B, D, 2 * B_WIDTH), D ** -0.5),
        "b_ln_g": 1.0 + nrm(ks[5], (N_LAYERS_B, B_WIDTH), 0.02),
        "b_ln_b": nrm(ks[6], (N_LAYERS_B, B_WIDTH), 0.02),
        "b_w_s": nrm(ks[7], (N_LAYERS_B, B_GROUPS, B_CHUNK, B_CHUNK), B_CHUNK ** -0.5),
        "b_b_s": 1.0 + nrm(ks[8], (N_LAYERS_B, B_GROUPS, B_CHUNK), 0.02),
        "b_w_out": nrm(ks[9], (N_LAYERS_B, B_WIDTH, D), B_WIDTH ** -0.5 * DEEPNORM_BETA),
        "c_w_in": nrm(ks[10], (N_LAYERS_C, D, C_IN_WIDTH), D ** -0.5),
        "c_w_gk_up": nrm(ks[11], (N_LAYERS_C, C_GATE_RANK, C_KEY_DIM), C_GATE_RANK ** -0.5),
        "c_b_gk": nrm(ks[12], (N_LAYERS_C, C_KEY_DIM), 0.1),
        "c_norm_g": 1.0 + nrm(ks[13], (N_LAYERS_C, C_DV), 0.02),
        "c_w_out": nrm(ks[14], (N_LAYERS_C, C_VAL_DIM, D), C_VAL_DIM ** -0.5 * DEEPNORM_BETA),
        "ln_g": 1.0 + nrm(ks[15], (DEPTH_2, 2, D), 0.02),
        "ln_b": nrm(ks[16], (DEPTH_2, 2, D), 0.02),
        "moe_w_router": nrm(ks[17], (DEPTH_2, D, N_EXPERTS), D ** -0.5),
        "moe_b_router": nrm(ks[18], (DEPTH_2, N_EXPERTS), 0.01),
        "moe_w_gate_up": nrm(ks[19], (DEPTH_2, N_EXPERTS, D, 2 * D_EXPERT), D ** -0.5),
        "moe_b_gate_up": nrm(ks[20], (DEPTH_2, N_EXPERTS, 2 * D_EXPERT), 0.01),
        "moe_w_down": nrm(ks[21], (DEPTH_2, N_EXPERTS, D_EXPERT, D), D_EXPERT ** -0.5 * DEEPNORM_BETA),
        "moe_b_down": nrm(ks[22], (DEPTH_2, N_EXPERTS, D), 0.01),
    }

def second_block(x, rel_bias, a_w_in, a_w_out, b_w_in, b_ln_g, b_ln_b, b_w_s, b_b_s, b_w_out,
              c_w_in, c_w_gk_up, c_b_gk, c_norm_g, c_w_out, ln_g, ln_b,
              moe_w_router, moe_b_router, moe_w_gate_up, moe_b_gate_up, moe_w_down, moe_b_down):
    h = x
    for i in range(DEPTH_2):
        j = i // N_MIXERS_2
        mixer = i % N_MIXERS_2
        if mixer == 0:
            t = moba_attention(h, a_w_in[j], a_w_out[j], rel_bias)
        elif mixer == 1:
            t = gmlp_mixer(h, b_w_in[j], b_ln_g[j], b_ln_b[j], b_w_s[j], b_b_s[j], b_w_out[j])
        else:
            t = gla_mixer(h, c_w_in[j], c_w_gk_up[j], c_b_gk[j], c_norm_g[j], c_w_out[j])
        h = layer_norm(DEEPNORM_ALPHA * h + t, ln_g[i, 0], ln_b[i, 0])
        f = moe_ffn(h, moe_w_router[i], moe_b_router[i], moe_w_gate_up[i], moe_b_gate_up[i],
                    moe_w_down[i], moe_b_down[i])
        h = layer_norm(DEEPNORM_ALPHA * h + f, ln_g[i, 1], ln_b[i, 1])
    return h


def setup_inputs(seed=0):
    out = dict(first_inputs(seed))
    for name, value in second_inputs(seed + 1).items():
        if name != "x":
            out[name + "_2"] = value
    return out


def reference(
    x, mem, positions, ffn1_norm, ffn1_w_gate, ffn1_w_up, ffn1_w_down, mix_norm, mem_norm, w_in,
    w_mem_kv, mem_q_norm, mem_k_norm, w_out, a_q_norm, a_k_norm, a_rel_bias, b_q_norm, b_k_norm,
    b_lambda_q1, b_lambda_k1, b_lambda_q2, b_lambda_k2, b_subln, ffn2_norm, ffn2_w_gate,
    ffn2_w_up, ffn2_w_down, rel_bias_2, a_w_in_2, a_w_out_2, b_w_in_2, b_ln_g_2, b_ln_b_2,
    b_w_s_2, b_b_s_2, b_w_out_2, c_w_in_2, c_w_gk_up_2, c_b_gk_2, c_norm_g_2, c_w_out_2, ln_g_2,
    ln_b_2, moe_w_router_2, moe_b_router_2, moe_w_gate_up_2, moe_b_gate_up_2, moe_w_down_2,
    moe_b_down_2,
):
    x = first_block(
        x, mem, positions, ffn1_norm, ffn1_w_gate, ffn1_w_up, ffn1_w_down, mix_norm, mem_norm,
        w_in, w_mem_kv, mem_q_norm, mem_k_norm, w_out, a_q_norm, a_k_norm, a_rel_bias, b_q_norm,
        b_k_norm, b_lambda_q1, b_lambda_k1, b_lambda_q2, b_lambda_k2, b_subln, ffn2_norm,
        ffn2_w_gate, ffn2_w_up, ffn2_w_down,
    )
    return second_block(
        x, rel_bias_2, a_w_in_2, a_w_out_2, b_w_in_2, b_ln_g_2, b_ln_b_2, b_w_s_2, b_b_s_2,
        b_w_out_2, c_w_in_2, c_w_gk_up_2, c_b_gk_2, c_norm_g_2, c_w_out_2, ln_g_2, ln_b_2,
        moe_w_router_2, moe_b_router_2, moe_w_gate_up_2, moe_b_gate_up_2, moe_w_down_2,
        moe_b_down_2,
    )


_drawn_inputs = setup_inputs


def setup_inputs(seed=0):
    import zlib

    import numpy as np

    out = dict(_drawn_inputs(seed))
    spreads = {}
    factors = {'mem_norm': 6.696,
     'mem_q_norm': 8.0,
     'mem_k_norm': 8.0,
     'a_q_norm': 4.641,
     'a_k_norm': 6.18,
     'b_q_norm': 2.953,
     'b_k_norm': 2.827,
     'b_lambda_k1': 2.8,
     'b_lambda_k2': 2.752,
     'b_subln': 3.146,
     'moe_b_router_2': 2.833,
     'moe_b_gate_up_2': 8.0,
     'moe_b_down_2': 8.0}
    for name, (base, spread) in spreads.items():
        noise = np.random.default_rng([zlib.crc32(name.encode()), seed]).standard_normal(out[name].shape)
        drawn = base * np.exp(spread * noise) if base else spread * noise
        out[name] = __import__('jax').numpy.asarray(drawn.astype(out[name].dtype))
    for name, factor in factors.items():
        out[name] = (out[name] * factor).astype(out[name].dtype)
    return out
```

```python
from contextlib import ExitStack
import math

import numpy as np

import concourse.bass as bass
from concourse import mybir

F32 = mybir.dt.float32
F32R = mybir.dt.float32r
BF16 = mybir.dt.bfloat16
I32 = mybir.dt.int32
ALU = mybir.AluOpType
ACT = mybir.ActivationFunctionType
AX = mybir.AxisListType

P = 128
D = 1024
KT = D // P
TB = 2
S = TB * P
HD = 64
D_FF = 2816
SELF_W = 768
IN_W = 2560
N_E = 32
TOP_K = 4
NEG = -1e30
EPS = 1e-6
LN_EPS = 1e-5
ALPHA = 2.0 ** 0.25
LAMBDA_INIT = 0.8 - 0.6 * math.exp(-0.3)
LIMIT = 7.0
SWIGLU_ALPHA = 1.702

TRIG_STEPS = 20
ROUTE_EXP = 18
LN_STEPS = 12
MOE_LOADS = 16 * 8
PI_BELOW = 3.1415925

CH = 2048
RAW = 6
CUT = 3
AHEAD = 2
LAP = 6

FFN_PAIRS = D_FF // 256
FFN_C = 3 * FFN_PAIRS
KV_C, IN_C, OUT_C = 2, 10, 4
LAYER_C = 2 * FFN_C + KV_C + IN_C + OUT_C
MOBA_IN_C = 12
MOE_C0 = 2 * LAYER_C + MOBA_IN_C + OUT_C
EXPERT_C = 12
REL_W = 384


def is_key(kind, tile):
    return tile >= 8 if kind == "moba" else 6 <= tile < 12 or tile >= 14


def n_diff(groups, n):
    return sum(g["diff"] for g in groups[:n + 1])


def gather_bank(q, par):
    return 2 - 2 * par + (1 - q)


def build(nc, a, out):
    with ExitStack() as ctx:
        sem = lambda name: ctx.enter_context(nc.semaphore(name))

        def sb(name, shape, dt=F32, stack=ctx):
            return stack.enter_context(nc.sbuf_tensor("sb_" + name, shape, dt))

        raw = sb("raw", [P, RAW, CH])
        w_hi = sb("w_hi", [P, CUT, CH], F32R)
        w_lo = sb("w_lo", [P, CUT, CH], F32R)
        x = sb("x", [P, TB, D])
        nat = sb("nat", [P, TB, D])
        ident = sb("ident", [P, P])
        flip = sb("flip", [P, P])
        gcol = sb("gcol", [P, 72])
        grow = sb("grow", [P, P])
        qscale = sb("qscale", [P, 4])
        stat = sb("stat", [P, 16])
        bias_parts = sb("bias_parts", [96, 3 * D], BF16)
        bc = sb("bc", [P, 512])
        inv_row = sb("inv_row", [P, 32])
        pos_i = sb("pos_i", [P, TB], I32)
        pos_f = sb("pos_f", [P, TB])
        trig = sb("trig", [P, TB, 2, 32])
        ang = sb("ang", [P, 5, TB * 32])
        turns_i = sb("turns_i", [P, TB * 32], I32)
        lam = sb("lam", [P, 8])

        early = ExitStack()
        strip = sb("strip", [P, 12, REL_W], stack=early)
        early.close()
        late = ExitStack()
        m_hi = sb("m_hi", [P, KT, P], F32R, late)
        m_lo = sb("m_lo", [P, KT, P], F32R, late)
        y_hi = sb("y_hi", [P, D], F32R, late)
        y_lo = sb("y_lo", [P, D], F32R, late)
        late.close()
        turned_rows = ExitStack()
        xT_hi = sb("xT_hi", [P, KT, S], F32R, turned_rows)
        xT_lo = sb("xT_lo", [P, KT, S], F32R, turned_rows)
        spare = sb("spare", [P, 12 * REL_W - 2 * KT * S], stack=turned_rows)
        ffn = ExitStack()
        a_hi = sb("a_hi", [P, 2, 512], F32R, ffn)
        a_lo = sb("a_lo", [P, 2, 512], F32R, ffn)
        sig = sb("sig", [P, 2, 512], stack=ffn)
        gated = sb("gated", [P, 2, 512], stack=ffn)
        act = sb("act", [P, 2, 512], stack=ffn)
        ffn.close()
        att = ExitStack()
        pr = sb("pr", [P, TB * 3 * D], stack=att)
        qkT = sb("qkT", [P, 16, S], stack=att)
        kvm = sb("kvm", [P, TB, 512], stack=att)
        prob = sb("prob", [P, 2, 4, S], stack=att)
        probT = sb("probT", [P, 4, TB, P], stack=att)
        sums = sb("sums", [P, TB, 32], stack=att)
        soft = sb("soft", [P, 2, 24], stack=att)
        att.close()
        moe, routing = ExitStack(), ExitStack()
        xn_hi = sb("xn_hi", [P, TB, D], F32R, moe)
        xn_lo = sb("xn_lo", [P, TB, D], F32R, moe)
        pick = sb("pick", [P, 2, TB, P], F32R, moe)
        pickT = sb("pickT", [P, S], F32R, moe)
        slot_gate = sb("slot_gate", [P, 2], stack=moe)
        sel = sb("sel", [96, 2, P], BF16, moe)
        gate = sb("gate", [P, TB, 2 * N_E + 2], stack=moe)
        place = sb("place", [P, TB, 2 * N_E + 2], stack=moe)
        ln = sb("ln", [P, 2, 2, D], stack=moe)
        crowd_i = sb("crowd_i", [P, 2], I32, moe)
        masks = sb("masks", [P, 3 * P + 34], stack=moe)
        iota_row, before, ones = masks[:, 0:P], masks[:, P:2 * P], masks[:, 2 * P:3 * P]
        onehot96 = masks[0:96, 3 * P:3 * P + 34]
        wr_hi = sb("wr_hi", [P, KT, N_E], F32R, routing)
        wr_lo = sb("wr_lo", [P, KT, N_E], F32R, routing)
        wr = sb("wr", [P, KT, N_E], stack=routing)
        lg = sb("lg", [P, TB, N_E], stack=routing)
        lg_row = sb("lg_row", [P, N_E], stack=routing)
        tri = sb("tri", [P, N_E, N_E], stack=routing)
        above = sb("above", [P, N_E, N_E], stack=routing)
        equal = sb("equal", [P, N_E, N_E], stack=routing)
        rank = sb("rank", [P, TB, N_E], stack=routing)
        chosen = sb("chosen", [P, TB, N_E], stack=routing)
        crowd = sb("crowd", [P, N_E + 4], stack=routing)
        routing.close()
        xs_hi = sb("xs_hi", [P, KT, P], F32R, moe)
        xs_lo = sb("xs_lo", [P, KT, P], F32R, moe)
        m_g = sb("m_g", [P, 512], stack=moe)
        m_sig = sb("m_sig", [P, 512], stack=moe)
        m_u = sb("m_u", [P, 512], stack=moe)
        m_gu = sb("m_gu", [P, 512], stack=moe)
        m_act = sb("m_act", [P, 2, 512], stack=moe)
        moe.close()
        turned_rows.close()

        ps = ctx.enter_context(nc.psum_tensor("ps", [P, 8, 512], F32))

        qk_flat = qkT[:].rearrange("p a b -> p (a b)")
        rel_rows = probT[:].rearrange("p a b c -> p (a b c)")
        mem = prob[:].rearrange("p a b c -> p (a b c)").rearrange("p (b d) -> p b d", b=TB)
        ext = nc.dram_tensor("ext", (3, 12, 512), F32)

        raw_loaded = [sem(f"raw_loaded{i}") for i in range(RAW)]
        hi_made, lo_made, chunk_used = sem("hi_made"), sem("lo_made"), sem("chunk_used")
        x_loaded, ident_loaded, rows_loaded = sem("x_loaded"), sem("ident_loaded"), sem("rows_loaded")
        small_loaded = sem("small_loaded")
        up_limited = sem("up_limited")
        flip_loaded = sem("flip_loaded")
        bias_loaded, bias_step, bias_made = sem("bias_loaded"), sem("bias_step"), sem("bias_made")
        gcol_turned, gcol_made, qscale_made = sem("gcol_turned"), sem("gcol_made"), sem("qscale_made")
        squared, ms_made, std_made, rstd_made, normed = (sem("squared"), sem("ms_made"), sem("std_made"),
                                                         sem("rstd_made"), sem("normed"))
        turned, turn_hi, turn_lo = sem("turned"), sem("turn_hi"), sem("turn_lo")
        sig_made, gated_made, act_made = sem("sig_made"), sem("gated_made"), sem("act_made")
        act_hi, act_lo = sem("act_hi"), sem("act_lo")
        x_updated = sem("x_updated")
        mem_loaded, proj_read = sem("mem_loaded"), sem("proj_read")
        rel_loaded, ext_turned, ext_rows, ext_made, ext_copied, ext_stored, strip_loaded, strip_ready = (
            sem("rel_loaded"), sem("ext_turned"), sem("ext_rows"), sem("ext_made"), sem("ext_copied"),
            sem("ext_stored"), sem("strip_loaded"), sem("strip_ready"))
        head_sq, head_sum, head_ms, head_std, head_rstd, head_normed = (
            sem("head_sq"), sem("head_sum"), sem("head_ms"), sem("head_std"), sem("head_rstd"),
            sem("head_normed"))
        rope_step = sem("rope_step")
        qk_turned, q_copied, k_copied = sem("qk_turned"), sem("q_copied"), sem("k_copied")
        scored, max_made, prob_made, total_read, mixed, probT_turned, probT_made, pv_done, o_made = (
            sem("scored"), sem("max_made"), sem("prob_made"), sem("total_read"),
            sem("mixed"), sem("probT_turned"), sem("probT_made"), sem("pv_done"), sem("o_made"))
        sub_step, lam_step, lam_exp, trig_step, trig_sin = (sem("sub_step"), sem("lam_step"),
                                                          sem("lam_exp"), sem("trig_step"), sem("trig_sin"))
        ln_step, ln_sq, ln_std = sem("ln_step"), sem("ln_sq"), sem("ln_std")
        moe_loaded, wr_cut, wr_ready, logits_done, route_step, route_exp, crowd_done, crowd_made = (
            sem("moe_loaded"), sem("wr_cut"), sem("wr_ready"), sem("logits_done"), sem("route_step"),
            sem("route_exp"), sem("crowd_done"), sem("crowd_made"))
        xn_hi_made, xn_lo_made = sem("xn_hi_made"), sem("xn_lo_made")
        m_zero, acc_zeroed = sem("m_zero"), sem("acc_zeroed")
        picked, gathered, xs_hi_made, xs_lo_made = (sem("picked"), sem("gathered"), sem("xs_hi_made"),
                                                    sem("xs_lo_made"))
        limited, m_sig_made, m_gu_made, m_act_made = (sem("limited"), sem("m_sig_made"), sem("m_gu_made"),
                                                      sem("m_act_made"))
        m_turned, m_hi_made, m_lo_made, pickT_turned, pickT_made, gate_made = (
            sem("m_turned"), sem("m_hi_made"), sem("m_lo_made"), sem("pickT_turned"), sem("pickT_made"),
            sem("gate_made"))
        y_hi_made, y_lo_made, scattered, last_hi, last_lo, last_scattered = (
            sem("y_hi_made"), sem("y_lo_made"), sem("scattered"), sem("last_hi"),
            sem("last_lo"), sem("last_scattered"))
        out_ready, out_stored = sem("out_ready"), sem("out_stored")

        block = ctx.enter_context(nc.Block())

        c_ffn1 = lambda i: i * LAYER_C
        c_kv = lambda i: i * LAYER_C + FFN_C
        c_in = lambda i: c_kv(i) + KV_C
        c_out = lambda i: c_in(i) + IN_C
        c_ffn2 = lambda i: c_out(i) + OUT_C
        c_moba = 2 * LAYER_C
        c_moba_out = c_moba + MOBA_IN_C
        g_kv, g_in, g_out = (lambda i: 8 * i), (lambda i: 8 * i + 1), (lambda i: 8 * i + 6)
        g_moba, g_moba_out = 16, 22
        u_layer, u_moba = (lambda i: 8 * i), 16
        T_FFN1, T_MEM, T_MIX, T_O, T_FFN2 = range(5)
        t_of = lambda i, which: 5 * i + which
        t_moba, t_moba_o, t_moe = 10, 11, 12
        n_of = lambda i, which: 4 * i + (which if which < 3 else 3)
        gain0 = {T_FFN1: 0, T_MEM: 16, T_MIX: 32, T_FFN2: 48}

        def attention_groups(kind):
            groups = []
            for b in range(TB):
                if kind == "moba":
                    for h0 in (0, 4):
                        groups.append(dict(b=b, qk=[(h, 8 + h, None) for h in range(h0, h0 + 4)],
                                           bias=(h0, 4), dv=P, v=("pr", 2 * D + h0 * P), o=h0 * P, n=4, diff=False))
                    continue
                for h0 in (0, 4, 8):
                    qk = [(h // 2, 6 + h // 2, h % 2) for h in range(h0, h0 + 4)]
                    if kind == "rel":
                        groups.append(dict(b=b, qk=qk, bias=(h0, 4), dv=HD, v=("pr", 2 * SELF_W + h0 * HD),
                                           o=h0 * HD, n=4, diff=False))
                    else:
                        groups.append(dict(b=b, qk=qk, bias=(0, 1), dv=2 * HD, v=("pr", 2 * SELF_W + h0 * HD),
                                           o=h0 * HD, n=2, diff=True))
                groups.append(dict(b=b, qk=[(12 + h // 2, 14 + h // 2, h % 2) for h in range(4)], bias=None,
                                   dv=HD, v=("kvm", 256), o=SELF_W, n=4, diff=False))
            return groups

        def pr_width(kind):
            return 3 * D if kind == "moba" else IN_W

        def pr_view(kind):
            w = pr_width(kind)
            return pr[:, 0:TB * w].rearrange("p (b w) -> p b w", b=TB)

        def row_by_distance(heads):
            return rel_rows[0:heads, 512:1024]

        @block.sync
        def _(sp):
            def load_chunk(c, src, laps=0, shape=None):
                if c >= RAW or not isinstance(laps, int):
                    sp.wait_ge(lo_made, LAP * laps + (c - RAW + 1))
                dst = raw[:, c % RAW, :].rearrange("p (a n) -> p a n", a=shape)
                sp.dma_start(dst, src).then_inc(raw_loaded[c % RAW], 16)

            def ffn_chunks(c0, wg, wu, wd):
                gsrc = lambda w, j: w.rearrange("(k p) f -> p k f", p=P)[:, :, bass.ds(j * 256, 256)]
                dsrc = lambda j: wd.rearrange("(j k p) n -> j p k n", p=P, k=2)[j]
                dsl = lambda j: wd[bass.ds(j * 256, 256), :].rearrange("(k p) n -> p k n", p=P)
                load_chunk(c0, gsrc(wg, 0), shape=KT)
                load_chunk(c0 + 1, gsrc(wu, 0), shape=KT)

                def two_steps(it):
                    for jj in range(2):
                        j = 1 + jj + 2 * it
                        c = c0 + 2 + 3 * jj
                        load_chunk(c, gsrc(wg, j), it, shape=KT)
                        load_chunk(c + 1, gsrc(wu, j), it, shape=KT)
                        load_chunk(c + 2, dsl(j - 1), it, shape=2)

                two_steps(0)
                with sp.Fori(1, (FFN_PAIRS - 1) // 2) as it:
                    two_steps(it)
                load_chunk(c0 + FFN_C - 1, dsl(FFN_PAIRS - 1), shape=2)

            def product_chunks(c0, w, cols):
                for n in range(cols // 512):
                    for h in range(2):
                        src = w[h * 512:(h + 1) * 512, n * 512:(n + 1) * 512].rearrange("(k p) n -> p k n", p=P)
                        load_chunk(c0 + 2 * n + h, src, shape=4)

            def load_strips(n, heads, used):
                sp.wait_ge(ext_copied, n + 1)
                sp.dma_start(ext[n, 0:heads, :], row_by_distance(heads)).then_inc(ext_stored, 16)
                sp.wait_ge(ext_stored, 16 * (n + 1))
                sp.wait_ge(chunk_used, used)
                for h in range(heads):
                    src = bass.AP(ext, (n * 12 + h) * 512, [[1, P], [1, REL_W]])
                    sp.dma_start(strip[:, h, :], src).then_inc(strip_loaded, 16)

            tok = lambda t: t.rearrange("(b p) d -> p b d", p=P)
            rows = lambda v, n: bass.AP(v.tensor, v.offset, [[0, P], [1, n]])
            sp.dma_start(x[:], tok(a["x"][0])).then_inc(x_loaded, 16)
            sp.dma_start(ident[:], a["c_ident"]).then_inc(ident_loaded, 16)
            sp.dma_start(flip[:], a["c_flip"]).then_inc(flip_loaded, 16)
            sp.dma_start(mem, tok(a["mem"][0])).then_inc(mem_loaded, 16)
            for n, name in enumerate(("ffn1_norm", "mem_norm", "mix_norm", "ffn2_norm")):
                for i in range(2):
                    r = 16 * n + 8 * i
                    sp.dma_start(grow[r:r + 8, :], a[name][i].rearrange("(k p) -> k p", p=P)).then_inc(rows_loaded, 16)
            for h in range(2):
                cols = slice(h * HD, (h + 1) * HD)
                for r, name, n in ((64, "mem_q_norm", 2), (66, "mem_k_norm", 2), (68, "a_q_norm", 1),
                                   (69, "a_k_norm", 1)):
                    sp.dma_start(grow[r:r + n, cols], a[name]).then_inc(rows_loaded, 16)
            for r in range(3):
                sp.dma_start(qk_flat[32 * r:32 * r + 32, 0:2 * D], a["moe_b_gate_up_2"][0]).then_inc(bias_loaded, 16)
                sp.dma_start(qk_flat[32 * r:32 * r + 32, 2 * D:3 * D], a["moe_b_down_2"][0]).then_inc(bias_loaded, 16)
            for n, name in enumerate(("b_lambda_q1", "b_lambda_k1", "b_lambda_q2", "b_lambda_k2", "b_q_norm",
                                      "b_k_norm")):
                sp.dma_start(bc[:, HD * n:HD * (n + 1)], rows(a[name][0], HD)).then_inc(small_loaded, 16)
            sp.dma_start(bc[:, 384:512], rows(a["b_subln"][0], P)).then_inc(small_loaded, 16)
            sp.dma_start(inv_row[:], rows(a["c_inv_freq"], 32)).then_inc(small_loaded, 16)
            with nc.allow_non_contiguous_dma(reason="256 positions, one per partition"):
                sp.dma_start(pos_i[:], a["positions"][0].rearrange("(b p) -> p b", p=P)).then_inc(small_loaded, 16)

            for i in range(2):
                ffn_chunks(c_ffn1(i), a["ffn1_w_gate"][i], a["ffn1_w_up"][i], a["ffn1_w_down"][i])
                if i == 0:
                    sp.wait_ge(bias_made, 1)
                    sp.dma_start(qk_flat[:, 0:4 * S], a["c_rel"]).then_inc(rel_loaded, 16)
                    sp.dma_start(rel_rows[0:12, 0:257], a["a_rel_bias"][0]).then_inc(rel_loaded, 16)
                product_chunks(c_kv(i), a["w_mem_kv"][i], 512)
                product_chunks(c_in(i), a["w_in"][i], IN_W)
                product_chunks(c_out(i), a["w_out"][i], D)
                if i == 0:
                    load_strips(0, 12, c_out(0))
                    sp.wait_ge(o_made, u_layer(1))
                    sp.dma_start(mem, tok(a["mem"][0])).then_inc(mem_loaded, 16)
                ffn_chunks(c_ffn2(i), a["ffn2_w_gate"][i], a["ffn2_w_up"][i], a["ffn2_w_down"][i])
            sp.wait_ge(o_made, u_moba)
            sp.dma_start(qk_flat[0:32, 0:2 * S], a["c_t5"]).then_inc(rel_loaded, 16)
            sp.dma_start(rel_rows[0:32, 0:8], a["rel_bias_2"]).then_inc(rel_loaded, 16)
            product_chunks(c_moba, a["a_w_in_2"][0], 3 * D)
            product_chunks(c_moba_out, a["a_w_out_2"][0], D)
            load_strips(1, 8, c_moba_out)
            sp.wait_ge(o_made, u_moba + 4)
            sp.dma_start(masks[:], a["c_masks"]).then_inc(moe_loaded, 16)
            for n in range(2):
                sp.dma_start(ln[:, n, 0, :], rows(a["ln_g_2"][0, n], D)).then_inc(moe_loaded, 16)
                sp.dma_start(ln[:, n, 1, :], rows(a["ln_b_2"][0, n], D)).then_inc(moe_loaded, 16)
            sp.dma_start(wr[:], a["moe_w_router_2"][0].rearrange("(k p) e -> p k e", p=P)).then_inc(moe_loaded, 16)
            sp.dma_start(lg_row[:], rows(a["moe_b_router_2"][0], N_E)).then_inc(moe_loaded, 16)
            sp.dma_start(tri[:].rearrange("p a b -> p (a b)"), rows(a["c_tri"], N_E * N_E)).then_inc(moe_loaded, 16)

            def expert_chunk(e, n, c, laps):
                if n < 8:
                    col = (n // 4) * 512 + ((n // 2) % 2) * D
                    h = n % 2
                    w = a["moe_w_gate_up_2"][0]
                else:
                    col = ((n - 8) % 2) * 512
                    h = (n - 8) // 2
                    w = a["moe_w_down_2"][0]
                src = w[bass.ds(e, 1), h * 512:(h + 1) * 512, col:col + 512].rearrange("e (k p) n -> p (e k) n", p=P)
                load_chunk(c, src, laps, shape=4)

            def expert_loads(c0):
                with sp.Fori(0, N_E // 2 - 1) as it:
                    for n in range(2, 2 + 2 * EXPERT_C):
                        expert_chunk(2 * it + n // EXPERT_C, n % EXPERT_C, c0 + n, 4 * it)
                c = c0 + (N_E - 2) * EXPERT_C
                for n in range(2, 2 + 2 * EXPERT_C):
                    expert_chunk((N_E - 2 + n // EXPERT_C) % N_E, n % EXPERT_C, c + n, 0)

            for n in range(2):
                expert_chunk(0, n, MOE_C0 + n, 0)
            expert_loads(MOE_C0)
            sp.wait_ge(crowd_made, 1)
            more = sp.value_load(crowd_i[0:1, 0:1], min_val=0, max_val=1)
            with sp.If(more > 0):
                expert_loads(MOE_C0 + N_E * EXPERT_C)
            sp.wait_ge(out_ready, 2)
            sp.dma_start(tok(out[0]), x[:]).then_inc(out_stored, 16)
            sp.wait_ge(out_stored, 16)

        @block.gpsimd
        def _(pool):
            pool.wait_ge(bias_loaded, 16 * 6)
            n = 0
            for t in range(3):
                src = qk_flat[0:96, t * D:(t + 1) * D]
                part = qk_flat[0:96, 3 * D:3 * D + 512].bitcast(BF16)
                for r in range(3):
                    if r:
                        pool.tensor_tensor(src, src, part, ALU.subtract).then_inc(bias_step, 1)
                        n += 1
                        pool.wait_ge(bias_step, n)
                    pool.tensor_copy(part, src).then_inc(bias_step, 1)
                    n += 1
                    pool.wait_ge(bias_step, n)
                    last = pool.tensor_copy(bias_parts[32 * r:32 * r + 32, t * D:(t + 1) * D],
                                            part[32 * r:32 * r + 32, :])
                    if t < 2 or r < 2:
                        last.then_inc(bias_step, 1)
                        n += 1
                        pool.wait_ge(bias_step, n)
            last.then_inc(bias_made, 1)

        @block.scalar
        def _(sc):
            def cut(c, laps=0):
                sc.wait_ge(raw_loaded[c % RAW], 16 * (c // RAW + 1) + 16 * laps)
                if c >= CUT:
                    sc.wait_ge(chunk_used, c - CUT + 1 + LAP * laps)
                sc.activation(w_hi[:, c % CUT, :], raw[:, c % RAW, :], ACT.Copy).then_inc(hi_made, 1)

            def norm(n, t, src):
                if t:
                    sc.wait_ge(turned, 4 * t)
                for b in range(TB):
                    sc.activation(nat[:, b, :], src[:, b, :], ACT.Square,
                                  accum_out=stat[:, b:b + 1]).then_inc(squared, 1)
                sc.wait_ge(ms_made, n + 1)
                sc.activation(stat[:, 4:6], stat[:, 2:4], ACT.Sqrt).then_inc(std_made, 1)

            def turn(t, gain=None):
                for q in range(4):
                    sc.wait_ge(turned, 4 * t + q + 1)
                    if gain is None:
                        sc.activation(xT_hi[:, 2 * q:2 * q + 2, :].rearrange("p a b -> p (a b)"), ps[:, q, :],
                                      ACT.Copy).then_inc(turn_hi, 1)
                    else:
                        for k in (2 * q, 2 * q + 1):
                            ins = sc.activation(xT_hi[:, k, :], ps[:, q, (k % 2) * S:(k % 2 + 1) * S],
                                                ACT.Identity, scale=gcol[:, gain + k:gain + k + 1])
                        ins.then_inc(turn_hi, 1)

            def ffn_step(g, c, slot, laps=0):
                sc.wait_ge(chunk_used, c + 1 + LAP * laps)
                sc.activation(sig[:, slot, :], ps[:, 2 * slot, :], ACT.Sigmoid).then_inc(sig_made, 1)
                sc.wait_ge(act_made, g + 1)
                sc.activation(a_hi[:, slot, :], act[:, slot, :], ACT.Copy).then_inc(act_hi, 1)

            def ffn_phase(f, c0):
                cut(c0 + AHEAD)
                cut(c0 + 1 + AHEAD)
                ffn_step(FFN_PAIRS * f, c0, 0)
                with sc.Fori(0, (FFN_PAIRS - 1) // 2) as it:
                    for jj in range(2):
                        c = c0 + 2 + 3 * jj
                        cut(c + AHEAD, it)
                        cut(c + 1 + AHEAD, it)
                        ffn_step(2 * it + (FFN_PAIRS * f + 1 + jj), c, 1 - jj, it)
                        cut(c + 2 + AHEAD, it)
                cut(c0 + FFN_C - 1 + AHEAD)

            def project(g0, c0, n_groups, dst):
                for n in range(n_groups):
                    g, c = g0 + n, c0 + 2 * n
                    cut(c + AHEAD)
                    cut(c + 1 + AHEAD)
                    if dst is None:
                        continue
                    sc.wait_ge(chunk_used, c + 2)
                    bank = 4 + 2 * (g % 2)
                    sc.activation(dst[:, :, 512 * n:512 * (n + 1)], ps[:, bank:bank + 2, :],
                                  ACT.Copy).then_inc(proj_read, 1)

            def qk_copies(w, kind):
                for r in range(2):
                    for t in range(8):
                        if is_key(kind, 8 * r + t):
                            sc.wait_ge(qk_turned, 8 * w + 4 * r + t // 2 + 1)
                            sc.activation(qkT[:, 8 * r + t, :], ps[:, t // 2, (t % 2) * S:(t % 2 + 1) * S],
                                          ACT.Copy).then_inc(k_copied, 1)

            def attend(u0, groups):
                def exps(n):
                    g, u, p = groups[n], u0 + n, (u0 + n) % 2
                    sc.wait_ge(max_made, u + 1)
                    for h in range(4):
                        src = ps[:, 2 * p + h % 2, (h // 2) * S:(h // 2 + 1) * S]
                        ins = sc.activation(prob[:, p, h, :], src, ACT.Exp, bias=soft[:, p, h:h + 1],
                                            accum_out=soft[:, p, 4 + h:5 + h])
                    ins.then_inc(prob_made, 1)

                exps(0)
                for n in range(len(groups)):
                    if n + 1 < len(groups):
                        exps(n + 1)
                    g, u = groups[n], u0 + n
                    sc.wait_ge(probT_turned, u + 1)
                    if u:
                        sc.wait_ge(pv_done, u)
                    m = g["n"] * TB * P
                    sc.activation(probT[:].rearrange("p a b c -> p (a b c)")[:, 0:m],
                                  ps[:, 4:6, :].rearrange("p a b -> p (a b)")[:, 0:m],
                                  ACT.Copy).then_inc(probT_made, 1)

            def layer_norm(n):
                for b in range(TB):
                    sc.wait_ge(ln_step, LN_STEPS * n + 3 * (b + 1))
                    sc.activation(nat[:, b, :], x[:, b, :], ACT.Square,
                                  accum_out=stat[:, b:b + 1]).then_inc(ln_sq, 1)
                sc.wait_ge(ln_step, LN_STEPS * n + 7)
                sc.activation(stat[:, 4:6], stat[:, 2:4], ACT.Sqrt).then_inc(ln_std, 1)

            for c in range(AHEAD):
                cut(c)
            sc.wait_ge(lam_step, 4)
            sc.activation(lam[:, 2:4], lam[:, 0:2], ACT.Exp).then_inc(lam_exp, 1)
            sc.wait_ge(trig_step, TRIG_STEPS)
            sc.activation(trig[:, :, 0, :], ang[:, 3, :].rearrange("p (b f) -> p b f", b=TB), ACT.Sin).then_inc(trig_sin, 1)
            sc.activation(trig[:, :, 1, :], ang[:, 2, :].rearrange("p (b f) -> p b f", b=TB), ACT.Sin).then_inc(trig_sin, 1)
            for i in range(2):
                kind = ("rel", "diff")[i]
                if i == 0:
                    sc.wait_ge(x_loaded, 16)
                else:
                    sc.wait_ge(x_updated, 4 * i)
                norm(n_of(i, T_FFN1), t_of(i, T_FFN1), x)
                turn(t_of(i, T_FFN1), gain0[T_FFN1] + 8 * i)
                ffn_phase(2 * i, c_ffn1(i))
                sc.wait_ge(mem_loaded, 16 * (i + 1))
                norm(n_of(i, T_MEM), t_of(i, T_MEM), mem)
                turn(t_of(i, T_MEM), gain0[T_MEM] + 8 * i)
                project(g_kv(i), c_kv(i), 1, kvm)
                sc.wait_ge(x_updated, 4 * i + 2)
                norm(n_of(i, T_MIX), t_of(i, T_MIX), x)
                turn(t_of(i, T_MIX), gain0[T_MIX] + 8 * i)
                project(g_in(i), c_in(i), 5, pr_view("rel"))
                sc.wait_ge(head_ms, i + 1)
                sc.activation(sums[:], sums[:], ACT.Sqrt).then_inc(head_std, 1)
                qk_copies(i, kind)
                attend(u_layer(i), attention_groups(kind))
                if i == 1:
                    sc.wait_ge(sub_step, 3)
                    sc.activation(sums[:, :, 0:6], sums[:, :, 0:6], ACT.Sqrt).then_inc(sub_step, 1)
                turn(t_of(i, T_O))
                project(g_out(i), c_out(i), 2, None)
                sc.wait_ge(proj_read, g_out(i) + 2)
                norm(n_of(i, T_FFN2), t_of(i, T_FFN2), x)
                turn(t_of(i, T_FFN2), gain0[T_FFN2] + 8 * i)
                ffn_phase(2 * i + 1, c_ffn2(i))
            turn(t_moba)
            project(g_moba, c_moba, 6, pr_view("moba"))
            qk_copies(2, "moba")
            attend(u_moba, attention_groups("moba"))
            turn(t_moba_o)
            project(g_moba_out, c_moba_out, 2, None)
            layer_norm(0)
            sc.wait_ge(moe_loaded, MOE_LOADS)
            sc.activation(wr_hi[:], wr[:], ACT.Copy).then_inc(wr_cut, 1)
            sc.wait_ge(ln_step, LN_STEPS)
            turn(t_moe)
            for b in range(TB):
                sc.activation(xn_hi[:, b, :], x[:, b, :], ACT.Copy).then_inc(xn_hi_made, 1)
            sc.wait_ge(route_step, ROUTE_EXP)
            sc.activation(rank[:], rank[:], ACT.Exp).then_inc(route_exp, 1)

            def gathered_part(e, q, par):
                sc.wait_ge(gathered, 2 * e + q + 1)
                sc.activation(xs_hi[:, 4 * q:4 * q + 4, :].rearrange("p a b -> p (a b)"),
                              ps[:, gather_bank(q, par), :], ACT.Copy).then_inc(xs_hi_made, 1)

            def expert(e, par, c, laps):
                g0 = 2 * par
                g1 = 2 - g0
                cut(c + AHEAD, laps)
                sc.wait_ge(chunk_used, c + LAP * laps)
                sc.wait_ge(scattered, e + 1)
                sc.wait_ge(gate_made, e + 1)
                sc.activation(y_hi[:], ps[:, g1:g1 + 2, :].rearrange("p a b -> p (a b)"), ACT.Identity,
                              scale=slot_gate[:, 1 - par:2 - par]).then_inc(y_hi_made, 1)
                for n in range(1, EXPERT_C):
                    cut(c + n + AHEAD, laps)
                    if n in (3, 7):
                        half = n // 4
                        sc.wait_ge(limited, 2 * e + half + 1)
                        sc.activation(m_sig[:], m_g[:], ACT.Sigmoid, scale=SWIGLU_ALPHA).then_inc(m_sig_made, 1)
                    if n == 5:
                        turned_half(e, 0, g0)
                        sc.wait_ge(pickT_turned, e + 1)
                        sc.wait_ge(scattered, e + 2)
                        sc.activation(pickT[:], ps[:, g0 + 1, 0:S], ACT.Copy).then_inc(pickT_made, 1)
                        sc.activation(slot_gate[:, par:par + 1], ps[:, g0 + 1, S:S + 1], ACT.Copy).then_inc(gate_made, 1)
                    if n == 9:
                        turned_half(e, 1, g1)
                        gathered_part(e + 1, 0, par)
                    if n == 10:
                        gathered_part(e + 1, 1, par)

            def turned_half(e, half, bank):
                sc.wait_ge(m_turned, 2 * e + half + 1)
                sc.activation(m_hi[:, 4 * half:4 * half + 4, :].rearrange("p a b -> p (a b)"), ps[:, bank, :],
                              ACT.Copy).then_inc(m_hi_made, 1)

            gathered_part(0, 0, 1)
            gathered_part(0, 1, 1)

            def round_of_experts(r):
                c0 = MOE_C0 + r * N_E * EXPERT_C
                with sc.Fori(0, N_E // 2) as it:
                    expert(2 * it + r * N_E, 0, c0, 4 * it)
                    expert(2 * it + (r * N_E + 1), 1, c0 + EXPERT_C, 4 * it)

            round_of_experts(0)
            sc.wait_ge(crowd_made, 1)
            more = sc.value_load(crowd_i[0:1, 0:1], min_val=0, max_val=1)
            with sc.If(more > 0):
                round_of_experts(1)
            sc.wait_ge(chunk_used, N_E * EXPERT_C * more + (MOE_C0 + N_E * EXPERT_C))
            sc.activation(y_hi[:], ps[:, 2:4, :].rearrange("p a b -> p (a b)"), ACT.Identity,
                          scale=slot_gate[:, 1:2]).then_inc(last_hi, 1)
            layer_norm(1)

        @block.vector
        def _(ve):
            def cut(c, laps=0):
                ve.wait_ge(hi_made, c + 1 + LAP * laps)
                ve.tensor_tensor(w_lo[:, c % CUT, :], raw[:, c % RAW, :], w_hi[:, c % CUT, :].bitcast(F32),
                                 ALU.subtract).then_inc(lo_made, 1)

            def norm(n, src):
                ve.wait_ge(squared, TB * (n + 1))
                ve.tensor_scalar(stat[:, 2:4], stat[:, 0:2], 1.0 / D, EPS, ALU.mult, ALU.add).then_inc(ms_made, 1)
                ve.wait_ge(std_made, n + 1)
                ve.reciprocal(stat[:, 6:8], stat[:, 4:6]).then_inc(rstd_made, 1)
                ve.wait_ge(rstd_made, n + 1)
                for b in range(TB):
                    ve.tensor_scalar(nat[:, b, :], src[:, b, :], stat[:, 6 + b:7 + b], None, ALU.mult).then_inc(normed, 1)

            def turn(t, gain=None):
                for q in range(4):
                    ve.wait_ge(turn_hi, 4 * t + q + 1)
                    hi = xT_hi[:, 2 * q:2 * q + 2, :].bitcast(F32)
                    if gain is None:
                        ve.tensor_tensor(xT_lo[:, 2 * q:2 * q + 2, :].rearrange("p a b -> p (a b)"), ps[:, q, :],
                                         hi.rearrange("p a b -> p (a b)"), ALU.subtract).then_inc(turn_lo, 1)
                    else:
                        for k in (2 * q, 2 * q + 1):
                            ins = ve.scalar_tensor_tensor(
                                out=xT_lo[:, k, :], in0=ps[:, q, (k % 2) * S:(k % 2 + 1) * S],
                                scalar=gcol[:, gain + k:gain + k + 1], in1=xT_hi[:, k, :].bitcast(F32),
                                op0=ALU.mult, op1=ALU.subtract)
                        ins.then_inc(turn_lo, 1)

            def ffn_step(g, c, slot, laps=0):
                ve.wait_ge(sig_made, g + 1)
                ve.tensor_tensor(gated[:, slot, :], ps[:, 2 * slot, :], sig[:, slot, :], ALU.mult).then_inc(gated_made, 1)
                ve.wait_ge(gated_made, g + 1)
                ve.wait_ge(chunk_used, c + 2 + LAP * laps)
                ve.tensor_tensor(act[:, slot, :], ps[:, 2 * slot + 1, :], gated[:, slot, :], ALU.mult).then_inc(act_made, 1)
                ve.wait_ge(act_hi, g + 1)
                ve.tensor_tensor(a_lo[:, slot, :], act[:, slot, :], a_hi[:, slot, :].bitcast(F32),
                                 ALU.subtract).then_inc(act_lo, 1)

            def ffn_phase(f, c0):
                cut(c0 + AHEAD)
                cut(c0 + 1 + AHEAD)
                ffn_step(FFN_PAIRS * f, c0, 0)
                with ve.Fori(0, (FFN_PAIRS - 1) // 2) as it:
                    for jj in range(2):
                        c = c0 + 2 + 3 * jj
                        cut(c + AHEAD, it)
                        cut(c + 1 + AHEAD, it)
                        ffn_step(2 * it + (FFN_PAIRS * f + 1 + jj), c, 1 - jj, it)
                        cut(c + 2 + AHEAD, it)
                cut(c0 + FFN_C - 1 + AHEAD)
                ve.wait_ge(chunk_used, c0 + FFN_C)
                for b in range(TB):
                    ve.scalar_tensor_tensor(out=x[:, b, :], in0=ps[:, 4 + 2 * b:6 + 2 * b, :].rearrange("p a b -> p (a b)"),
                                            scalar=0.5, in1=x[:, b, :], op0=ALU.mult, op1=ALU.add).then_inc(x_updated, 1)

            def project(g0, c0, n_groups, add=None):
                for n in range(n_groups):
                    g, c = g0 + n, c0 + 2 * n
                    cut(c + AHEAD)
                    cut(c + 1 + AHEAD)
                    if add is None:
                        continue
                    ve.wait_ge(chunk_used, c + 2)
                    bank = 4 + 2 * (g % 2)
                    cols = x[:, :, 512 * n:512 * (n + 1)]
                    ve.scalar_tensor_tensor(out=cols, in0=cols, scalar=add, in1=ps[:, bank:bank + 2, :],
                                            op0=ALU.mult, op1=ALU.add).then_inc(proj_read, 1)

            def heads(t, n):
                return t.rearrange("p (h d) -> p h d", h=n)

            def head_norms(i):
                v = pr_view("rel")
                spans = [(v, 0, 24, 0), (v, 3 * SELF_W, 4, 24), (kvm, 0, 4, 28)]
                ve.wait_ge(proj_read, g_in(i) + 5)
                k = 0
                for b in range(TB):
                    for src, c0, n, s0 in spans:
                        sq = prob[:].rearrange("p a b c -> p (a b c)")[:, 0:n * HD]
                        ve.tensor_tensor(sq, src[:, b, c0:c0 + n * HD], src[:, b, c0:c0 + n * HD],
                                         ALU.mult).then_inc(head_sq, 1)
                        k += 1
                        ve.wait_ge(head_sq, 6 * i + k)
                        ve.tensor_reduce(sums[:, b, s0:s0 + n], heads(sq, n), AX.X, ALU.add).then_inc(head_sum, 1)
                        ve.wait_ge(head_sum, 6 * i + k)
                ve.tensor_scalar(sums[:], sums[:], 1.0 / HD, EPS, ALU.mult, ALU.add).then_inc(head_ms, 1)
                ve.wait_ge(head_std, i + 1)
                ve.reciprocal(sums[:], sums[:]).then_inc(head_rstd, 1)
                ve.wait_ge(head_rstd, i + 1)
                for b in range(TB):
                    for src, c0, n, s0 in spans:
                        view = heads(src[:, b, c0:c0 + n * HD], n)
                        ve.tensor_tensor(view, view, sums[:, b, s0:s0 + n].unsqueeze(2).to_broadcast([P, n, HD]),
                                         ALU.mult).then_inc(head_normed, 1)

            def rope_all():
                v = pr_view("rel")
                tmp = prob[:].rearrange("p a b c -> p (a b c)")
                s = 0
                ve.wait_ge(head_normed, 12)
                ve.wait_ge(trig_sin, 2)
                for b in range(TB):
                    for n, gain in ((0, 4), (1, 5)):
                        view = heads(v[:, b, n * SELF_W:(n + 1) * SELF_W], 12)
                        g = bc[:, HD * gain:HD * (gain + 1)].unsqueeze(1).to_broadcast([P, 12, HD])
                        ve.tensor_tensor(view, view, g, ALU.mult).then_inc(rope_step, 1)
                        s += 1
                    ve.wait_ge(rope_step, s)
                    view = heads(v[:, b, 0:2 * SELF_W], 24)
                    x1, x2 = view[:, :, 0:32], view[:, :, 32:64]
                    t1, t2 = heads(tmp[:, 0:SELF_W], 24), heads(tmp[:, SELF_W:2 * SELF_W], 24)
                    cos = trig[:, b, 0, :].unsqueeze(1).to_broadcast([P, 24, 32])
                    sin = trig[:, b, 1, :].unsqueeze(1).to_broadcast([P, 24, 32])
                    for o, p, q, op in ((t1, x2, sin, ALU.mult), (t2, x1, sin, ALU.mult), (x1, x1, cos, ALU.mult),
                                        (x2, x2, cos, ALU.mult), (x1, x1, t1, ALU.subtract), (x2, x2, t2, ALU.add)):
                        ve.tensor_tensor(o, p, q, op).then_inc(rope_step, 1)
                        s += 1
                        ve.wait_ge(rope_step, s)

            def qk_copies(w, kind):
                for r in range(2):
                    for t in range(8):
                        tile = 8 * r + t
                        if is_key(kind, tile):
                            continue
                        ve.wait_ge(qk_turned, 8 * w + tile // 2 + 1)
                        src = ps[:, t // 2, (t % 2) * S:(t % 2 + 1) * S]
                        if kind == "moba":
                            scale = P ** -0.5
                        elif tile >= 12:
                            scale = qscale[:, w:w + 1]
                        else:
                            scale = qscale[:, 2:3] if kind == "rel" else HD ** -0.5
                        ve.tensor_scalar(qkT[:, tile, :], src, scale, None, ALU.mult).then_inc(q_copied, 1)

            def attend(u0, groups):
                def lead(n):
                    g, u, p = groups[n], u0 + n, (u0 + n) % 2
                    ve.wait_ge(scored, u + 1)
                    s = ps[:, 2 * p:2 * p + 2, :].rearrange("p a (c k) -> p c a k", c=2)
                    if u >= 2:
                        ve.wait_ge(probT_turned, u - 1)
                    for c in range(2):
                        ins = ve.tensor_reduce(soft[:, p, 2 * c:2 * c + 2], s[:, c], AX.X, ALU.max, negate=True)
                    ins.then_inc(max_made, 1)

                def follow(n):
                    g, u, p = groups[n], u0 + n, (u0 + n) % 2
                    ve.wait_ge(prob_made, u + 1)
                    if n >= 2:
                        ve.wait_ge(o_made, u - 1)
                    ve.reciprocal(soft[:, p, 8:12], soft[:, p, 4:8]).then_inc(total_read, 1)
                    ve.wait_ge(total_read, u + 1)
                    if g["diff"]:
                        m = n_diff(groups, n)
                        for h in range(2):
                            ve.tensor_scalar(soft[:, p, 12 + h:13 + h], soft[:, p, 9 + 2 * h:10 + 2 * h],
                                             lam[:, 5:6], None, ALU.mult).then_inc(mixed, 1)
                        ve.wait_ge(mixed, 6 * m - 4)
                        for h in range(2):
                            ve.tensor_scalar(prob[:, p, 2 * h + 1, :], prob[:, p, 2 * h + 1, :],
                                             soft[:, p, 12 + h:13 + h], None, ALU.mult).then_inc(mixed, 1)
                        ve.wait_ge(mixed, 6 * m - 2)
                        for h in range(2):
                            ve.scalar_tensor_tensor(out=prob[:, p, 2 * h, :], in0=prob[:, p, 2 * h, :],
                                                    scalar=soft[:, p, 8 + 2 * h:9 + 2 * h], in1=prob[:, p, 2 * h + 1, :],
                                                    op0=ALU.mult, op1=ALU.subtract).then_inc(mixed, 1)

                def outputs(n):
                    g, u, p = groups[n], u0 + n, (u0 + n) % 2
                    ve.wait_ge(pv_done, u + 1)
                    k, dv = g["n"], g["dv"]
                    dst = nat[:, g["b"], g["o"]:g["o"] + k * dv]
                    src = ps[:, 6 + p, 0:k * dv]
                    if g["diff"]:
                        ve.tensor_copy(dst, src).then_inc(o_made, 1)
                    else:
                        ve.tensor_tensor(heads(dst, k), heads(src, k),
                                         soft[:, p, 8:12].unsqueeze(2).to_broadcast([P, k, dv]), ALU.mult).then_inc(o_made, 1)

                lead(0)
                for n in range(len(groups)):
                    if n + 1 < len(groups):
                        lead(n + 1)
                    follow(n)
                    if n:
                        outputs(n - 1)
                outputs(len(groups) - 1)

            def layer_norm(n):
                s = [LN_STEPS * n]

                def step(ins, by=ln_step):
                    ins.then_inc(by, 1)
                    if by is ln_step:
                        s[0] += 1
                        ve.wait_ge(ln_step, s[0])

                for b in range(TB):
                    step(ve.tensor_reduce(stat[:, 8 + b:9 + b], x[:, b, :], AX.X, ALU.add))
                    step(ve.tensor_scalar(stat[:, 10 + b:11 + b], stat[:, 8 + b:9 + b], 1.0 / D, None, ALU.mult))
                    step(ve.tensor_scalar(x[:, b, :], x[:, b, :], stat[:, 10 + b:11 + b], None, ALU.subtract))
                ve.wait_ge(ln_sq, TB * (n + 1))
                step(ve.tensor_scalar(stat[:, 2:4], stat[:, 0:2], 1.0 / D, LN_EPS, ALU.mult, ALU.add))
                ve.wait_ge(ln_std, n + 1)
                step(ve.reciprocal(stat[:, 6:8], stat[:, 4:6]))
                for b in range(TB):
                    step(ve.scalar_tensor_tensor(out=x[:, b, :], in0=x[:, b, :], scalar=stat[:, 6 + b:7 + b],
                                                 in1=ln[:, n, 0, :], op0=ALU.mult, op1=ALU.mult))
                    step(ve.tensor_tensor(x[:, b, :], x[:, b, :], ln[:, n, 1, :], ALU.add), (ln_step, out_ready)[n])

            ve.wait_ge(gcol_turned, 1)
            ve.tensor_copy(gcol[:, 0:70], ps[:, 0, 0:70]).then_inc(qscale_made, 1)
            ve.wait_ge(qscale_made, 1)
            for n, (q, k) in enumerate(((64, 66), (65, 67), (68, 69))):
                ve.scalar_tensor_tensor(out=qscale[:, n:n + 1], in0=gcol[:, q:q + 1], scalar=HD ** -0.5,
                                        in1=gcol[:, k:k + 1], op0=ALU.mult, op1=ALU.mult).then_inc(qscale_made, 1)
            ve.wait_ge(qscale_made, 4)
            for c in range(AHEAD):
                cut(c)
            ve.wait_ge(small_loaded, 16 * 9)
            for n in range(2):
                ve.tensor_tensor(ang[:, n, 0:HD], bc[:, 128 * n:128 * n + 64], bc[:, 128 * n + 64:128 * n + 128],
                                 ALU.mult).then_inc(lam_step, 1)
                ve.wait_ge(lam_step, 2 * n + 1)
                ve.tensor_reduce(lam[:, n:n + 1], ang[:, n, 0:HD], AX.X, ALU.add).then_inc(lam_step, 1)
            ve.wait_ge(lam_exp, 1)
            ve.tensor_tensor(lam[:, 4:5], lam[:, 2:3], lam[:, 3:4], ALU.subtract).then_inc(lam_step, 1)
            ve.wait_ge(lam_step, 5)
            ve.tensor_scalar(lam[:, 5:6], lam[:, 4:5], LAMBDA_INIT, None, ALU.add).then_inc(lam_step, 1)
            t = [0]

            def step(ins):
                ins.then_inc(trig_step, 1)
                t[0] += 1
                ve.wait_ge(trig_step, t[0])

            step(ve.tensor_copy(pos_f[:], pos_i[:]))
            for b in range(TB):
                step(ve.tensor_scalar(ang[:, 0, 32 * b:32 * b + 32], inv_row[:], pos_f[:, b:b + 1], None, ALU.mult))
            step(ve.tensor_scalar(ang[:, 1, :], ang[:, 0, :], 1.0 / (2 * math.pi), None, ALU.mult))
            step(ve.tensor_copy(turns_i[:], ang[:, 1, :]))
            step(ve.tensor_copy(ang[:, 1, :], turns_i[:]))
            c1 = 6.28125
            c2 = float(np.float32(np.round((2 * math.pi - c1) * 2 ** 21) / 2 ** 21))
            c3 = 2 * math.pi - c1 - c2
            src = 0
            for c in (c1, c2, c3):
                step(ve.scalar_tensor_tensor(out=ang[:, 2, :], in0=ang[:, 1, :], scalar=-c, in1=ang[:, src, :],
                                             op0=ALU.mult, op1=ALU.add))
                src = 2
            step(ve.tensor_scalar(ang[:, 3, :], ang[:, 2, :], math.pi / 2, None, ALU.add))
            for k in (2, 3):
                for bound, op, off in ((math.pi, ALU.is_gt, -2 * math.pi), (-math.pi, ALU.is_lt, 2 * math.pi)):
                    step(ve.tensor_scalar(ang[:, 4, :], ang[:, k, :], bound, off, op, ALU.mult))
                    step(ve.tensor_tensor(ang[:, k, :], ang[:, k, :], ang[:, 4, :], ALU.add))
                step(ve.tensor_scalar(ang[:, k, :], ang[:, k, :], PI_BELOW, -PI_BELOW, ALU.min, ALU.max))
            assert t[0] == TRIG_STEPS
            ve.wait_ge(lam_step, 6)
            ve.tensor_scalar(bc[:, 384:512], bc[:, 384:512], 1.0 - LAMBDA_INIT, None, ALU.mult).then_inc(lam_step, 1)
            for i in range(2):
                kind = ("rel", "diff")[i]
                norm(n_of(i, T_FFN1), x)
                turn(t_of(i, T_FFN1), gain0[T_FFN1] + 8 * i)
                ffn_phase(2 * i, c_ffn1(i))
                norm(n_of(i, T_MEM), mem)
                turn(t_of(i, T_MEM), gain0[T_MEM] + 8 * i)
                project(g_kv(i), c_kv(i), 1)
                norm(n_of(i, T_MIX), x)
                turn(t_of(i, T_MIX), gain0[T_MIX] + 8 * i)
                if i == 0:
                    ve.wait_ge(ext_turned, 1)
                    ve.tensor_copy(ang[:, 0, 0:24], ps[:, 7, 0:24]).then_inc(ext_made, 1)
                    ve.wait_ge(ext_rows, 1)
                    ve.tensor_copy(row_by_distance(12), ps[0:12, 7, :]).then_inc(ext_copied, 1)
                project(g_in(i), c_in(i), 5)
                head_norms(i)
                if i == 1:
                    rope_all()
                qk_copies(i, kind)
                if i == 0:
                    ve.wait_ge(strip_loaded, 16 * 12)
                    ve.memset(strip[64:P, :, 192:REL_W], NEG).then_inc(strip_ready, 1)
                    ve.memset(strip[0:64, :, 256:REL_W], NEG).then_inc(strip_ready, 1)
                else:
                    ve.memset(strip[:, 0, :], 0.0).then_inc(strip_ready, 1)
                    ve.wait_ge(strip_ready, 3)
                    ve.memset(strip[64:P, 0, 192:REL_W], NEG).then_inc(strip_ready, 1)
                    ve.memset(strip[0:64, 0, 256:REL_W], NEG).then_inc(strip_ready, 1)
                attend(u_layer(i), attention_groups(kind))
                if i == 1:
                    ve.wait_ge(o_made, u_moba)
                    sq = prob[:].rearrange("p a b c -> p (a b c)")[:, 0:2 * SELF_W].rearrange("p (b w) -> p b w", b=TB)
                    o = nat[:, :, 0:SELF_W]
                    ve.tensor_tensor(sq, o, o, ALU.mult).then_inc(sub_step, 1)
                    ve.wait_ge(sub_step, 1)
                    for b in range(TB):
                        ins = ve.tensor_reduce(sums[:, b, 0:6], heads(sq[:, b, :], 6), AX.X, ALU.add)
                    ins.then_inc(sub_step, 1)
                    ve.wait_ge(sub_step, 2)
                    ve.tensor_scalar(sums[:, :, 0:6], sums[:, :, 0:6], 1.0 / P, EPS, ALU.mult, ALU.add).then_inc(sub_step, 1)
                    ve.wait_ge(sub_step, 4)
                    ve.reciprocal(sums[:, :, 0:6], sums[:, :, 0:6]).then_inc(sub_step, 1)
                    ve.wait_ge(sub_step, 5)
                    for b in range(TB):
                        view = heads(nat[:, b, 0:SELF_W], 6)
                        ins = ve.tensor_tensor(view, view, sums[:, b, 0:6].unsqueeze(2).to_broadcast([P, 6, P]), ALU.mult)
                    ins.then_inc(sub_step, 1)
                    ve.wait_ge(sub_step, 6)
                    for b in range(TB):
                        view = heads(nat[:, b, 0:SELF_W], 6)
                        ins = ve.tensor_tensor(view, view, bc[:, 384:512].unsqueeze(1).to_broadcast([P, 6, P]), ALU.mult)
                    ins.then_inc(sub_step, 1)
                turn(t_of(i, T_O))
                project(g_out(i), c_out(i), 2, add=1.0)
                norm(n_of(i, T_FFN2), x)
                turn(t_of(i, T_FFN2), gain0[T_FFN2] + 8 * i)
                ffn_phase(2 * i + 1, c_ffn2(i))
            turn(t_moba)
            ve.wait_ge(ext_rows, 2)
            ve.tensor_copy(row_by_distance(8), ps[0:8, 7, :]).then_inc(ext_made, 1)
            ve.wait_ge(ext_made, 2)
            ve.memset(row_by_distance(8)[:, S:512], NEG).then_inc(ext_copied, 1)
            project(g_moba, c_moba, 6)
            qk_copies(2, "moba")
            attend(u_moba, attention_groups("moba"))
            turn(t_moba_o)
            project(g_moba_out, c_moba_out, 2, add=ALPHA)
            ve.wait_ge(proj_read, g_moba_out + 2)
            ve.wait_ge(moe_loaded, MOE_LOADS)
            layer_norm(0)
            ve.wait_ge(wr_cut, 1)
            ve.tensor_tensor(wr_lo[:], wr[:], wr_hi[:].bitcast(F32), ALU.subtract).then_inc(wr_ready, 1)
            turn(t_moe)
            for b in range(TB):
                ve.wait_ge(xn_hi_made, b + 1)
                ve.tensor_tensor(xn_lo[:, b, :], x[:, b, :], xn_hi[:, b, :].bitcast(F32), ALU.subtract).then_inc(xn_lo_made, 1)
            r = [0]

            def route(ins):
                ins.then_inc(route_step, 1)
                r[0] += 1
                ve.wait_ge(route_step, r[0])

            ve.wait_ge(logits_done, 1)
            for b in range(TB):
                route(ve.tensor_tensor(lg[:, b, :], ps[:, 4 + b, 0:N_E], lg_row[:], ALU.add))
            for b in range(TB):
                mine = lg[:, b, :].unsqueeze(2).to_broadcast([P, N_E, N_E])
                other = lg[:, b, :].unsqueeze(1).to_broadcast([P, N_E, N_E])
                route(ve.tensor_tensor(above[:], other, mine, ALU.is_gt))
                route(ve.tensor_tensor(equal[:], other, mine, ALU.is_equal))
                route(ve.tensor_tensor(equal[:], equal[:], tri[:], ALU.mult))
                route(ve.tensor_tensor(above[:], above[:], equal[:], ALU.add))
                route(ve.tensor_reduce(rank[:, b, :], above[:], AX.X, ALU.add))
                route(ve.tensor_scalar(chosen[:, b, :], rank[:, b, :], float(TOP_K), None, ALU.is_lt))
                route(ve.tensor_reduce(stat[:, 12 + b:13 + b], lg[:, b, :], AX.X, ALU.max))
                route(ve.tensor_scalar(rank[:, b, :], lg[:, b, :], stat[:, 12 + b:13 + b], None, ALU.subtract))
            assert r[0] == ROUTE_EXP
            ve.wait_ge(route_exp, 1)
            for b in range(TB):
                route(ve.tensor_tensor(rank[:, b, :], rank[:, b, :], chosen[:, b, :], ALU.mult))
                route(ve.tensor_reduce(stat[:, 14 + b:15 + b], rank[:, b, :], AX.X, ALU.add))
                route(ve.reciprocal(stat[:, 14 + b:15 + b], stat[:, 14 + b:15 + b]))
                for k in range(2):
                    route(ve.tensor_scalar(gate[:, b, N_E * k:N_E * (k + 1)], rank[:, b, :], stat[:, 14 + b:15 + b], None, ALU.mult))
                route(ve.memset(gate[:, b, 2 * N_E:2 * N_E + 2], 0.0))
            ve.wait_ge(crowd_done, 1)
            for b in range(TB):
                route(ve.scalar_tensor_tensor(out=place[:, b, 0:N_E], in0=ps[:, 6, N_E * b:N_E * (b + 1)], scalar=1.0,
                                              in1=chosen[:, b, :], op0=ALU.add, op1=ALU.mult))
                route(ve.tensor_scalar(place[:, b, 0:N_E], place[:, b, 0:N_E], -1.0, None, ALU.add))
                route(ve.tensor_scalar(place[:, b, N_E:2 * N_E], place[:, b, 0:N_E], float(-P), None, ALU.add))
                route(ve.memset(place[:, b, 2 * N_E:2 * N_E + 2], -1.0))
            route(ve.tensor_reduce(crowd[:, N_E:N_E + 1], ps[:, 6, 2 * N_E:3 * N_E], AX.X, ALU.max))
            route(ve.tensor_scalar(crowd[:, N_E + 1:N_E + 2], crowd[:, N_E:N_E + 1], float(P), None, ALU.is_gt))
            ve.tensor_copy(crowd_i[:, 0:1], crowd[:, N_E + 1:N_E + 2]).then_inc(crowd_made, 1)
            ve.memset(slot_gate[:], 0.0).then_inc(gate_made, 1)
            for b in range(TB):
                ve.tensor_scalar(pickT[:, b * P:(b + 1) * P], ones, 0.0, None, ALU.mult).then_inc(m_zero, 1)

            def picks(e, par):
                for b in range(TB):
                    ins = ve.tensor_scalar(pick[:, par, b, :], iota_row, place[:, b, bass.ds(e, 1)], None, ALU.is_equal)
                ins.then_inc(picked, 1)

            def bias_rows(e, par):
                ve.tensor_scalar(sel[:, par, :], ones[0:96, :], onehot96[:, bass.ds(e, 1)], None, ALU.mult).then_inc(picked, 1)

            def gathered_part(e, q, par):
                ve.wait_ge(xs_hi_made, 2 * e + q + 1)
                ve.tensor_tensor(xs_lo[:, 4 * q:4 * q + 4, :].rearrange("p a b -> p (a b)"), ps[:, gather_bank(q, par), :],
                                 xs_hi[:, 4 * q:4 * q + 4, :].rearrange("p a b -> p (a b)").bitcast(F32),
                                 ALU.subtract).then_inc(xs_lo_made, 1)

            def swiglu(e, half, bank, c, laps):
                ve.wait_ge(chunk_used, c + LAP * laps)
                ve.tensor_scalar(m_g[:], ps[:, bank, :], LIMIT, None, ALU.min).then_inc(limited, 1)
                ve.tensor_scalar(m_u[:], ps[:, bank + 1, :], LIMIT, -LIMIT, ALU.min, ALU.max).then_inc(up_limited, 1)
                ve.wait_ge(limited, 2 * e + half + 1)
                ve.wait_ge(up_limited, 2 * e + half + 1)
                ve.scalar_tensor_tensor(out=m_gu[:], in0=m_u[:], scalar=1.0, in1=m_g[:], op0=ALU.add,
                                        op1=ALU.mult).then_inc(m_gu_made, 1)
                ve.wait_ge(m_gu_made, 2 * e + half + 1)
                ve.wait_ge(m_sig_made, 2 * e + half + 1)
                ve.tensor_tensor(m_act[:, half, :], m_gu[:], m_sig[:], ALU.mult).then_inc(m_act_made, 1)

            def turned_half(e, half, bank):
                ve.wait_ge(m_hi_made, 2 * e + half + 1)
                ve.tensor_tensor(m_lo[:, 4 * half:4 * half + 4, :].rearrange("p a b -> p (a b)"), ps[:, bank, :],
                                 m_hi[:, 4 * half:4 * half + 4, :].rearrange("p a b -> p (a b)").bitcast(F32),
                                 ALU.subtract).then_inc(m_lo_made, 1)

            def expert(e, e_in_round, par, c, laps):
                g0 = 2 * par
                g1 = 2 - g0
                cut(c + AHEAD, laps)
                ve.wait_ge(y_hi_made, e + 1)
                ve.scalar_tensor_tensor(out=y_lo[:], in0=ps[:, g1:g1 + 2, :].rearrange("p a b -> p (a b)"),
                                        scalar=slot_gate[:, 1 - par:2 - par], in1=y_hi[:].bitcast(F32),
                                        op0=ALU.mult, op1=ALU.subtract).then_inc(y_lo_made, 1)
                for n in range(1, EXPERT_C):
                    cut(c + n + AHEAD, laps)
                    if n == 1:
                        picks(e + 1, 1 - par)
                        bias_rows(e_in_round + 1, 1 - par)
                    if n in (3, 7):
                        swiglu(e, n // 4, (g0, g1)[n // 4], c + n + 1, laps)
                    if n == 5:
                        turned_half(e, 0, g0)
                    if n == 9:
                        turned_half(e, 1, g1)
                        gathered_part(e + 1, 0, par)
                    if n == 10:
                        gathered_part(e + 1, 1, par)

            picks(0, 0)
            bias_rows(0, 0)
            gathered_part(0, 0, 1)
            gathered_part(0, 1, 1)

            def round_of_experts(rnd):
                c0 = MOE_C0 + rnd * N_E * EXPERT_C
                with ve.Fori(0, N_E // 2) as it:
                    expert(2 * it + rnd * N_E, 2 * it, 0, c0, 4 * it)
                    expert(2 * it + (rnd * N_E + 1), 2 * it + 1, 1, c0 + EXPERT_C, 4 * it)

            round_of_experts(0)
            ve.wait_ge(crowd_made, 1)
            more = ve.value_load(crowd_i[0:1, 0:1], min_val=0, max_val=1)
            with ve.If(more > 0):
                round_of_experts(1)
            ve.wait_ge(last_hi, 1)
            ve.scalar_tensor_tensor(out=y_lo[:], in0=ps[:, 2:4, :].rearrange("p a b -> p (a b)"),
                                    scalar=slot_gate[:, 1:2], in1=y_hi[:].bitcast(F32),
                                    op0=ALU.mult, op1=ALU.subtract).then_inc(last_lo, 1)
            ve.wait_ge(last_scattered, 1)
            for b in range(TB):
                ve.scalar_tensor_tensor(out=x[:, b, :], in0=x[:, b, :], scalar=ALPHA,
                                        in1=ps[:, 4 + 2 * b:6 + 2 * b, :].rearrange("p a b -> p (a b)"),
                                        op0=ALU.mult, op1=ALU.add).then_inc(x_updated, 1)
            ve.wait_ge(x_updated, 8 + TB)
            layer_norm(1)

        @block.tensor
        def _(pe):
            def three(o, l_hi, l_lo, r_hi, r_lo, start, stop):
                pe.matmul(o, l_hi, r_hi, start=start, stop=False)
                pe.matmul(o, l_hi, r_lo, start=False, stop=False)
                return pe.matmul(o, l_lo, r_hi, start=False, stop=stop)

            def turn(src):
                for q in range(4):
                    for k in (2 * q, 2 * q + 1):
                        for b in range(TB):
                            o = (k % 2) * S + b * P
                            ins = pe.transpose(ps[:, q, o:o + P], src[:, b, k * P:(k + 1) * P], ident[:])
                    ins.then_inc(turned, 1)

            def ffn_in(c, bank, laps=0):
                pe.wait_ge(lo_made, c + 1 + LAP * laps)
                s = c % CUT
                for f in range(2):
                    for k in range(KT):
                        w = slice(k * 256 + f * P, k * 256 + (f + 1) * P)
                        ins = three(ps[:, bank, f * S:(f + 1) * S], w_hi[:, s, w], w_lo[:, s, w],
                                    xT_hi[:, k, :], xT_lo[:, k, :], k == 0, k == KT - 1)
                ins.then_inc(chunk_used, 1)

            def ffn_out(c, slot, g, first=False, last=False, laps=0):
                pe.wait_ge(act_lo, g + 1)
                pe.wait_ge(lo_made, c + 1 + LAP * laps)
                s = c % CUT
                for k in range(2):
                    for b in range(TB):
                        for h in range(2):
                            l = slice(k * S + b * P, k * S + (b + 1) * P)
                            w = slice(k * D + h * 512, k * D + (h + 1) * 512)
                            ins = three(ps[:, 4 + 2 * b + h, :], a_hi[:, slot, l], a_lo[:, slot, l],
                                        w_hi[:, s, w], w_lo[:, s, w], first and k == 0, last and k == 1)
                ins.then_inc(chunk_used, 1)

            def ffn_phase(f, c0, xparts):
                pe.wait_ge(turn_lo, xparts)
                g0 = FFN_PAIRS * f
                ffn_in(c0, 0)
                ffn_in(c0 + 1, 1)

                def step(slot, c, laps, first, g):
                    if not first:
                        pe.wait_ge(act_made, g - 1)
                    ffn_in(c, 2 * slot, laps)
                    ffn_in(c + 1, 2 * slot + 1, laps)
                    ffn_out(c + 2, 1 - slot, g - 1, first=first, laps=laps)

                step(1, c0 + 2, 0, True, g0 + 1)
                step(0, c0 + 5, 0, False, g0 + 2)
                with pe.Fori(1, (FFN_PAIRS - 1) // 2) as it:
                    for jj in range(2):
                        step(1 - jj, c0 + 2 + 3 * jj, it, False, 2 * it + (g0 + 1 + jj))
                ffn_out(c0 + FFN_C - 1, 0, g0 + FFN_PAIRS - 1, last=True)

            def project(g0, c0, n_groups):
                for n in range(n_groups):
                    g = g0 + n
                    if g >= 2:
                        pe.wait_ge(proj_read, g - 1)
                    for h in range(2):
                        c = c0 + 2 * n + h
                        pe.wait_ge(lo_made, c + 1)
                        s = c % CUT
                        for b in range(TB):
                            for k in range(4):
                                kk = 4 * h + k
                                w = slice(k * 512, (k + 1) * 512)
                                l = slice(b * P, (b + 1) * P)
                                ins = three(ps[:, 4 + 2 * (g % 2) + b, :], xT_hi[:, kk, l], xT_lo[:, kk, l],
                                            w_hi[:, s, w], w_lo[:, s, w], kk == 0, kk == KT - 1)
                        ins.then_inc(chunk_used, 1)

            def turn_qk(w, kind):
                v = pr_view(kind)
                for r in range(2):
                    for t in range(8):
                        tile = 8 * r + t
                        if r == 1 and t % 2 == 0:
                            for tt in (t, t + 1):
                                if is_key(kind, tt):
                                    pe.wait_ge(k_copied, 8 * w + 1 + sum(is_key(kind, m) for m in range(tt)))
                                else:
                                    pe.wait_ge(q_copied, 8 * w + 1 + sum(not is_key(kind, m) for m in range(tt)))
                        for b in range(TB):
                            if kind != "moba" and tile >= 14:
                                src = kvm[:, b, (tile - 14) * P:(tile - 13) * P]
                            elif kind != "moba" and tile >= 12:
                                c = 3 * SELF_W + (tile - 12) * P
                                src = v[:, b, c:c + P]
                            else:
                                src = v[:, b, tile * P:(tile + 1) * P]
                            o = (t % 2) * S + b * P
                            ins = pe.transpose(ps[:, t // 2, o:o + P], src, ident[:])
                        if t % 2:
                            ins.then_inc(qk_turned, 1)

            def attend(u0, groups, kind, w):
                def scores(n):
                    g, u, p = groups[n], u0 + n, (u0 + n) % 2
                    if n >= 2:
                        pe.wait_ge(prob_made, u - 1)
                    for h, (qt, kt, half) in enumerate(g["qk"]):
                        rows = slice(0, P) if half is None else slice(half * HD, (half + 1) * HD)
                        q0 = g["b"] * P
                        o = ps[:, 2 * p + h % 2, (h // 2) * S:(h // 2 + 1) * S]
                        ins = pe.matmul(o, qkT[rows, qt, q0:q0 + P], qkT[rows, kt, :], start=True, stop=not g["bias"])
                        if g["bias"]:
                            h0, k = g["bias"]
                            m0 = P if g["b"] == 0 else 0
                            ins = pe.matmul(o, flip[:], strip[:, h0 + min(h, k - 1), m0:m0 + S], start=False, stop=True)
                    ins.then_inc(scored, 1)

                def values(n):
                    g, u, p = groups[n], u0 + n, (u0 + n) % 2
                    if g["diff"]:
                        pe.wait_ge(mixed, 6 * n_diff(groups, n))
                    else:
                        pe.wait_ge(prob_made, u + 1)
                    if n:
                        pe.wait_ge(probT_made, u)
                    for h in range(g["n"]):
                        row = 2 * h if g["diff"] else h
                        for k in range(TB):
                            col = (h * TB + k) * P
                            ins = pe.transpose(ps[:, 4 + col // 512, col % 512:col % 512 + P],
                                               prob[:, p, row, k * P:(k + 1) * P], ident[:])
                    ins.then_inc(probT_turned, 1)

                def outputs(n):
                    g, u, p = groups[n], u0 + n, (u0 + n) % 2
                    pe.wait_ge(probT_made, u + 1)
                    if n >= 2:
                        pe.wait_ge(o_made, u - 1)
                    where, v0 = g["v"]
                    v = kvm if where == "kvm" else pr_view(kind)
                    dv = g["dv"]
                    for h in range(g["n"]):
                        for k in range(TB):
                            ins = pe.matmul(ps[:, 6 + p, h * dv:(h + 1) * dv], probT[:, h, k, :],
                                            v[:, k, v0 + h * dv:v0 + (h + 1) * dv], start=k == 0, stop=k == TB - 1)
                    ins.then_inc(pv_done, 1)

                pe.wait_ge(flip_loaded, 16)
                if kind == "moba":
                    pe.wait_ge(strip_loaded, 16 * 20)
                else:
                    pe.wait_ge(strip_ready, (2, 5)[w])
                pe.wait_ge(q_copied, 8 * (w + 1))
                pe.wait_ge(k_copied, 8 * (w + 1))
                scores(0)
                for n in range(len(groups)):
                    if n + 1 < len(groups):
                        scores(n + 1)
                    values(n)
                    outputs(n)

            pe.wait_ge(ident_loaded, 16)
            pe.wait_ge(rows_loaded, 16 * 16)
            pe.transpose(ps[:, 0, 0:70], grow[0:70, :], ident[0:70, 0:70]).then_inc(gcol_turned, 1)
            pe.wait_ge(qscale_made, 1)
            for i in range(2):
                kind = ("rel", "diff")[i]
                pe.wait_ge(normed, TB * (n_of(i, T_FFN1) + 1))
                turn(nat)
                ffn_phase(2 * i, c_ffn1(i), 4 * (t_of(i, T_FFN1) + 1))
                pe.wait_ge(normed, TB * (n_of(i, T_MEM) + 1))
                turn(nat)
                pe.wait_ge(turn_lo, 4 * (t_of(i, T_MEM) + 1))
                pe.wait_ge(x_updated, 4 * i + 2)
                project(g_kv(i), c_kv(i), 1)
                pe.wait_ge(normed, TB * (n_of(i, T_MIX) + 1))
                turn(nat)
                pe.wait_ge(turn_lo, 4 * (t_of(i, T_MIX) + 1))
                if i == 0:
                    pe.wait_ge(rel_loaded, 32)
                    for k in range(2):
                        ins = pe.transpose(ps[:, 7, 12 * k:12 * k + 12], rel_rows[0:12, 1 + k * P:1 + (k + 1) * P], ident[0:12, 0:12])
                    ins.then_inc(ext_turned, 1)
                    pe.wait_ge(ext_made, 1)
                    for k in range(2):
                        ins = pe.matmul(ps[0:12, 7, :], ang[:, 0, 12 * k:12 * k + 12],
                                        qk_flat[:, 512 * k:512 * (k + 1)],
                                        start=k == 0, stop=k == 1)
                    ins.then_inc(ext_rows, 1)
                    pe.wait_ge(ext_copied, 1)
                project(g_in(i), c_in(i), 5)
                pe.wait_ge(proj_read, g_in(i) + 5)
                if i == 0:
                    pe.wait_ge(head_normed, 6)
                else:
                    pe.wait_ge(rope_step, 16)
                turn_qk(i, kind)
                attend(u_layer(i), attention_groups(kind), kind, i)
                pe.wait_ge(o_made, u_layer(i) + 8)
                if i == 1:
                    pe.wait_ge(sub_step, 7)
                turn(nat)
                pe.wait_ge(turn_lo, 4 * (t_of(i, T_O) + 1))
                project(g_out(i), c_out(i), 2)
                pe.wait_ge(normed, TB * (n_of(i, T_FFN2) + 1))
                turn(nat)
                pe.wait_ge(proj_read, g_out(i) + 2)
                ffn_phase(2 * i + 1, c_ffn2(i), 4 * (t_of(i, T_FFN2) + 1))
            pe.wait_ge(x_updated, 8)
            turn(x)
            pe.wait_ge(turn_lo, 4 * (t_moba + 1))
            pe.wait_ge(rel_loaded, 64)
            pe.matmul(ps[0:8, 7, :], rel_rows[0:32, 0:8], qk_flat[0:32, 0:512],
                      start=True, stop=True).then_inc(ext_rows, 1)
            pe.wait_ge(ext_copied, 2)
            project(g_moba, c_moba, 6)
            pe.wait_ge(proj_read, g_moba + 6)
            turn_qk(2, "moba")
            attend(u_moba, attention_groups("moba"), "moba", 2)
            pe.wait_ge(o_made, u_moba + 4)
            turn(nat)
            pe.wait_ge(turn_lo, 4 * (t_moba_o + 1))
            project(g_moba_out, c_moba_out, 2)
            pe.wait_ge(ln_step, LN_STEPS)
            turn(x)
            pe.wait_ge(turn_lo, 4 * (t_moe + 1))
            pe.wait_ge(wr_ready, 1)
            for b in range(TB):
                for k in range(KT):
                    l = slice(b * P, (b + 1) * P)
                    ins = three(ps[:, 4 + b, 0:N_E], xT_hi[:, k, l], xT_lo[:, k, l], wr_hi[:, k, :], wr_lo[:, k, :],
                                k == 0, k == KT - 1)
            ins.then_inc(logits_done, 1)
            pe.wait_ge(route_step, ROUTE_EXP)
            pe.matmul(ps[:, 6, 0:N_E], before, chosen[:, 0, :], start=True, stop=True)
            pe.matmul(ps[:, 6, N_E:2 * N_E], ones, chosen[:, 0, :], start=True, stop=False)
            pe.matmul(ps[:, 6, N_E:2 * N_E], before, chosen[:, 1, :], start=False, stop=True)
            pe.matmul(ps[:, 6, 2 * N_E:3 * N_E], ones, chosen[:, 0, :], start=True, stop=False)
            pe.matmul(ps[:, 6, 2 * N_E:3 * N_E], ones, chosen[:, 1, :], start=False, stop=True).then_inc(crowd_done, 1)

            def gather(e, q, bank, par):
                for k in range(4):
                    f = slice((4 * q + k) * P, (4 * q + k + 1) * P)
                    o = ps[:, bank, k * P:(k + 1) * P]
                    for b in range(TB):
                        pe.matmul(o, xn_hi[:, b, f], pick[:, par, b, :], start=b == 0, stop=False)
                        ins = pe.matmul(o, xn_lo[:, b, f], pick[:, par, b, :], start=False, stop=b == 1)
                ins.then_inc(gathered, 1)

            def scatter():
                for b in range(TB):
                    for h in range(2):
                        o = ps[:, 4 + 2 * b + h, :]
                        l, r = pickT[:, b * P:(b + 1) * P], slice(h * 512, (h + 1) * 512)
                        pe.matmul(o, l, y_hi[:, r], start=False, stop=False, skip_group_check=True)
                        ins = pe.matmul(o, l, y_lo[:, r], start=False, stop=False, skip_group_check=True)
                return ins

            def bias(bank, col, par):
                pe.matmul(ps[:, bank, :], sel[:, par, :], bias_parts[:, col:col + 512], start=True, stop=False)

            def rows_in(c, bank, h, laps, stop):
                pe.wait_ge(lo_made, c + 1 + LAP * laps)
                s = c % CUT
                for k in range(4):
                    w = slice(k * 512, (k + 1) * 512)
                    ins = three(ps[:, bank, :], xs_hi[:, 4 * h + k, :], xs_lo[:, 4 * h + k, :],
                                w_hi[:, s, w], w_lo[:, s, w], False, stop and k == 3)
                ins.then_inc(chunk_used, 1)

            def rows_out(c, bank, h, laps, stop):
                pe.wait_ge(lo_made, c + 1 + LAP * laps)
                s = c % CUT
                for k in range(4):
                    w = slice(k * 512, (k + 1) * 512)
                    ins = three(ps[:, bank, :], m_hi[:, 4 * h + k, :], m_lo[:, 4 * h + k, :],
                                w_hi[:, s, w], w_lo[:, s, w], False, stop and k == 3)
                ins.then_inc(chunk_used, 1)

            def turn_half(e, half, bank):
                pe.wait_ge(m_act_made, 2 * e + half + 1)
                for k in range(4):
                    ins = pe.transpose(ps[:, bank, k * P:(k + 1) * P], m_act[:, half, k * P:(k + 1) * P], ident[:])
                ins.then_inc(m_turned, 1)

            def expert(e, par, c, laps):
                g0 = 2 * par
                g1 = 2 - g0
                pe.wait_ge(xs_lo_made, 2 * e + 2)
                bias(g0, 0, par)
                rows_in(c, g0, 0, laps, False)
                rows_in(c + 1, g0, 1, laps, True)
                pe.wait_ge(y_lo_made, e + 1)
                scatter().then_inc(scattered, 1)
                bias(g0 + 1, D, par)
                rows_in(c + 2, g0 + 1, 0, laps, False)
                rows_in(c + 3, g0 + 1, 1, laps, True)
                bias(g1, 512, par)
                rows_in(c + 4, g1, 0, laps, False)
                rows_in(c + 5, g1, 1, laps, True)
                turn_half(e, 0, g0)
                for b in range(TB):
                    pe.transpose(ps[:, g0 + 1, b * P:(b + 1) * P], pick[:, par, b, :].bitcast(F32), ident[:])
                for b in range(TB):
                    ins = pe.matmul(ps[:, g0 + 1, S:S + 1], pick[:, par, b, :].bitcast(F32), gate[:, b, bass.ds(e, 1)],
                                    start=b == 0, stop=b == 1)
                ins.then_inc(pickT_turned, 1)
                bias(g1 + 1, D + 512, par)
                rows_in(c + 6, g1 + 1, 0, laps, False)
                rows_in(c + 7, g1 + 1, 1, laps, True)
                pe.wait_ge(m_lo_made, 2 * e + 1)
                bias(g0, 2 * D, par)
                rows_out(c + 8, g0, 0, laps, False)
                pe.wait_ge(gate_made, e + 2)
                pe.wait_ge(pickT_made, e + 1)
                bias(g0 + 1, 2 * D + 512, par)
                rows_out(c + 9, g0 + 1, 0, laps, False)
                turn_half(e, 1, g1)
                pe.wait_ge(picked, 2 * e + 4)
                gather(e + 1, 0, g1 + 1, 1 - par)
                pe.wait_ge(m_lo_made, 2 * e + 2)
                rows_out(c + 10, g0, 1, laps, True)
                gather(e + 1, 1, g1, 1 - par)
                rows_out(c + 11, g0 + 1, 1, laps, True)

            pe.wait_ge(m_zero, 2)
            pe.wait_ge(xn_lo_made, 2)
            for bank in (4, 5, 6, 7, 2, 3):
                ins = pe.matmul(ps[:, bank, :], pickT[:, 0:P], xn_hi[:, 0, 0:512], start=True, stop=True)
            ins.then_inc(scattered, 1)
            pe.wait_ge(picked, 2)
            gather(0, 0, 1, 0)
            gather(0, 1, 0, 0)

            def round_of_experts(r):
                c0 = MOE_C0 + r * N_E * EXPERT_C
                with pe.Fori(0, N_E // 2) as it:
                    expert(2 * it + r * N_E, 0, c0, 4 * it)
                    expert(2 * it + (r * N_E + 1), 1, c0 + EXPERT_C, 4 * it)

            round_of_experts(0)
            pe.wait_ge(crowd_made, 1)
            more = pe.value_load(crowd_i[0:1, 0:1], min_val=0, max_val=1)
            with pe.If(more > 0):
                round_of_experts(1)
            pe.wait_ge(last_lo, 1)
            scatter().then_inc(last_scattered, 1)


NAMES = ["x", "mem", "positions", "ffn1_norm", "ffn1_w_gate", "ffn1_w_up", "ffn1_w_down", "mix_norm", "mem_norm",
         "w_in", "w_mem_kv", "mem_q_norm", "mem_k_norm", "w_out", "a_q_norm", "a_k_norm", "a_rel_bias",
         "b_q_norm", "b_k_norm", "b_lambda_q1", "b_lambda_k1", "b_lambda_q2", "b_lambda_k2", "b_subln",
         "ffn2_norm", "ffn2_w_gate", "ffn2_w_up", "ffn2_w_down", "rel_bias_2", "a_w_in_2", "a_w_out_2",
         "ln_g_2", "ln_b_2", "moe_w_router_2", "moe_b_router_2", "moe_w_gate_up_2", "moe_b_gate_up_2",
         "moe_w_down_2", "moe_b_down_2"]


def constants():
    f = np.float32
    m = np.arange(512)
    rel = np.clip(255 - m, -128, 128) + 128
    c_rel = np.zeros((P, 2, 512), f)
    for k in range(2):
        c_rel[:, k, :] = rel[None, :] == 1 + k * P + np.arange(P)[:, None]
    n = np.maximum(255 - m, 0)
    large = 16 + (np.log(np.maximum(n, 1).astype(f) / f(16)) / f(math.log(8)) * f(16)).astype(np.int32)
    bucket = np.where(n < 16, n, np.minimum(large, 31))
    c_t5 = (bucket[None, :] == np.arange(32)[:, None]).astype(f)
    masks = np.zeros((P, 3 * P + 34), f)
    i = np.arange(P)
    masks[:, 0:P] = i[None, :]
    masks[:, P:2 * P] = i[:, None] < i[None, :]
    masks[:, 2 * P:3 * P] = 1
    for e in range(34):
        for r in range(3):
            masks[32 * r + e % N_E, 3 * P + e] = 1
    e = np.arange(N_E)
    return {"c_ident": np.eye(P, dtype=f), "c_flip": np.eye(P, dtype=f)[::-1].copy(), "c_rel": c_rel.reshape(P, 1024), "c_t5": c_t5, "c_masks": masks,
            "c_tri": (e[None, :] < e[:, None]).astype(f).reshape(-1),
            "c_inv_freq": (f(1.0) / (f(10000.0) ** (np.arange(0, HD, 2, dtype=f) / f(HD)))).astype(f)}


def kernel(**inputs):
    import concourse.bacc as bacc
    from concourse.bass_utils import run_bass_kernel_spmd

    nc = bacc.Bacc("TRN2", target_bir_lowering=False, num_devices=1)
    arrays, aps = {}, {}
    for name, v in [(n, inputs[n]) for n in NAMES] + list(constants().items()):
        v = np.ascontiguousarray(v)
        arrays["in_" + name] = v
        aps[name] = nc.dram_tensor("in_" + name, v.shape, mybir.dt.from_np(v.dtype), kind="ExternalInput").ap()
    out = nc.dram_tensor("out", (1, S, D), F32, kind="ExternalOutput").ap()
    build(nc, aps, out)
    r = run_bass_kernel_spmd(nc, [arrays], core_ids=[0])
    return r.results[0]["out"]
```

```python
from contextlib import ExitStack
import math

import numpy as np

import concourse.bass as bass
from concourse import mybir

F32 = mybir.dt.float32
F32R = mybir.dt.float32r
BF16 = mybir.dt.bfloat16
I32 = mybir.dt.int32
ALU = mybir.AluOpType
ACT = mybir.ActivationFunctionType
AX = mybir.AxisListType

P = 128
D = 1024
KT = D // P
TB = 2
S = TB * P
HD = 64
D_FF = 2816
SELF_W = 768
IN_W = 2560
IN_ORDER = (4, 0, 1, 2, 3)
N_E = 32
TOP_K = 4
NEG = -1e30
EPS = 1e-6
LN_EPS = 1e-5
ALPHA = 2.0 ** 0.25
LAMBDA_INIT = 0.8 - 0.6 * math.exp(-0.3)
LIMIT = 7.0
SWIGLU_ALPHA = 1.702

TRIG_STEPS = 20
ROUTE_EXP = 18
LN_STEPS = 12
MOE_LOADS = 16 * 8
MASK_W = 4 * 128 + 64 + 34
PI_BELOW = 3.1415925

CH = 2048
RAW = 6
CUT = 3
AHEAD = 2
MOE_CUT, MOE_AHEAD = 4, 3
LAP = 6

FFN_PAIRS = D_FF // 256
FFN_C = 3 * FFN_PAIRS
KV_C, IN_C, OUT_C = 2, 10, 4
LAYER_C = 2 * FFN_C + KV_C + IN_C + OUT_C
MOBA_IN_C = 12
MOE_C0 = 2 * LAYER_C + MOBA_IN_C + OUT_C
EXPERT_C = 12
SLOTS = 64
ROUNDS = S // SLOTS
EV = ROUNDS * N_E + 2
REL_W = 384


def is_key(kind, tile):
    return tile >= 8 if kind == "moba" else 6 <= tile < 12 or tile >= 14


def n_diff(groups, n):
    return sum(g["diff"] for g in groups[:n + 1])


def build(nc, a, out):
    with ExitStack() as ctx:
        sem = lambda name: ctx.enter_context(nc.semaphore(name))

        def sb(name, shape, dt=F32, stack=ctx):
            return stack.enter_context(nc.sbuf_tensor("sb_" + name, shape, dt))

        raw = sb("raw", [P, RAW, CH])
        w_hi = sb("w_hi", [P, CUT, CH], F32R)
        w_lo = sb("w_lo", [P, CUT, CH], F32R)
        x = sb("x", [P, TB, D])
        more_hi = ExitStack()
        w_hi3 = sb("w_hi3", [P, CH], F32R, more_hi)
        more_hi.close()
        nat = sb("nat", [P, TB, D])
        ident = sb("ident", [P, P])
        flip = sb("flip", [P, P])
        gcol = sb("gcol", [P, 72])
        grow = sb("grow", [P, P])
        qscale = sb("qscale", [P, 4])
        stat = sb("stat", [P, 16])
        bias_parts = sb("bias_parts", [96, 3 * D], BF16)
        bc = sb("bc", [P, 512])
        inv_row = sb("inv_row", [P, 32])
        pos_i = sb("pos_i", [P, TB], I32)
        pos_f = sb("pos_f", [P, TB])
        trig = sb("trig", [P, TB, 2, 32])
        ang = sb("ang", [P, 5, TB * 32])
        turns_i = sb("turns_i", [P, TB * 32], I32)
        lam = sb("lam", [P, 8])

        early = ExitStack()
        strip = sb("strip", [P, 12, REL_W], stack=early)
        early.close()
        late = ExitStack()
        m = sb("m", [P, KT, P], F32R, late)
        xs = sb("xs", [P, KT, P], F32R, late)
        y_hi = sb("y_hi", [P, D], F32R, late)
        y_lo = sb("y_lo", [P, D], F32R, late)
        late.close()
        turned_rows = ExitStack()
        xT_hi = sb("xT_hi", [P, KT, S], F32R, turned_rows)
        xT_lo = sb("xT_lo", [P, KT, S], F32R, turned_rows)
        spare = sb("spare", [P, 12 * REL_W - 2 * KT * S], stack=turned_rows)
        ffn = ExitStack()
        a_hi = sb("a_hi", [P, 2, 512], F32R, ffn)
        a_lo = sb("a_lo", [P, 2, 512], F32R, ffn)
        sig = sb("sig", [P, 2, 512], stack=ffn)
        gated = sb("gated", [P, 2, 512], stack=ffn)
        act = sb("act", [P, 2, 512], stack=ffn)
        ffn.close()
        att = ExitStack()
        pr = sb("pr", [P, TB * 3 * D], stack=att)
        qkT = sb("qkT", [P, 16, S], stack=att)
        kvm = sb("kvm", [P, TB, 512], stack=att)
        prob = sb("prob", [P, 2, 4, S], stack=att)
        probT = sb("probT", [P, 4, TB, P], stack=att)
        sums = sb("sums", [P, TB, 32], stack=att)
        soft = sb("soft", [P, 2, 24], stack=att)
        att.close()
        moe, routing = ExitStack(), ExitStack()
        xn_hi = sb("xn_hi", [P, TB, D], F32R, moe)
        xn_lo = sb("xn_lo", [P, TB, D], F32R, moe)
        pick = sb("pick", [P, 2, TB, P], F32R, moe)
        pickT = sb("pickT", [P, S], F32R, moe)
        slot_gate = sb("slot_gate", [P, 2], stack=moe)
        sel = sb("sel", [96, 2, P], BF16, moe)
        gate = sb("gate", [P, TB, EV], stack=moe)
        place = sb("place", [P, TB, EV], stack=moe)
        more_lo = ExitStack()
        w_lo3 = sb("w_lo3", [P, CH], F32R, more_lo)
        more_lo.close()
        ln = sb("ln", [P, 2, 2, D], stack=moe)
        crowd_i = sb("crowd_i", [P, 2], I32, moe)
        masks = sb("masks", [P, MASK_W], stack=moe)
        iota_row, before, ones = masks[:, 0:P], masks[:, P:2 * P], masks[:, 2 * P:3 * P]
        first_slots, fold = masks[:, 3 * P:4 * P], masks[:, 4 * P:4 * P + SLOTS]
        onehot96 = masks[0:96, MASK_W - 34:MASK_W]
        wr_hi = sb("wr_hi", [P, KT, N_E], F32R, routing)
        wr_lo = sb("wr_lo", [P, KT, N_E], F32R, routing)
        wr = sb("wr", [P, KT, N_E], stack=routing)
        lg = sb("lg", [P, TB, N_E], stack=routing)
        lg_row = sb("lg_row", [P, N_E], stack=routing)
        tri = sb("tri", [P, N_E, N_E], stack=routing)
        above = sb("above", [P, N_E, N_E], stack=routing)
        equal = sb("equal", [P, N_E, N_E], stack=routing)
        rank = sb("rank", [P, TB, N_E], stack=routing)
        chosen = sb("chosen", [P, TB, N_E], stack=routing)
        crowd = sb("crowd", [P, N_E + 4], stack=routing)
        routing.close()
        h_rows = sb("h_rows", [P, 2, 2, 512], stack=moe)
        m_g = sb("m_g", [P, 256], stack=moe)
        m_sig = sb("m_sig", [P, 256], stack=moe)
        m_u = sb("m_u", [P, 256], stack=moe)
        m_gu = sb("m_gu", [P, 256], stack=moe)
        m_act = sb("m_act", [P, 2, 256], stack=moe)
        moe.close()
        turned_rows.close()

        def cut_slot(c):
            s = c % (CUT if c < MOE_C0 else MOE_CUT)
            return (w_hi[:, s, :], w_lo[:, s, :]) if s < CUT else (w_hi3[:], w_lo3[:])

        ps = ctx.enter_context(nc.psum_tensor("ps", [P, 8, 512], F32))

        qk_flat = qkT[:].rearrange("p a b -> p (a b)")
        rel_rows = probT[:].rearrange("p a b c -> p (a b c)")
        mem = prob[:].rearrange("p a b c -> p (a b c)").rearrange("p (b d) -> p b d", b=TB)
        ext = nc.dram_tensor("ext", (3, 12, 512), F32)

        raw_loaded = [sem(f"raw_loaded{i}") for i in range(RAW)]
        hi_made, lo_made, chunk_used = sem("hi_made"), sem("lo_made"), sem("chunk_used")
        x_loaded, ident_loaded, rows_loaded = sem("x_loaded"), sem("ident_loaded"), sem("rows_loaded")
        small_loaded = sem("small_loaded")
        up_limited = sem("up_limited")
        flip_loaded = sem("flip_loaded")
        bias_loaded, bias_step, bias_made = sem("bias_loaded"), sem("bias_step"), sem("bias_made")
        gcol_turned, gcol_made, qscale_made = sem("gcol_turned"), sem("gcol_made"), sem("qscale_made")
        squared, ms_made, std_made, rstd_made, normed = (sem("squared"), sem("ms_made"), sem("std_made"),
                                                         sem("rstd_made"), sem("normed"))
        turned, turn_hi, turn_lo = sem("turned"), sem("turn_hi"), sem("turn_lo")
        sig_made, gated_made, act_made = sem("sig_made"), sem("gated_made"), sem("act_made")
        act_hi, act_lo = sem("act_hi"), sem("act_lo")
        x_updated = sem("x_updated")
        mem_loaded, proj_read = sem("mem_loaded"), sem("proj_read")
        rel_loaded, ext_turned, ext_rows, ext_made, ext_copied, ext_stored, strip_loaded, strip_ready = (
            sem("rel_loaded"), sem("ext_turned"), sem("ext_rows"), sem("ext_made"), sem("ext_copied"),
            sem("ext_stored"), sem("strip_loaded"), sem("strip_ready"))
        head_sq, head_sum, head_ms, head_std, head_rstd, head_normed = (
            sem("head_sq"), sem("head_sum"), sem("head_ms"), sem("head_std"), sem("head_rstd"),
            sem("head_normed"))
        rope_step = sem("rope_step")
        qk_turned, q_copied, k_copied = sem("qk_turned"), sem("q_copied"), sem("k_copied")
        scored, max_made, prob_made, total_read, mixed, probT_turned, probT_made, pv_done, o_made = (
            sem("scored"), sem("max_made"), sem("prob_made"), sem("total_read"),
            sem("mixed"), sem("probT_turned"), sem("probT_made"), sem("pv_done"), sem("o_made"))
        sub_step, lam_step, lam_exp, trig_step, trig_sin = (sem("sub_step"), sem("lam_step"),
                                                          sem("lam_exp"), sem("trig_step"), sem("trig_sin"))
        ln_step, ln_sq, ln_std = sem("ln_step"), sem("ln_sq"), sem("ln_std")
        moe_loaded, wr_cut, wr_ready, logits_done, route_step, route_exp, crowd_done, crowd_made = (
            sem("moe_loaded"), sem("wr_cut"), sem("wr_ready"), sem("logits_done"), sem("route_step"),
            sem("route_exp"), sem("crowd_done"), sem("crowd_made"))
        xn_hi_made, xn_lo_made = sem("xn_hi_made"), sem("xn_lo_made")
        m_zero, acc_zeroed = sem("m_zero"), sem("acc_zeroed")
        picked, gathered, xs_hi_made, xs_lo_made = (sem("picked"), sem("gathered"), sem("xs_hi_made"),
                                                    sem("xs_lo_made"))
        limited, m_sig_made, m_gu_made, m_act_made = (sem("limited"), sem("m_sig_made"), sem("m_gu_made"),
                                                      sem("m_act_made"))
        h_read = sem("h_read")
        folded, m_hi_made, m_lo_made, pickT_turned, pickT_made, gate_made = (
            sem("folded"), sem("m_hi_made"), sem("m_lo_made"), sem("pickT_turned"), sem("pickT_made"),
            sem("gate_made"))
        y_hi_made, y_lo_made, scattered, last_hi, last_lo, last_scattered = (
            sem("y_hi_made"), sem("y_lo_made"), sem("scattered"), sem("last_hi"),
            sem("last_lo"), sem("last_scattered"))
        out_ready, out_stored = sem("out_ready"), sem("out_stored")

        block = ctx.enter_context(nc.Block())

        c_ffn1 = lambda i: i * LAYER_C
        c_kv = lambda i: i * LAYER_C + FFN_C
        c_in = lambda i: c_kv(i) + KV_C
        c_out = lambda i: c_in(i) + IN_C
        c_ffn2 = lambda i: c_out(i) + OUT_C
        c_moba = 2 * LAYER_C
        c_moba_out = c_moba + MOBA_IN_C
        round_laps = lambda r: (N_E * EXPERT_C // LAP) * r
        g_kv, g_in, g_out = (lambda i: 8 * i), (lambda i: 8 * i + 1), (lambda i: 8 * i + 6)
        g_moba, g_moba_out = 16, 22
        u_layer, u_moba = (lambda i: 8 * i), 16
        T_FFN1, T_MEM, T_MIX, T_O, T_FFN2 = range(5)
        t_of = lambda i, which: 5 * i + which
        t_moba, t_moba_o, t_moe = 10, 11, 12
        n_of = lambda i, which: 4 * i + (which if which < 3 else 3)
        gain0 = {T_FFN1: 0, T_MEM: 16, T_MIX: 32, T_FFN2: 48}

        def attention_groups(kind):
            groups = []
            for b in range(TB):
                if kind == "moba":
                    for h0 in (0, 4):
                        groups.append(dict(b=b, qk=[(h, 8 + h, None) for h in range(h0, h0 + 4)],
                                           bias=(h0, 4), dv=P, v=("pr", 2 * D + h0 * P), o=h0 * P, n=4, diff=False))
                    continue
                groups.append(dict(b=b, qk=[(12 + h // 2, 14 + h // 2, h % 2) for h in range(4)], bias=None,
                                   dv=HD, v=("kvm", 256), o=SELF_W, n=4, diff=False))
                for h0 in (0, 4, 8):
                    qk = [(h // 2, 6 + h // 2, h % 2) for h in range(h0, h0 + 4)]
                    if kind == "rel":
                        groups.append(dict(b=b, qk=qk, bias=(h0, 4), dv=HD, v=("pr", 2 * SELF_W + h0 * HD),
                                           o=h0 * HD, n=4, diff=False))
                    else:
                        groups.append(dict(b=b, qk=qk, bias=(0, 1), dv=2 * HD, v=("pr", 2 * SELF_W + h0 * HD),
                                           o=h0 * HD, n=2, diff=True))
            return groups

        def pr_width(kind):
            return 3 * D if kind == "moba" else IN_W

        def pr_view(kind):
            w = pr_width(kind)
            return pr[:, 0:TB * w].rearrange("p (b w) -> p b w", b=TB)

        def row_by_distance(heads):
            return rel_rows[0:heads, 512:1024]

        @block.sync
        def _(sp):
            def load_chunk(c, src, laps=0, shape=None):
                if c >= RAW or not isinstance(laps, int):
                    sp.wait_ge(lo_made, LAP * laps + (c - RAW + 1))
                dst = raw[:, c % RAW, :].rearrange("p (a n) -> p a n", a=shape)
                sp.dma_start(dst, src).then_inc(raw_loaded[c % RAW], 16)

            def ffn_chunks(c0, wg, wu, wd):
                gsrc = lambda w, j: w.rearrange("(k p) f -> p k f", p=P)[:, :, bass.ds(j * 256, 256)]
                dsrc = lambda j: wd.rearrange("(j k p) n -> j p k n", p=P, k=2)[j]
                dsl = lambda j: wd[bass.ds(j * 256, 256), :].rearrange("(k p) n -> p k n", p=P)
                load_chunk(c0, gsrc(wg, 0), shape=KT)
                load_chunk(c0 + 1, gsrc(wu, 0), shape=KT)
                if c0 == 0:
                    small_loads()

                def two_steps(it):
                    for jj in range(2):
                        j = 1 + jj + 2 * it
                        c = c0 + 2 + 3 * jj
                        load_chunk(c, gsrc(wg, j), it, shape=KT)
                        load_chunk(c + 1, gsrc(wu, j), it, shape=KT)
                        load_chunk(c + 2, dsl(j - 1), it, shape=2)

                two_steps(0)
                with sp.Fori(1, (FFN_PAIRS - 1) // 2) as it:
                    two_steps(it)
                load_chunk(c0 + FFN_C - 1, dsl(FFN_PAIRS - 1), shape=2)

            def product_chunks(c0, w, order):
                for n, col in enumerate(order):
                    for h in range(2):
                        src = w[h * 512:(h + 1) * 512, col * 512:(col + 1) * 512].rearrange("(k p) n -> p k n", p=P)
                        load_chunk(c0 + 2 * n + h, src, shape=4)

            def load_strips(n, heads, used):
                sp.wait_ge(ext_copied, n + 1)
                sp.dma_start(ext[n, 0:heads, :], row_by_distance(heads)).then_inc(ext_stored, 16)
                sp.wait_ge(ext_stored, 16 * (n + 1))
                sp.wait_ge(chunk_used, used)
                for h in range(heads):
                    src = bass.AP(ext, (n * 12 + h) * 512, [[1, P], [1, REL_W]])
                    sp.dma_start(strip[:, h, :], src).then_inc(strip_loaded, 16)

            tok = lambda t: t.rearrange("(b p) d -> p b d", p=P)
            rows = lambda v, n: bass.AP(v.tensor, v.offset, [[0, P], [1, n]])
            sp.dma_start(x[:], tok(a["x"][0])).then_inc(x_loaded, 16)
            sp.dma_start(ident[:], a["c_ident"]).then_inc(ident_loaded, 16)
            for n, name in enumerate(("ffn1_norm", "mem_norm", "mix_norm", "ffn2_norm")):
                sp.dma_start(grow[16 * n:16 * n + 16, :], a[name].rearrange("i (k p) -> (i k) p", p=P)).then_inc(rows_loaded, 16)
            for r, name, n in ((64, "mem_q_norm", 2), (66, "mem_k_norm", 2), (68, "a_q_norm", 1), (69, "a_k_norm", 1)):
                sp.dma_start(grow[r:r + n, :].rearrange("i (h d) -> i h d", h=2),
                             bass.AP(a[name].tensor, a[name].offset, [[HD, n], [0, 2], [1, HD]])).then_inc(rows_loaded, 16)

            def small_loads():
                sp.dma_start(mem, tok(a["mem"][0])).then_inc(mem_loaded, 16)
                for r in range(3):
                    sp.dma_start(qk_flat[32 * r:32 * r + 32, 0:2 * D], a["moe_b_gate_up_2"][0]).then_inc(bias_loaded, 16)
                    sp.dma_start(qk_flat[32 * r:32 * r + 32, 2 * D:3 * D], a["moe_b_down_2"][0]).then_inc(bias_loaded, 16)
                sp.dma_start(flip[:], a["c_flip"]).then_inc(flip_loaded, 16)
                for n, name in enumerate(("b_lambda_q1", "b_lambda_k1", "b_lambda_q2", "b_lambda_k2", "b_q_norm",
                                          "b_k_norm")):
                    sp.dma_start(bc[:, HD * n:HD * (n + 1)], rows(a[name][0], HD)).then_inc(small_loaded, 16)
                sp.dma_start(bc[:, 384:512], rows(a["b_subln"][0], P)).then_inc(small_loaded, 16)
                sp.dma_start(inv_row[:], rows(a["c_inv_freq"], 32)).then_inc(small_loaded, 16)
                with nc.allow_non_contiguous_dma(reason="256 positions, one per partition"):
                    sp.dma_start(pos_i[:], a["positions"][0].rearrange("(b p) -> p b", p=P)).then_inc(small_loaded, 16)

            for i in range(2):
                ffn_chunks(c_ffn1(i), a["ffn1_w_gate"][i], a["ffn1_w_up"][i], a["ffn1_w_down"][i])
                if i == 0:
                    sp.wait_ge(bias_made, 1)
                    sp.dma_start(qk_flat[:, 0:4 * S], a["c_rel"]).then_inc(rel_loaded, 16)
                    sp.dma_start(rel_rows[0:12, 0:257], a["a_rel_bias"][0]).then_inc(rel_loaded, 16)
                product_chunks(c_kv(i), a["w_mem_kv"][i], (0,))
                product_chunks(c_in(i), a["w_in"][i], IN_ORDER)
                product_chunks(c_out(i), a["w_out"][i], range(2))
                if i == 0:
                    load_strips(0, 12, c_out(0))
                    sp.wait_ge(o_made, u_layer(1))
                    sp.dma_start(mem, tok(a["mem"][0])).then_inc(mem_loaded, 16)
                ffn_chunks(c_ffn2(i), a["ffn2_w_gate"][i], a["ffn2_w_up"][i], a["ffn2_w_down"][i])
            sp.wait_ge(o_made, u_moba)
            sp.dma_start(qk_flat[0:32, 0:2 * S], a["c_t5"]).then_inc(rel_loaded, 16)
            sp.dma_start(rel_rows[0:32, 0:8], a["rel_bias_2"]).then_inc(rel_loaded, 16)
            product_chunks(c_moba, a["a_w_in_2"][0], range(6))
            product_chunks(c_moba_out, a["a_w_out_2"][0], range(2))
            load_strips(1, 8, c_moba_out)
            sp.wait_ge(o_made, u_moba + 4)
            sp.dma_start(masks[:], a["c_masks"]).then_inc(moe_loaded, 16)
            for n in range(2):
                sp.dma_start(ln[:, n, 0, :], rows(a["ln_g_2"][0, n], D)).then_inc(moe_loaded, 16)
                sp.dma_start(ln[:, n, 1, :], rows(a["ln_b_2"][0, n], D)).then_inc(moe_loaded, 16)
            sp.dma_start(wr[:], a["moe_w_router_2"][0].rearrange("(k p) e -> p k e", p=P)).then_inc(moe_loaded, 16)
            sp.dma_start(lg_row[:], rows(a["moe_b_router_2"][0], N_E)).then_inc(moe_loaded, 16)
            sp.dma_start(tri[:].rearrange("p a b -> p (a b)"), rows(a["c_tri"], N_E * N_E)).then_inc(moe_loaded, 16)

            def expert_chunk(e, n, c, laps):
                if n < 8:
                    col = (n // 4) * 512 + ((n // 2) % 2) * D
                    h = n % 2
                    w = a["moe_w_gate_up_2"][0]
                else:
                    col = ((n - 8) % 2) * 512
                    h = (n - 8) // 2
                    w = a["moe_w_down_2"][0]
                src = w[bass.ds(e, 1), h * 512:(h + 1) * 512, col:col + 512].rearrange("e (k p) n -> p (e k) n", p=P)
                load_chunk(c, src, laps, shape=4)

            def expert_loads(r):
                with sp.Fori(0, N_E // 2 - 1) as it:
                    for n in range(MOE_AHEAD, MOE_AHEAD + 2 * EXPERT_C):
                        expert_chunk(2 * it + n // EXPERT_C, n % EXPERT_C, MOE_C0 + n, round_laps(r) + 4 * it)
                c = MOE_C0 + (N_E - 2) * EXPERT_C
                for n in range(MOE_AHEAD, MOE_AHEAD + 2 * EXPERT_C):
                    expert_chunk((N_E - 2 + n // EXPERT_C) % N_E, n % EXPERT_C, c + n, round_laps(r))

            for n in range(MOE_AHEAD):
                expert_chunk(0, n, MOE_C0 + n, 0)
            expert_loads(0)
            sp.wait_ge(crowd_made, 1)
            more = sp.value_load(crowd_i[0:1, 0:1], min_val=0, max_val=ROUNDS - 1)
            with sp.If(more > 0):
                with sp.Fori(1, more + 1) as r:
                    expert_loads(r)
            sp.wait_ge(out_ready, 2)
            sp.dma_start(tok(out[0]), x[:]).then_inc(out_stored, 16)
            sp.wait_ge(out_stored, 16)

        @block.gpsimd
        def _(pool):
            pool.wait_ge(bias_loaded, 16 * 6)
            n = 0
            for t in range(3):
                src = qk_flat[0:96, t * D:(t + 1) * D]
                part = qk_flat[0:96, 3 * D:3 * D + 512].bitcast(BF16)
                for r in range(3):
                    if r:
                        pool.tensor_tensor(src, src, part, ALU.subtract).then_inc(bias_step, 1)
                        n += 1
                        pool.wait_ge(bias_step, n)
                    pool.tensor_copy(part, src).then_inc(bias_step, 1)
                    n += 1
                    pool.wait_ge(bias_step, n)
                    last = pool.tensor_copy(bias_parts[32 * r:32 * r + 32, t * D:(t + 1) * D],
                                            part[32 * r:32 * r + 32, :])
                    if t < 2 or r < 2:
                        last.then_inc(bias_step, 1)
                        n += 1
                        pool.wait_ge(bias_step, n)
            last.then_inc(bias_made, 1)

        @block.scalar
        def _(sc):
            def cut(c, laps=0):
                sc.wait_ge(raw_loaded[c % RAW], 16 * (c // RAW + 1) + 16 * laps)
                if c >= CUT:
                    sc.wait_ge(chunk_used, c + 1 + LAP * laps - (CUT if c < MOE_C0 + MOE_AHEAD else MOE_CUT))
                sc.activation(cut_slot(c)[0], raw[:, c % RAW, :], ACT.Copy).then_inc(hi_made, 1)

            def warm(func):
                sc.activation(stat[:, 12:13], ident[:, 0:1], func)

            def norm(n, t, src, ready=None):
                warm(ACT.Sqrt)
                if t:
                    sc.wait_ge(turned, 4 * t)
                for b in range(TB):
                    if ready:
                        sc.wait_ge(x_updated, ready + b)
                    sc.activation(nat[:, b, :], src[:, b, :], ACT.Square,
                                  accum_out=stat[:, b:b + 1]).then_inc(squared, 1)
                sc.wait_ge(ms_made, n + 1)
                sc.activation(stat[:, 4:6], stat[:, 2:4], ACT.Sqrt).then_inc(std_made, 1)

            def turn(t, gain=None):
                for q in range(4):
                    sc.wait_ge(turned, 4 * t + q + 1)
                    if gain is None:
                        sc.activation(xT_hi[:, 2 * q:2 * q + 2, :].rearrange("p a b -> p (a b)"), ps[:, q, :],
                                      ACT.Copy).then_inc(turn_hi, 1)
                    else:
                        for k in (2 * q, 2 * q + 1):
                            ins = sc.activation(xT_hi[:, k, :], ps[:, q, (k % 2) * S:(k % 2 + 1) * S],
                                                ACT.Identity, scale=gcol[:, gain + k:gain + k + 1])
                        ins.then_inc(turn_hi, 1)

            def ffn_step(g, c, slot, laps=0):
                sc.wait_ge(chunk_used, c + 1 + LAP * laps)
                sc.activation(sig[:, slot, :], ps[:, 2 * slot, :], ACT.Sigmoid).then_inc(sig_made, 1)
                sc.wait_ge(act_made, g + 1)
                sc.activation(a_hi[:, slot, :], act[:, slot, :], ACT.Copy).then_inc(act_hi, 1)

            def ffn_phase(f, c0, other=None):
                cut(c0 + AHEAD)
                cut(c0 + 1 + AHEAD)
                ffn_step(FFN_PAIRS * f, c0, 0)
                if other:
                    other()
                with sc.Fori(0, (FFN_PAIRS - 1) // 2) as it:
                    for jj in range(2):
                        c = c0 + 2 + 3 * jj
                        cut(c + AHEAD, it)
                        cut(c + 1 + AHEAD, it)
                        ffn_step(2 * it + (FFN_PAIRS * f + 1 + jj), c, 1 - jj, it)
                        cut(c + 2 + AHEAD, it)
                cut(c0 + FFN_C - 1 + AHEAD)

            def project(g0, c0, order, dst, during=None):
                for n, col in enumerate(order):
                    g, c = g0 + n, c0 + 2 * n
                    cut(c + AHEAD)
                    cut(c + 1 + AHEAD)
                    if during and n == len(order) - 1:
                        during()
                    if dst is None:
                        continue
                    sc.wait_ge(chunk_used, c + 2)
                    bank = 4 + 2 * (g % 2)
                    sc.activation(dst[:, :, 512 * col:512 * (col + 1)], ps[:, bank:bank + 2, :],
                                  ACT.Copy).then_inc(proj_read, 1)

            def qk_copies(w, kind):
                for r in range(2):
                    for t in range(8):
                        if is_key(kind, 8 * r + t):
                            sc.wait_ge(qk_turned, 8 * w + 4 * r + t // 2 + 1)
                            sc.activation(qkT[:, 8 * r + t, :], ps[:, t // 2, (t % 2) * S:(t % 2 + 1) * S],
                                          ACT.Copy).then_inc(k_copied, 1)

            def attend(u0, groups):
                def exps(n):
                    g, u, p = groups[n], u0 + n, (u0 + n) % 2
                    sc.wait_ge(max_made, u + 1)
                    for h in range(4):
                        src = ps[:, 2 * p + h % 2, (h // 2) * S:(h // 2 + 1) * S]
                        ins = sc.activation(prob[:, p, h, :], src, ACT.Exp, bias=soft[:, p, h:h + 1],
                                            accum_out=soft[:, p, 4 + h:5 + h])
                    ins.then_inc(prob_made, 1)

                exps(0)
                exps(1)
                for n in range(len(groups)):
                    g, u = groups[n], u0 + n
                    sc.wait_ge(probT_turned, u + 1)
                    if u:
                        sc.wait_ge(pv_done, u)
                    m = g["n"] * TB * P
                    sc.activation(probT[:].rearrange("p a b c -> p (a b c)")[:, 0:m],
                                  ps[:, 4:6, :].rearrange("p a b -> p (a b)")[:, 0:m],
                                  ACT.Copy).then_inc(probT_made, 1)
                    if n + 2 < len(groups):
                        exps(n + 2)

            def layer_norm(n):
                for b in range(TB):
                    sc.wait_ge(ln_step, LN_STEPS * n + 3 * (b + 1))
                    sc.activation(nat[:, b, :], x[:, b, :], ACT.Square,
                                  accum_out=stat[:, b:b + 1]).then_inc(ln_sq, 1)
                sc.wait_ge(ln_step, LN_STEPS * n + 7)
                sc.activation(stat[:, 4:6], stat[:, 2:4], ACT.Sqrt).then_inc(ln_std, 1)

            def head_roots(i):
                warm(ACT.Sqrt)
                sc.wait_ge(head_ms, i + 1)
                sc.activation(sums[:], sums[:], ACT.Sqrt).then_inc(head_std, 1)

            def angles():
                sc.wait_ge(lam_step, 4)
                sc.activation(lam[:, 2:4], lam[:, 0:2], ACT.Exp).then_inc(lam_exp, 1)
                sc.wait_ge(trig_step, TRIG_STEPS)
                sc.activation(trig[:, :, 0, :], ang[:, 3, :].rearrange("p (b f) -> p b f", b=TB), ACT.Sin).then_inc(trig_sin, 1)
                sc.activation(trig[:, :, 1, :], ang[:, 2, :].rearrange("p (b f) -> p b f", b=TB), ACT.Sin).then_inc(trig_sin, 1)

            def memory_norm(i):
                sc.wait_ge(mem_loaded, 16 * (i + 1))
                norm(n_of(i, T_MEM), t_of(i, T_MEM), mem)

            sc.wait_ge(ident_loaded, 16)
            for i in range(2):
                kind = ("rel", "diff")[i]
                if i == 0:
                    sc.wait_ge(x_loaded, 16)
                norm(n_of(i, T_FFN1), t_of(i, T_FFN1), x, 4 * i - 1 if i else None)
                if i == 0:
                    cut(0)
                    cut(1)
                turn(t_of(i, T_FFN1), gain0[T_FFN1] + 8 * i)
                ffn_phase(2 * i, c_ffn1(i), lambda: memory_norm(i))
                turn(t_of(i, T_MEM), gain0[T_MEM] + 8 * i)
                project(g_kv(i), c_kv(i), range(1), kvm, lambda: norm(n_of(i, T_MIX), t_of(i, T_MIX), x, 4 * i + 1))
                turn(t_of(i, T_MIX), gain0[T_MIX] + 8 * i)
                project(g_in(i), c_in(i), IN_ORDER, pr_view("rel"), lambda: head_roots(i))
                qk_copies(i, kind)
                attend(u_layer(i), attention_groups(kind))
                if i == 1:
                    sc.wait_ge(sub_step, 3)
                    sc.activation(sums[:, :, 0:6], sums[:, :, 0:6], ACT.Sqrt).then_inc(sub_step, 1)
                turn(t_of(i, T_O))
                project(g_out(i), c_out(i), range(2), None)
                sc.wait_ge(proj_read, g_out(i) + 2)
                norm(n_of(i, T_FFN2), t_of(i, T_FFN2), x)
                turn(t_of(i, T_FFN2), gain0[T_FFN2] + 8 * i)
                ffn_phase(2 * i + 1, c_ffn2(i), angles if i == 0 else None)
            turn(t_moba)
            project(g_moba, c_moba, range(6), pr_view("moba"))
            qk_copies(2, "moba")
            attend(u_moba, attention_groups("moba"))
            turn(t_moba_o)
            project(g_moba_out, c_moba_out, range(2), None)
            layer_norm(0)
            sc.wait_ge(moe_loaded, MOE_LOADS)
            sc.activation(wr_hi[:], wr[:], ACT.Copy).then_inc(wr_cut, 1)
            sc.wait_ge(ln_step, LN_STEPS)
            turn(t_moe)
            for b in range(TB):
                sc.activation(xn_hi[:, b, :], x[:, b, :], ACT.Copy).then_inc(xn_hi_made, 1)
            sc.wait_ge(route_step, ROUTE_EXP)
            sc.activation(rank[:], rank[:], ACT.Exp).then_inc(route_exp, 1)

            def gathered_rows(e, bank):
                sc.wait_ge(gathered, e + 1)
                sc.activation(xs[:, :, 0:SLOTS], ps[:, bank, :].rearrange("p (k s) -> p k s", k=KT),
                              ACT.Copy).then_inc(xs_hi_made, 1)

            def read_rows(half, up, bank, c, laps):
                sc.wait_ge(chunk_used, c + LAP * laps)
                sc.activation(h_rows[:, half, up, :], ps[:, bank, :], ACT.Copy).then_inc(h_read, 1)

            def sigmoid(e, half):
                sc.wait_ge(limited, 2 * e + half + 1)
                sc.activation(m_sig[:], m_g[:], ACT.Sigmoid, scale=SWIGLU_ALPHA).then_inc(m_sig_made, 1)

            def activations(e, half):
                sc.wait_ge(m_act_made, 2 * e + half + 1)
                sc.activation(m[:, 4 * half:4 * half + 4, 0:SLOTS],
                              m_act[:, half, :].rearrange("p (k s) -> p k s", k=4), ACT.Copy).then_inc(m_hi_made, 1)

            def expert(e, par, c, laps):
                g0 = 2 * par
                g1 = 2 - g0
                sc.wait_ge(chunk_used, c + LAP * laps)
                sc.wait_ge(scattered, e + 1)
                sc.wait_ge(gate_made, e + 1)
                sc.activation(y_hi[:], ps[:, g1:g1 + 2, :].rearrange("p a b -> p (a b)"), ACT.Identity,
                              scale=slot_gate[:, 1 - par:2 - par]).then_inc(y_hi_made, 1)
                for n in range(EXPERT_C):
                    cut(c + n + MOE_AHEAD, laps)
                    if n in (1, 3, 5, 7):
                        half, up = n // 4, (n // 2) % 2
                        read_rows(half, up, (g0, g1)[half] + up, c + n + 1, laps)
                    if n == 5:
                        sigmoid(e, 0)
                        sc.wait_ge(pickT_turned, e + 1)
                        sc.wait_ge(scattered, e + 2)
                        sc.activation(pickT[:], ps[:, g0 + 1, 0:S], ACT.Copy).then_inc(pickT_made, 1)
                        sc.activation(slot_gate[:, par:par + 1], ps[:, g0 + 1, S:S + 1], ACT.Copy).then_inc(gate_made, 1)
                    if n == 6:
                        activations(e, 0)
                    if n == 8:
                        sigmoid(e, 1)
                        activations(e, 1)
                    if n == 10:
                        gathered_rows(e + 1, g1 + 1)

            sc.activation(stat[:, 6:7], stat[:, 4:5], ACT.Sigmoid)
            gathered_rows(0, 1)
            cut(MOE_C0 + AHEAD)

            def round_of_experts(r):
                with sc.Fori(0, N_E // 2) as it:
                    for par in range(2):
                        expert(2 * it + N_E * r + par, par, MOE_C0 + par * EXPERT_C, round_laps(r) + 4 * it)

            round_of_experts(0)
            sc.wait_ge(crowd_made, 1)
            more = sc.value_load(crowd_i[0:1, 0:1], min_val=0, max_val=ROUNDS - 1)
            with sc.If(more > 0):
                with sc.Fori(1, more + 1) as r:
                    round_of_experts(r)
            sc.wait_ge(chunk_used, N_E * EXPERT_C * more + (MOE_C0 + N_E * EXPERT_C))
            sc.activation(y_hi[:], ps[:, 2:4, :].rearrange("p a b -> p (a b)"), ACT.Identity,
                          scale=slot_gate[:, 1:2]).then_inc(last_hi, 1)
            layer_norm(1)

        @block.vector
        def _(ve):
            def cut(c, laps=0):
                ve.wait_ge(hi_made, c + 1 + LAP * laps)
                hi, lo = cut_slot(c)
                ve.tensor_tensor(lo, raw[:, c % RAW, :], hi.bitcast(F32),
                                 ALU.subtract).then_inc(lo_made, 1)

            def norm(n, src):
                ve.wait_ge(squared, TB * (n + 1))
                ve.tensor_scalar(stat[:, 2:4], stat[:, 0:2], 1.0 / D, EPS, ALU.mult, ALU.add).then_inc(ms_made, 1)
                ve.wait_ge(std_made, n + 1)
                ve.reciprocal(stat[:, 6:8], stat[:, 4:6]).then_inc(rstd_made, 1)
                ve.wait_ge(rstd_made, n + 1)
                for b in range(TB):
                    ve.tensor_scalar(nat[:, b, :], src[:, b, :], stat[:, 6 + b:7 + b], None, ALU.mult).then_inc(normed, 1)

            def turn(t, gain=None):
                for q in range(4):
                    ve.wait_ge(turn_hi, 4 * t + q + 1)
                    hi = xT_hi[:, 2 * q:2 * q + 2, :].bitcast(F32)
                    if gain is None:
                        ve.tensor_tensor(xT_lo[:, 2 * q:2 * q + 2, :].rearrange("p a b -> p (a b)"), ps[:, q, :],
                                         hi.rearrange("p a b -> p (a b)"), ALU.subtract).then_inc(turn_lo, 1)
                    else:
                        for k in (2 * q, 2 * q + 1):
                            ins = ve.scalar_tensor_tensor(
                                out=xT_lo[:, k, :], in0=ps[:, q, (k % 2) * S:(k % 2 + 1) * S],
                                scalar=gcol[:, gain + k:gain + k + 1], in1=xT_hi[:, k, :].bitcast(F32),
                                op0=ALU.mult, op1=ALU.subtract)
                        ins.then_inc(turn_lo, 1)

            def ffn_step(g, c, slot, laps=0):
                ve.wait_ge(sig_made, g + 1)
                ve.tensor_tensor(gated[:, slot, :], ps[:, 2 * slot, :], sig[:, slot, :], ALU.mult).then_inc(gated_made, 1)
                ve.wait_ge(gated_made, g + 1)
                ve.wait_ge(chunk_used, c + 2 + LAP * laps)
                ve.tensor_tensor(act[:, slot, :], ps[:, 2 * slot + 1, :], gated[:, slot, :], ALU.mult).then_inc(act_made, 1)
                ve.wait_ge(act_hi, g + 1)
                ve.tensor_tensor(a_lo[:, slot, :], act[:, slot, :], a_hi[:, slot, :].bitcast(F32),
                                 ALU.subtract).then_inc(act_lo, 1)

            def ffn_phase(f, c0, other=None):
                cut(c0 + AHEAD)
                cut(c0 + 1 + AHEAD)
                ffn_step(FFN_PAIRS * f, c0, 0)
                if other:
                    other()
                with ve.Fori(0, (FFN_PAIRS - 1) // 2) as it:
                    for jj in range(2):
                        c = c0 + 2 + 3 * jj
                        cut(c + AHEAD, it)
                        cut(c + 1 + AHEAD, it)
                        ffn_step(2 * it + (FFN_PAIRS * f + 1 + jj), c, 1 - jj, it)
                        cut(c + 2 + AHEAD, it)
                cut(c0 + FFN_C - 1 + AHEAD)
                ve.wait_ge(chunk_used, c0 + FFN_C)
                for b in range(TB):
                    ve.scalar_tensor_tensor(out=x[:, b, :], in0=ps[:, 4 + 2 * b:6 + 2 * b, :].rearrange("p a b -> p (a b)"),
                                            scalar=0.5, in1=x[:, b, :], op0=ALU.mult, op1=ALU.add).then_inc(x_updated, 1)

            def project(g0, c0, n_groups, add=None, during=None):
                for n in range(n_groups):
                    g, c = g0 + n, c0 + 2 * n
                    cut(c + AHEAD)
                    cut(c + 1 + AHEAD)
                    if during:
                        during(n)
                    if add is None:
                        continue
                    ve.wait_ge(chunk_used, c + 2)
                    bank = 4 + 2 * (g % 2)
                    cols = x[:, :, 512 * n:512 * (n + 1)]
                    ve.scalar_tensor_tensor(out=cols, in0=cols, scalar=add, in1=ps[:, bank:bank + 2, :],
                                            op0=ALU.mult, op1=ALU.add).then_inc(proj_read, 1)

            def heads(t, n):
                return t.rearrange("p (h d) -> p h d", h=n)

            def head_squares(i, n):
                v = pr_view("rel")
                col = IN_ORDER[n - 1]
                spans = [(v, 3 * SELF_W, 4, 24), (kvm, 0, 4, 28)] if n == 1 else [(v, 512 * col, 8, 8 * col)]
                ve.wait_ge(proj_read, g_in(i) + n)
                for m, (src, c0, k, s0) in enumerate(spans):
                    done = 5 * i + n - 1 + (m if n == 1 else 1)
                    sq = prob[:].rearrange("p a b c -> p (a b c)")[:, 0:TB * k * HD]
                    sq = sq.rearrange("p (b w) -> p b w", b=TB)
                    ve.tensor_tensor(sq, src[:, :, c0:c0 + k * HD], src[:, :, c0:c0 + k * HD], ALU.mult).then_inc(head_sq, 1)
                    ve.wait_ge(head_sq, done + 1)
                    ve.tensor_reduce(sums[:, :, s0:s0 + k], sq.rearrange("p b (h d) -> p b h d", h=k), AX.X,
                                     ALU.add).then_inc(head_sum, 1)
                    ve.wait_ge(head_sum, done + 1)

            def head_norms(i, n):
                if n:
                    head_squares(i, n)
                if n < 4:
                    return
                v = pr_view("rel")
                spans = [(v, 0, 24, 0), (v, 3 * SELF_W, 4, 24), (kvm, 0, 4, 28)]
                ve.tensor_scalar(sums[:], sums[:], 1.0 / HD, EPS, ALU.mult, ALU.add).then_inc(head_ms, 1)
                ve.wait_ge(head_std, i + 1)
                ve.reciprocal(sums[:], sums[:]).then_inc(head_rstd, 1)
                ve.wait_ge(head_rstd, i + 1)
                for b in range(TB):
                    for src, c0, k, s0 in spans:
                        view = heads(src[:, b, c0:c0 + k * HD], k)
                        ve.tensor_tensor(view, view, sums[:, b, s0:s0 + k].unsqueeze(2).to_broadcast([P, k, HD]),
                                         ALU.mult).then_inc(head_normed, 1)

            def rope_all():
                v = pr_view("rel")
                tmp = prob[:].rearrange("p a b c -> p (a b c)")
                s = 0
                ve.wait_ge(head_normed, 12)
                ve.wait_ge(trig_sin, 2)
                for b in range(TB):
                    for n, gain in ((0, 4), (1, 5)):
                        view = heads(v[:, b, n * SELF_W:(n + 1) * SELF_W], 12)
                        g = bc[:, HD * gain:HD * (gain + 1)].unsqueeze(1).to_broadcast([P, 12, HD])
                        ve.tensor_tensor(view, view, g, ALU.mult).then_inc(rope_step, 1)
                        s += 1
                    ve.wait_ge(rope_step, s)
                    view = heads(v[:, b, 0:2 * SELF_W], 24)
                    x1, x2 = view[:, :, 0:32], view[:, :, 32:64]
                    t1, t2 = heads(tmp[:, 0:SELF_W], 24), heads(tmp[:, SELF_W:2 * SELF_W], 24)
                    cos = trig[:, b, 0, :].unsqueeze(1).to_broadcast([P, 24, 32])
                    sin = trig[:, b, 1, :].unsqueeze(1).to_broadcast([P, 24, 32])
                    for o, p, q, op in ((t1, x2, sin, ALU.mult), (t2, x1, sin, ALU.mult), (x1, x1, cos, ALU.mult),
                                        (x2, x2, cos, ALU.mult), (x1, x1, t1, ALU.subtract), (x2, x2, t2, ALU.add)):
                        ve.tensor_tensor(o, p, q, op).then_inc(rope_step, 1)
                        s += 1
                        ve.wait_ge(rope_step, s)

            def qk_copies(w, kind):
                for r in range(2):
                    for t in range(8):
                        tile = 8 * r + t
                        if is_key(kind, tile):
                            continue
                        ve.wait_ge(qk_turned, 8 * w + tile // 2 + 1)
                        src = ps[:, t // 2, (t % 2) * S:(t % 2 + 1) * S]
                        if kind == "moba":
                            scale = P ** -0.5
                        elif tile >= 12:
                            scale = qscale[:, w:w + 1]
                        else:
                            scale = qscale[:, 2:3] if kind == "rel" else HD ** -0.5
                        ve.tensor_scalar(qkT[:, tile, :], src, scale, None, ALU.mult).then_inc(q_copied, 1)

            def attend(u0, groups, masks_made=None):
                def lead(n):
                    g, u, p = groups[n], u0 + n, (u0 + n) % 2
                    ve.wait_ge(scored, u + 1)
                    s = ps[:, 2 * p:2 * p + 2, :].rearrange("p a (c k) -> p c a k", c=2)
                    if u >= 2:
                        ve.wait_ge(probT_turned, u - 1)
                    for c in range(2):
                        ins = ve.tensor_reduce(soft[:, p, 2 * c:2 * c + 2], s[:, c], AX.X, ALU.max, negate=True)
                    ins.then_inc(max_made, 1)

                def follow(n):
                    g, u, p = groups[n], u0 + n, (u0 + n) % 2
                    ve.wait_ge(prob_made, u + 1)
                    if n >= 2:
                        ve.wait_ge(o_made, u - 1)
                    ve.reciprocal(soft[:, p, 8:12], soft[:, p, 4:8]).then_inc(total_read, 1)
                    ve.wait_ge(total_read, u + 1)
                    if g["diff"]:
                        m = n_diff(groups, n)
                        for h in range(2):
                            ve.tensor_scalar(soft[:, p, 12 + h:13 + h], soft[:, p, 9 + 2 * h:10 + 2 * h],
                                             lam[:, 5:6], None, ALU.mult).then_inc(mixed, 1)
                        ve.wait_ge(mixed, 6 * m - 4)
                        for h in range(2):
                            ve.tensor_scalar(prob[:, p, 2 * h + 1, :], prob[:, p, 2 * h + 1, :],
                                             soft[:, p, 12 + h:13 + h], None, ALU.mult).then_inc(mixed, 1)
                        ve.wait_ge(mixed, 6 * m - 2)
                        for h in range(2):
                            ve.scalar_tensor_tensor(out=prob[:, p, 2 * h, :], in0=prob[:, p, 2 * h, :],
                                                    scalar=soft[:, p, 8 + 2 * h:9 + 2 * h], in1=prob[:, p, 2 * h + 1, :],
                                                    op0=ALU.mult, op1=ALU.subtract).then_inc(mixed, 1)

                def outputs(n):
                    g, u, p = groups[n], u0 + n, (u0 + n) % 2
                    ve.wait_ge(pv_done, u + 1)
                    k, dv = g["n"], g["dv"]
                    dst = nat[:, g["b"], g["o"]:g["o"] + k * dv]
                    src = ps[:, 6 + p, 0:k * dv]
                    if g["diff"]:
                        ve.tensor_copy(dst, src).then_inc(o_made, 1)
                    else:
                        ve.tensor_tensor(heads(dst, k), heads(src, k),
                                         soft[:, p, 8:12].unsqueeze(2).to_broadcast([P, k, dv]), ALU.mult).then_inc(o_made, 1)

                lead(0)
                if masks_made:
                    masks_made()
                lead(1)
                follow(0)
                for n in range(len(groups)):
                    if n + 2 < len(groups):
                        lead(n + 2)
                    if n + 1 < len(groups):
                        follow(n + 1)
                    outputs(n)

            def layer_norm(n):
                s = [LN_STEPS * n]

                def step(ins, by=ln_step):
                    ins.then_inc(by, 1)
                    if by is ln_step:
                        s[0] += 1
                        ve.wait_ge(ln_step, s[0])

                for b in range(TB):
                    step(ve.tensor_reduce(stat[:, 8 + b:9 + b], x[:, b, :], AX.X, ALU.add))
                    step(ve.tensor_scalar(stat[:, 10 + b:11 + b], stat[:, 8 + b:9 + b], 1.0 / D, None, ALU.mult))
                    step(ve.tensor_scalar(x[:, b, :], x[:, b, :], stat[:, 10 + b:11 + b], None, ALU.subtract))
                ve.wait_ge(ln_sq, TB * (n + 1))
                step(ve.tensor_scalar(stat[:, 2:4], stat[:, 0:2], 1.0 / D, LN_EPS, ALU.mult, ALU.add))
                ve.wait_ge(ln_std, n + 1)
                step(ve.reciprocal(stat[:, 6:8], stat[:, 4:6]))
                for b in range(TB):
                    step(ve.scalar_tensor_tensor(out=x[:, b, :], in0=x[:, b, :], scalar=stat[:, 6 + b:7 + b],
                                                 in1=ln[:, n, 0, :], op0=ALU.mult, op1=ALU.mult))
                    step(ve.tensor_tensor(x[:, b, :], x[:, b, :], ln[:, n, 1, :], ALU.add), (ln_step, out_ready)[n])

            ve.wait_ge(gcol_turned, 1)
            ve.tensor_copy(gcol[:, 0:70], ps[:, 0, 0:70]).then_inc(qscale_made, 1)
            ve.wait_ge(qscale_made, 1)
            for n, (q, k) in enumerate(((64, 66), (65, 67), (68, 69))):
                ve.scalar_tensor_tensor(out=qscale[:, n:n + 1], in0=gcol[:, q:q + 1], scalar=HD ** -0.5,
                                        in1=gcol[:, k:k + 1], op0=ALU.mult, op1=ALU.mult).then_inc(qscale_made, 1)
            ve.wait_ge(qscale_made, 4)

            def angles():
                ve.wait_ge(small_loaded, 16 * 9)
                for n in range(2):
                    ve.tensor_tensor(ang[:, n, 0:HD], bc[:, 128 * n:128 * n + 64], bc[:, 128 * n + 64:128 * n + 128],
                                     ALU.mult).then_inc(lam_step, 1)
                    ve.wait_ge(lam_step, 2 * n + 1)
                    ve.tensor_reduce(lam[:, n:n + 1], ang[:, n, 0:HD], AX.X, ALU.add).then_inc(lam_step, 1)
                ve.wait_ge(lam_exp, 1)
                ve.tensor_tensor(lam[:, 4:5], lam[:, 2:3], lam[:, 3:4], ALU.subtract).then_inc(lam_step, 1)
                ve.wait_ge(lam_step, 5)
                ve.tensor_scalar(lam[:, 5:6], lam[:, 4:5], LAMBDA_INIT, None, ALU.add).then_inc(lam_step, 1)
                t = [0]

                def step(ins):
                    ins.then_inc(trig_step, 1)
                    t[0] += 1
                    ve.wait_ge(trig_step, t[0])

                step(ve.tensor_copy(pos_f[:], pos_i[:]))
                for b in range(TB):
                    step(ve.tensor_scalar(ang[:, 0, 32 * b:32 * b + 32], inv_row[:], pos_f[:, b:b + 1], None, ALU.mult))
                step(ve.tensor_scalar(ang[:, 1, :], ang[:, 0, :], 1.0 / (2 * math.pi), None, ALU.mult))
                step(ve.tensor_copy(turns_i[:], ang[:, 1, :]))
                step(ve.tensor_copy(ang[:, 1, :], turns_i[:]))
                c1 = 6.28125
                c2 = float(np.float32(np.round((2 * math.pi - c1) * 2 ** 21) / 2 ** 21))
                c3 = 2 * math.pi - c1 - c2
                src = 0
                for c in (c1, c2, c3):
                    step(ve.scalar_tensor_tensor(out=ang[:, 2, :], in0=ang[:, 1, :], scalar=-c, in1=ang[:, src, :],
                                                 op0=ALU.mult, op1=ALU.add))
                    src = 2
                step(ve.tensor_scalar(ang[:, 3, :], ang[:, 2, :], math.pi / 2, None, ALU.add))
                for k in (2, 3):
                    for bound, op, off in ((math.pi, ALU.is_gt, -2 * math.pi), (-math.pi, ALU.is_lt, 2 * math.pi)):
                        step(ve.tensor_scalar(ang[:, 4, :], ang[:, k, :], bound, off, op, ALU.mult))
                        step(ve.tensor_tensor(ang[:, k, :], ang[:, k, :], ang[:, 4, :], ALU.add))
                    step(ve.tensor_scalar(ang[:, k, :], ang[:, k, :], PI_BELOW, -PI_BELOW, ALU.min, ALU.max))
                assert t[0] == TRIG_STEPS
                ve.wait_ge(lam_step, 6)
                ve.tensor_scalar(bc[:, 384:512], bc[:, 384:512], 1.0 - LAMBDA_INIT, None, ALU.mult).then_inc(lam_step, 1)

            for i in range(2):
                kind = ("rel", "diff")[i]
                norm(n_of(i, T_FFN1), x)
                if i == 0:
                    cut(0)
                    cut(1)
                turn(t_of(i, T_FFN1), gain0[T_FFN1] + 8 * i)
                ffn_phase(2 * i, c_ffn1(i), lambda: norm(n_of(i, T_MEM), mem))
                turn(t_of(i, T_MEM), gain0[T_MEM] + 8 * i)
                project(g_kv(i), c_kv(i), 1)
                norm(n_of(i, T_MIX), x)
                turn(t_of(i, T_MIX), gain0[T_MIX] + 8 * i)
                if i == 0:
                    ve.wait_ge(ext_turned, 1)
                    ve.tensor_copy(ang[:, 0, 0:24], ps[:, 7, 0:24]).then_inc(ext_made, 1)
                    ve.wait_ge(ext_rows, 1)
                    ve.tensor_copy(row_by_distance(12), ps[0:12, 7, :]).then_inc(ext_copied, 1)
                project(g_in(i), c_in(i), 5, during=lambda n: head_norms(i, n))
                if i == 1:
                    rope_all()
                qk_copies(i, kind)

                def masks_made():
                    if i == 0:
                        ve.wait_ge(strip_loaded, 16 * 12)
                        ve.memset(strip[64:P, :, 192:REL_W], NEG).then_inc(strip_ready, 1)
                        ve.memset(strip[0:64, :, 256:REL_W], NEG).then_inc(strip_ready, 1)
                    else:
                        ve.memset(strip[:, 0, :], 0.0).then_inc(strip_ready, 1)
                        ve.wait_ge(strip_ready, 3)
                        ve.memset(strip[64:P, 0, 192:REL_W], NEG).then_inc(strip_ready, 1)
                        ve.memset(strip[0:64, 0, 256:REL_W], NEG).then_inc(strip_ready, 1)

                attend(u_layer(i), attention_groups(kind), masks_made)
                if i == 1:
                    ve.wait_ge(o_made, u_moba)
                    sq = prob[:].rearrange("p a b c -> p (a b c)")[:, 0:2 * SELF_W].rearrange("p (b w) -> p b w", b=TB)
                    o = nat[:, :, 0:SELF_W]
                    ve.tensor_tensor(sq, o, o, ALU.mult).then_inc(sub_step, 1)
                    ve.wait_ge(sub_step, 1)
                    for b in range(TB):
                        ins = ve.tensor_reduce(sums[:, b, 0:6], heads(sq[:, b, :], 6), AX.X, ALU.add)
                    ins.then_inc(sub_step, 1)
                    ve.wait_ge(sub_step, 2)
                    ve.tensor_scalar(sums[:, :, 0:6], sums[:, :, 0:6], 1.0 / P, EPS, ALU.mult, ALU.add).then_inc(sub_step, 1)
                    ve.wait_ge(sub_step, 4)
                    ve.reciprocal(sums[:, :, 0:6], sums[:, :, 0:6]).then_inc(sub_step, 1)
                    ve.wait_ge(sub_step, 5)
                    for b in range(TB):
                        view = heads(nat[:, b, 0:SELF_W], 6)
                        ins = ve.tensor_tensor(view, view, sums[:, b, 0:6].unsqueeze(2).to_broadcast([P, 6, P]), ALU.mult)
                    ins.then_inc(sub_step, 1)
                    ve.wait_ge(sub_step, 6)
                    for b in range(TB):
                        view = heads(nat[:, b, 0:SELF_W], 6)
                        ins = ve.tensor_tensor(view, view, bc[:, 384:512].unsqueeze(1).to_broadcast([P, 6, P]), ALU.mult)
                    ins.then_inc(sub_step, 1)
                turn(t_of(i, T_O))
                project(g_out(i), c_out(i), 2, add=1.0)
                norm(n_of(i, T_FFN2), x)
                turn(t_of(i, T_FFN2), gain0[T_FFN2] + 8 * i)
                ffn_phase(2 * i + 1, c_ffn2(i), angles if i == 0 else None)
            turn(t_moba)
            ve.wait_ge(ext_rows, 2)
            ve.tensor_copy(row_by_distance(8), ps[0:8, 7, :]).then_inc(ext_made, 1)
            ve.wait_ge(ext_made, 2)
            ve.memset(row_by_distance(8)[:, S:512], NEG).then_inc(ext_copied, 1)
            project(g_moba, c_moba, 6)
            qk_copies(2, "moba")
            attend(u_moba, attention_groups("moba"))
            turn(t_moba_o)
            project(g_moba_out, c_moba_out, 2, add=ALPHA)
            ve.wait_ge(proj_read, g_moba_out + 2)
            ve.wait_ge(moe_loaded, MOE_LOADS)
            layer_norm(0)
            ve.wait_ge(wr_cut, 1)
            ve.tensor_tensor(wr_lo[:], wr[:], wr_hi[:].bitcast(F32), ALU.subtract).then_inc(wr_ready, 1)
            turn(t_moe)
            for b in range(TB):
                ve.wait_ge(xn_hi_made, b + 1)
                ve.tensor_tensor(xn_lo[:, b, :], x[:, b, :], xn_hi[:, b, :].bitcast(F32), ALU.subtract).then_inc(xn_lo_made, 1)
            r = [0]

            def route(ins):
                ins.then_inc(route_step, 1)
                r[0] += 1
                ve.wait_ge(route_step, r[0])

            ve.wait_ge(logits_done, 1)
            for b in range(TB):
                route(ve.tensor_tensor(lg[:, b, :], ps[:, 4 + b, 0:N_E], lg_row[:], ALU.add))
            for b in range(TB):
                mine = lg[:, b, :].unsqueeze(2).to_broadcast([P, N_E, N_E])
                other = lg[:, b, :].unsqueeze(1).to_broadcast([P, N_E, N_E])
                route(ve.tensor_tensor(above[:], other, mine, ALU.is_gt))
                route(ve.tensor_tensor(equal[:], other, mine, ALU.is_equal))
                route(ve.tensor_tensor(equal[:], equal[:], tri[:], ALU.mult))
                route(ve.tensor_tensor(above[:], above[:], equal[:], ALU.add))
                route(ve.tensor_reduce(rank[:, b, :], above[:], AX.X, ALU.add))
                route(ve.tensor_scalar(chosen[:, b, :], rank[:, b, :], float(TOP_K), None, ALU.is_lt))
                route(ve.tensor_reduce(stat[:, 12 + b:13 + b], lg[:, b, :], AX.X, ALU.max))
                route(ve.tensor_scalar(rank[:, b, :], lg[:, b, :], stat[:, 12 + b:13 + b], None, ALU.subtract))
            assert r[0] == ROUTE_EXP
            ve.wait_ge(route_exp, 1)
            for b in range(TB):
                route(ve.tensor_tensor(rank[:, b, :], rank[:, b, :], chosen[:, b, :], ALU.mult))
                route(ve.tensor_reduce(stat[:, 14 + b:15 + b], rank[:, b, :], AX.X, ALU.add))
                route(ve.reciprocal(stat[:, 14 + b:15 + b], stat[:, 14 + b:15 + b]))
                for k in range(ROUNDS):
                    route(ve.tensor_scalar(gate[:, b, N_E * k:N_E * (k + 1)], rank[:, b, :], stat[:, 14 + b:15 + b], None, ALU.mult))
                route(ve.memset(gate[:, b, EV - 2:EV], 0.0))
            ve.wait_ge(crowd_done, 1)
            for b in range(TB):
                route(ve.scalar_tensor_tensor(out=place[:, b, 0:N_E], in0=ps[:, 6, N_E * b:N_E * (b + 1)], scalar=1.0,
                                              in1=chosen[:, b, :], op0=ALU.add, op1=ALU.mult))
                route(ve.tensor_scalar(place[:, b, 0:N_E], place[:, b, 0:N_E], -1.0, None, ALU.add))
                for k in range(1, ROUNDS):
                    route(ve.tensor_scalar(place[:, b, N_E * k:N_E * (k + 1)], place[:, b, 0:N_E], float(-k * SLOTS),
                                           None, ALU.add))
                route(ve.memset(place[:, b, EV - 2:EV], -1.0))
            route(ve.tensor_reduce(crowd[:, N_E:N_E + 1], ps[:, 6, 2 * N_E:3 * N_E], AX.X, ALU.max))
            route(ve.tensor_scalar(crowd[:, N_E + 1:N_E + 2], crowd[:, N_E:N_E + 1], float(SLOTS), None, ALU.is_gt))
            for k in range(2, ROUNDS):
                route(ve.scalar_tensor_tensor(out=crowd[:, N_E + k:N_E + k + 1], in0=crowd[:, N_E:N_E + 1],
                                              scalar=float(k * SLOTS), in1=crowd[:, N_E + k - 1:N_E + k],
                                              op0=ALU.is_gt, op1=ALU.add))
            ve.tensor_copy(crowd_i[:, 0:1], crowd[:, N_E + ROUNDS - 1:N_E + ROUNDS]).then_inc(crowd_made, 1)
            ve.memset(slot_gate[:], 0.0).then_inc(gate_made, 1)
            for b in range(TB):
                ve.tensor_scalar(pickT[:, b * P:(b + 1) * P], ones, 0.0, None, ALU.mult).then_inc(m_zero, 1)

            def picks(e, par):
                for b in range(TB):
                    ins = ve.tensor_scalar(pick[:, par, b, :], iota_row, place[:, b, bass.ds(e, 1)], None, ALU.is_equal)
                ins.then_inc(picked, 1)

            def bias_rows(e, par):
                ve.tensor_scalar(sel[:, par, :], first_slots[0:96, :], onehot96[:, bass.ds(e, 1)], None,
                                 ALU.mult).then_inc(picked, 1)

            def gathered_rows(e, bank):
                ve.wait_ge(xs_hi_made, e + 1)
                ve.tensor_tensor(xs[:, :, SLOTS:P], ps[:, bank, :].rearrange("p (k s) -> p k s", k=KT),
                                 xs[:, :, 0:SLOTS].bitcast(F32), ALU.subtract).then_inc(xs_lo_made, 1)

            def limits(e, half, bank):
                n = 2 * e + half + 1
                ve.wait_ge(folded, n)
                ve.tensor_scalar(m_g[:], ps[:, bank, 0:256], LIMIT, None, ALU.min).then_inc(limited, 1)
                ve.tensor_scalar(m_u[:], ps[:, bank, 256:512], LIMIT, -LIMIT, ALU.min, ALU.max).then_inc(up_limited, 1)
                ve.wait_ge(limited, n)
                ve.wait_ge(up_limited, n)
                ve.scalar_tensor_tensor(out=m_gu[:], in0=m_u[:], scalar=1.0, in1=m_g[:], op0=ALU.add,
                                        op1=ALU.mult).then_inc(m_gu_made, 1)

            def activations(e, half):
                n = 2 * e + half + 1
                ve.wait_ge(m_gu_made, n)
                ve.wait_ge(m_sig_made, n)
                ve.tensor_tensor(m_act[:, half, :], m_gu[:], m_sig[:], ALU.mult).then_inc(m_act_made, 1)

            def low_activations(e, half):
                ve.wait_ge(m_hi_made, 2 * e + half + 1)
                ks = slice(4 * half, 4 * half + 4)
                ve.tensor_tensor(m[:, ks, SLOTS:P], m_act[:, half, :].rearrange("p (k s) -> p k s", k=4),
                                 m[:, ks, 0:SLOTS].bitcast(F32), ALU.subtract).then_inc(m_lo_made, 1)

            def expert(e, e_in_round, par, c, laps):
                g0 = 2 * par
                g1 = 2 - g0
                ve.wait_ge(y_hi_made, e + 1)
                ve.scalar_tensor_tensor(out=y_lo[:], in0=ps[:, g1:g1 + 2, :].rearrange("p a b -> p (a b)"),
                                        scalar=slot_gate[:, 1 - par:2 - par], in1=y_hi[:].bitcast(F32),
                                        op0=ALU.mult, op1=ALU.subtract).then_inc(y_lo_made, 1)
                for n in range(EXPERT_C):
                    cut(c + n + MOE_AHEAD, laps)
                    if n == 1:
                        picks(e + 1, 1 - par)
                        bias_rows(e_in_round + 1, 1 - par)
                    if n == 4:
                        limits(e, 0, g0)
                    if n == 5:
                        activations(e, 0)
                    if n == 6:
                        low_activations(e, 0)
                    if n == 8:
                        limits(e, 1, g1)
                        activations(e, 1)
                        low_activations(e, 1)
                    if n == 10:
                        gathered_rows(e + 1, g1 + 1)

            picks(0, 0)
            bias_rows(0, 0)
            gathered_rows(0, 1)
            cut(MOE_C0 + AHEAD)

            def round_of_experts(r):
                with ve.Fori(0, N_E // 2) as it:
                    for par in range(2):
                        expert(2 * it + N_E * r + par, 2 * it + par, par, MOE_C0 + par * EXPERT_C,
                               round_laps(r) + 4 * it)

            round_of_experts(0)
            ve.wait_ge(crowd_made, 1)
            more = ve.value_load(crowd_i[0:1, 0:1], min_val=0, max_val=ROUNDS - 1)
            with ve.If(more > 0):
                with ve.Fori(1, more + 1) as r:
                    round_of_experts(r)
            ve.wait_ge(last_hi, 1)
            ve.scalar_tensor_tensor(out=y_lo[:], in0=ps[:, 2:4, :].rearrange("p a b -> p (a b)"),
                                    scalar=slot_gate[:, 1:2], in1=y_hi[:].bitcast(F32),
                                    op0=ALU.mult, op1=ALU.subtract).then_inc(last_lo, 1)
            ve.wait_ge(last_scattered, 1)
            for b in range(TB):
                ve.scalar_tensor_tensor(out=x[:, b, :], in0=x[:, b, :], scalar=ALPHA,
                                        in1=ps[:, 4 + 2 * b:6 + 2 * b, :].rearrange("p a b -> p (a b)"),
                                        op0=ALU.mult, op1=ALU.add).then_inc(x_updated, 1)
            ve.wait_ge(x_updated, 8 + TB)
            layer_norm(1)

        @block.tensor
        def _(pe):
            def three(o, l_hi, l_lo, r_hi, r_lo, start, stop):
                pe.matmul(o, l_hi, r_hi, start=start, stop=False)
                pe.matmul(o, l_hi, r_lo, start=False, stop=False)
                return pe.matmul(o, l_lo, r_hi, start=False, stop=stop)

            def turn(src):
                for q in range(4):
                    for k in (2 * q, 2 * q + 1):
                        for b in range(TB):
                            o = (k % 2) * S + b * P
                            ins = pe.transpose(ps[:, q, o:o + P], src[:, b, k * P:(k + 1) * P], ident[:])
                    ins.then_inc(turned, 1)

            def ffn_in(c, bank, laps=0):
                pe.wait_ge(lo_made, c + 1 + LAP * laps)
                s = c % CUT
                for f in range(2):
                    for k in range(KT):
                        w = slice(k * 256 + f * P, k * 256 + (f + 1) * P)
                        ins = three(ps[:, bank, f * S:(f + 1) * S], w_hi[:, s, w], w_lo[:, s, w],
                                    xT_hi[:, k, :], xT_lo[:, k, :], k == 0, k == KT - 1)
                ins.then_inc(chunk_used, 1)

            def ffn_out(c, slot, g, first=False, last=False, laps=0):
                pe.wait_ge(act_lo, g + 1)
                pe.wait_ge(lo_made, c + 1 + LAP * laps)
                s = c % CUT
                for k in range(2):
                    for b in range(TB):
                        for h in range(2):
                            l = slice(k * S + b * P, k * S + (b + 1) * P)
                            w = slice(k * D + h * 512, k * D + (h + 1) * 512)
                            ins = three(ps[:, 4 + 2 * b + h, :], a_hi[:, slot, l], a_lo[:, slot, l],
                                        w_hi[:, s, w], w_lo[:, s, w], first and k == 0, last and k == 1)
                ins.then_inc(chunk_used, 1)

            def ffn_phase(f, c0, xparts):
                pe.wait_ge(turn_lo, xparts)
                g0 = FFN_PAIRS * f
                ffn_in(c0, 0)
                ffn_in(c0 + 1, 1)

                def step(slot, c, laps, first, g):
                    if not first:
                        pe.wait_ge(act_made, g - 1)
                    ffn_in(c, 2 * slot, laps)
                    ffn_in(c + 1, 2 * slot + 1, laps)
                    ffn_out(c + 2, 1 - slot, g - 1, first=first, laps=laps)

                step(1, c0 + 2, 0, True, g0 + 1)
                step(0, c0 + 5, 0, False, g0 + 2)
                with pe.Fori(1, (FFN_PAIRS - 1) // 2) as it:
                    for jj in range(2):
                        step(1 - jj, c0 + 2 + 3 * jj, it, False, 2 * it + (g0 + 1 + jj))
                ffn_out(c0 + FFN_C - 1, 0, g0 + FFN_PAIRS - 1, last=True)

            def project(g0, c0, n_groups):
                for n in range(n_groups):
                    g = g0 + n
                    if g >= 2:
                        pe.wait_ge(proj_read, g - 1)
                    for h in range(2):
                        c = c0 + 2 * n + h
                        pe.wait_ge(lo_made, c + 1)
                        s = c % CUT
                        for b in range(TB):
                            for k in range(4):
                                kk = 4 * h + k
                                w = slice(k * 512, (k + 1) * 512)
                                l = slice(b * P, (b + 1) * P)
                                ins = three(ps[:, 4 + 2 * (g % 2) + b, :], xT_hi[:, kk, l], xT_lo[:, kk, l],
                                            w_hi[:, s, w], w_lo[:, s, w], kk == 0, kk == KT - 1)
                        ins.then_inc(chunk_used, 1)

            def turn_qk(w, kind):
                v = pr_view(kind)
                for r in range(2):
                    for t in range(8):
                        tile = 8 * r + t
                        if r == 1 and t % 2 == 0:
                            for tt in (t, t + 1):
                                if is_key(kind, tt):
                                    pe.wait_ge(k_copied, 8 * w + 1 + sum(is_key(kind, m) for m in range(tt)))
                                else:
                                    pe.wait_ge(q_copied, 8 * w + 1 + sum(not is_key(kind, m) for m in range(tt)))
                        for b in range(TB):
                            if kind != "moba" and tile >= 14:
                                src = kvm[:, b, (tile - 14) * P:(tile - 13) * P]
                            elif kind != "moba" and tile >= 12:
                                c = 3 * SELF_W + (tile - 12) * P
                                src = v[:, b, c:c + P]
                            else:
                                src = v[:, b, tile * P:(tile + 1) * P]
                            o = (t % 2) * S + b * P
                            ins = pe.transpose(ps[:, t // 2, o:o + P], src, ident[:])
                        if t % 2:
                            ins.then_inc(qk_turned, 1)

            def attend(u0, groups, kind, w):
                def scores(n):
                    g, u, p = groups[n], u0 + n, (u0 + n) % 2
                    if n >= 2:
                        pe.wait_ge(prob_made, u - 1)
                    if g["bias"] and kind != "moba":
                        pe.wait_ge(strip_ready, (2, 5)[w])
                    for h, (qt, kt, half) in enumerate(g["qk"]):
                        rows = slice(0, P) if half is None else slice(half * HD, (half + 1) * HD)
                        q0 = g["b"] * P
                        o = ps[:, 2 * p + h % 2, (h // 2) * S:(h // 2 + 1) * S]
                        ins = pe.matmul(o, qkT[rows, qt, q0:q0 + P], qkT[rows, kt, :], start=True, stop=not g["bias"])
                        if g["bias"]:
                            h0, k = g["bias"]
                            m0 = P if g["b"] == 0 else 0
                            ins = pe.matmul(o, flip[:], strip[:, h0 + min(h, k - 1), m0:m0 + S], start=False, stop=True)
                    ins.then_inc(scored, 1)

                def values(n):
                    g, u, p = groups[n], u0 + n, (u0 + n) % 2
                    if g["diff"]:
                        pe.wait_ge(mixed, 6 * n_diff(groups, n))
                    else:
                        pe.wait_ge(prob_made, u + 1)
                    if n:
                        pe.wait_ge(probT_made, u)
                    for h in range(g["n"]):
                        row = 2 * h if g["diff"] else h
                        for k in range(TB):
                            col = (h * TB + k) * P
                            ins = pe.transpose(ps[:, 4 + col // 512, col % 512:col % 512 + P],
                                               prob[:, p, row, k * P:(k + 1) * P], ident[:])
                    ins.then_inc(probT_turned, 1)

                def outputs(n):
                    g, u, p = groups[n], u0 + n, (u0 + n) % 2
                    pe.wait_ge(probT_made, u + 1)
                    if n >= 2:
                        pe.wait_ge(o_made, u - 1)
                    where, v0 = g["v"]
                    v = kvm if where == "kvm" else pr_view(kind)
                    dv = g["dv"]
                    for h in range(g["n"]):
                        for k in range(TB):
                            ins = pe.matmul(ps[:, 6 + p, h * dv:(h + 1) * dv], probT[:, h, k, :],
                                            v[:, k, v0 + h * dv:v0 + (h + 1) * dv], start=k == 0, stop=k == TB - 1)
                    ins.then_inc(pv_done, 1)

                pe.wait_ge(flip_loaded, 16)
                if kind == "moba":
                    pe.wait_ge(strip_loaded, 16 * 20)
                pe.wait_ge(q_copied, 8 * (w + 1))
                pe.wait_ge(k_copied, 8 * (w + 1))
                scores(0)
                scores(1)
                for n in range(len(groups)):
                    values(n)
                    if n + 2 < len(groups):
                        scores(n + 2)
                    outputs(n)

            pe.wait_ge(ident_loaded, 16)
            pe.wait_ge(rows_loaded, 16 * 8)
            pe.transpose(ps[:, 0, 0:70], grow[0:70, :], ident[0:70, 0:70]).then_inc(gcol_turned, 1)
            pe.wait_ge(qscale_made, 1)
            for i in range(2):
                kind = ("rel", "diff")[i]
                pe.wait_ge(normed, TB * (n_of(i, T_FFN1) + 1))
                turn(nat)
                ffn_phase(2 * i, c_ffn1(i), 4 * (t_of(i, T_FFN1) + 1))
                pe.wait_ge(normed, TB * (n_of(i, T_MEM) + 1))
                turn(nat)
                pe.wait_ge(turn_lo, 4 * (t_of(i, T_MEM) + 1))
                pe.wait_ge(x_updated, 4 * i + 2)
                project(g_kv(i), c_kv(i), 1)
                pe.wait_ge(normed, TB * (n_of(i, T_MIX) + 1))
                turn(nat)
                pe.wait_ge(turn_lo, 4 * (t_of(i, T_MIX) + 1))
                if i == 0:
                    pe.wait_ge(rel_loaded, 32)
                    for k in range(2):
                        ins = pe.transpose(ps[:, 7, 12 * k:12 * k + 12], rel_rows[0:12, 1 + k * P:1 + (k + 1) * P], ident[0:12, 0:12])
                    ins.then_inc(ext_turned, 1)
                    pe.wait_ge(ext_made, 1)
                    for k in range(2):
                        ins = pe.matmul(ps[0:12, 7, :], ang[:, 0, 12 * k:12 * k + 12],
                                        qk_flat[:, 512 * k:512 * (k + 1)],
                                        start=k == 0, stop=k == 1)
                    ins.then_inc(ext_rows, 1)
                    pe.wait_ge(ext_copied, 1)
                project(g_in(i), c_in(i), 5)
                pe.wait_ge(proj_read, g_in(i) + 5)
                if i == 0:
                    pe.wait_ge(head_normed, 6)
                else:
                    pe.wait_ge(rope_step, 16)
                turn_qk(i, kind)
                attend(u_layer(i), attention_groups(kind), kind, i)
                pe.wait_ge(o_made, u_layer(i) + 8)
                if i == 1:
                    pe.wait_ge(sub_step, 7)
                turn(nat)
                pe.wait_ge(turn_lo, 4 * (t_of(i, T_O) + 1))
                project(g_out(i), c_out(i), 2)
                pe.wait_ge(normed, TB * (n_of(i, T_FFN2) + 1))
                turn(nat)
                pe.wait_ge(proj_read, g_out(i) + 2)
                ffn_phase(2 * i + 1, c_ffn2(i), 4 * (t_of(i, T_FFN2) + 1))
            pe.wait_ge(x_updated, 8)
            turn(x)
            pe.wait_ge(turn_lo, 4 * (t_moba + 1))
            pe.wait_ge(rel_loaded, 64)
            pe.matmul(ps[0:8, 7, :], rel_rows[0:32, 0:8], qk_flat[0:32, 0:512],
                      start=True, stop=True).then_inc(ext_rows, 1)
            pe.wait_ge(ext_copied, 2)
            project(g_moba, c_moba, 6)
            pe.wait_ge(proj_read, g_moba + 6)
            turn_qk(2, "moba")
            attend(u_moba, attention_groups("moba"), "moba", 2)
            pe.wait_ge(o_made, u_moba + 4)
            turn(nat)
            pe.wait_ge(turn_lo, 4 * (t_moba_o + 1))
            project(g_moba_out, c_moba_out, 2)
            pe.wait_ge(ln_step, LN_STEPS)
            turn(x)
            pe.wait_ge(turn_lo, 4 * (t_moe + 1))
            pe.wait_ge(wr_ready, 1)
            for b in range(TB):
                for k in range(KT):
                    l = slice(b * P, (b + 1) * P)
                    ins = three(ps[:, 4 + b, 0:N_E], xT_hi[:, k, l], xT_lo[:, k, l], wr_hi[:, k, :], wr_lo[:, k, :],
                                k == 0, k == KT - 1)
            ins.then_inc(logits_done, 1)
            pe.wait_ge(route_step, ROUTE_EXP)
            pe.matmul(ps[:, 6, 0:N_E], before, chosen[:, 0, :], start=True, stop=True)
            pe.matmul(ps[:, 6, N_E:2 * N_E], ones, chosen[:, 0, :], start=True, stop=False)
            pe.matmul(ps[:, 6, N_E:2 * N_E], before, chosen[:, 1, :], start=False, stop=True)
            pe.matmul(ps[:, 6, 2 * N_E:3 * N_E], ones, chosen[:, 0, :], start=True, stop=False)
            pe.matmul(ps[:, 6, 2 * N_E:3 * N_E], ones, chosen[:, 1, :], start=False, stop=True).then_inc(crowd_done, 1)

            def gather(bank, par):
                for k in range(KT):
                    o = ps[:, bank, k * SLOTS:(k + 1) * SLOTS]
                    for b in range(TB):
                        slots = pick[:, par, b, 0:SLOTS]
                        pe.matmul(o, xn_hi[:, b, k * P:(k + 1) * P], slots, start=b == 0, stop=False)
                        ins = pe.matmul(o, xn_lo[:, b, k * P:(k + 1) * P], slots, start=False, stop=b == 1)
                ins.then_inc(gathered, 1)

            def scatter():
                for b in range(TB):
                    for h in range(2):
                        o = ps[:, 4 + 2 * b + h, :]
                        l, r = pickT[:, b * P:(b + 1) * P], slice(h * 512, (h + 1) * 512)
                        pe.matmul(o, l, y_hi[:, r], start=False, stop=False, skip_group_check=True)
                        ins = pe.matmul(o, l, y_lo[:, r], start=False, stop=False, skip_group_check=True)
                return ins

            def bias(bank, col, par):
                pe.matmul(ps[:, bank, :], sel[:, par, :], bias_parts[:, col:col + 512], start=True, stop=False)

            def rows(src, c, bank, h, laps, stop):
                pe.wait_ge(lo_made, c + 1 + LAP * laps)
                hi, lo = cut_slot(c)
                for k in range(4):
                    w = slice(k * 512, (k + 1) * 512)
                    pe.matmul(ps[:, bank, :], src[:, 4 * h + k, :], hi[:, w], start=False, stop=False)
                    ins = pe.matmul(ps[:, bank, :], src[:, 4 * h + k, :], lo[:, w], start=False,
                                    stop=stop and k == 3)
                ins.then_inc(chunk_used, 1)

            def fold_half(e, half, bank):
                pe.wait_ge(h_read, 4 * e + 2 * half + 2)
                for up in range(2):
                    for k in range(4):
                        o = 256 * up + SLOTS * k
                        ins = pe.matmul(ps[:, bank, o:o + SLOTS], h_rows[:, half, up, k * P:(k + 1) * P], fold,
                                        start=True, stop=True)
                ins.then_inc(folded, 1)

            def expert(e, par, c, laps):
                g0 = 2 * par
                g1 = 2 - g0
                pe.wait_ge(xs_lo_made, e + 1)
                bias(g0, 0, par)
                rows(xs, c, g0, 0, laps, False)
                rows(xs, c + 1, g0, 1, laps, True)
                pe.wait_ge(y_lo_made, e + 1)
                scatter().then_inc(scattered, 1)
                bias(g0 + 1, D, par)
                rows(xs, c + 2, g0 + 1, 0, laps, False)
                rows(xs, c + 3, g0 + 1, 1, laps, True)
                bias(g1, 512, par)
                rows(xs, c + 4, g1, 0, laps, False)
                fold_half(e, 0, g0)
                for b in range(TB):
                    pe.transpose(ps[:, g0 + 1, b * P:(b + 1) * P], pick[:, par, b, :].bitcast(F32), ident[:])
                for b in range(TB):
                    ins = pe.matmul(ps[:, g0 + 1, S:S + 1], pick[:, par, b, :].bitcast(F32), gate[:, b, bass.ds(e, 1)],
                                    start=b == 0, stop=b == 1)
                ins.then_inc(pickT_turned, 1)
                rows(xs, c + 5, g1, 1, laps, True)
                bias(g1 + 1, D + 512, par)
                rows(xs, c + 6, g1 + 1, 0, laps, False)
                rows(xs, c + 7, g1 + 1, 1, laps, True)
                pe.wait_ge(m_lo_made, 2 * e + 1)
                bias(g0, 2 * D, par)
                rows(m, c + 8, g0, 0, laps, False)
                fold_half(e, 1, g1)
                pe.wait_ge(pickT_made, e + 1)
                pe.wait_ge(gate_made, e + 2)
                bias(g0 + 1, 2 * D + 512, par)
                rows(m, c + 9, g0 + 1, 0, laps, False)
                pe.wait_ge(picked, 2 * e + 4)
                gather(g1 + 1, 1 - par)
                pe.wait_ge(m_lo_made, 2 * e + 2)
                rows(m, c + 10, g0, 1, laps, True)
                rows(m, c + 11, g0 + 1, 1, laps, True)

            pe.wait_ge(m_zero, 2)
            pe.wait_ge(xn_lo_made, 2)
            for bank in (4, 5, 6, 7, 2, 3):
                ins = pe.matmul(ps[:, bank, :], pickT[:, 0:P], xn_hi[:, 0, 0:512], start=True, stop=True)
            ins.then_inc(scattered, 1)
            pe.wait_ge(picked, 2)
            gather(1, 0)

            def round_of_experts(r):
                with pe.Fori(0, N_E // 2) as it:
                    for par in range(2):
                        expert(2 * it + N_E * r + par, par, MOE_C0 + par * EXPERT_C, round_laps(r) + 4 * it)

            round_of_experts(0)
            pe.wait_ge(crowd_made, 1)
            more = pe.value_load(crowd_i[0:1, 0:1], min_val=0, max_val=ROUNDS - 1)
            with pe.If(more > 0):
                with pe.Fori(1, more + 1) as r:
                    round_of_experts(r)
            pe.wait_ge(last_lo, 1)
            scatter().then_inc(last_scattered, 1)


NAMES = ["x", "mem", "positions", "ffn1_norm", "ffn1_w_gate", "ffn1_w_up", "ffn1_w_down", "mix_norm", "mem_norm",
         "w_in", "w_mem_kv", "mem_q_norm", "mem_k_norm", "w_out", "a_q_norm", "a_k_norm", "a_rel_bias",
         "b_q_norm", "b_k_norm", "b_lambda_q1", "b_lambda_k1", "b_lambda_q2", "b_lambda_k2", "b_subln",
         "ffn2_norm", "ffn2_w_gate", "ffn2_w_up", "ffn2_w_down", "rel_bias_2", "a_w_in_2", "a_w_out_2",
         "ln_g_2", "ln_b_2", "moe_w_router_2", "moe_b_router_2", "moe_w_gate_up_2", "moe_b_gate_up_2",
         "moe_w_down_2", "moe_b_down_2"]


def constants():
    f = np.float32
    m = np.arange(512)
    rel = np.clip(255 - m, -128, 128) + 128
    c_rel = np.zeros((P, 2, 512), f)
    for k in range(2):
        c_rel[:, k, :] = rel[None, :] == 1 + k * P + np.arange(P)[:, None]
    n = np.maximum(255 - m, 0)
    large = 16 + (np.log(np.maximum(n, 1).astype(f) / f(16)) / f(math.log(8)) * f(16)).astype(np.int32)
    bucket = np.where(n < 16, n, np.minimum(large, 31))
    c_t5 = (bucket[None, :] == np.arange(32)[:, None]).astype(f)
    masks = np.zeros((P, MASK_W), f)
    i = np.arange(P)
    masks[:, 0:P] = i[None, :] % SLOTS
    masks[:, P:2 * P] = i[:, None] < i[None, :]
    masks[:, 2 * P:3 * P] = 1
    masks[:, 3 * P:4 * P] = i[None, :] < SLOTS
    masks[:, 4 * P:4 * P + SLOTS] = i[:, None] % SLOTS == np.arange(SLOTS)[None, :]
    for e in range(34):
        for r in range(3):
            masks[32 * r + e % N_E, MASK_W - 34 + e] = 1
    e = np.arange(N_E)
    return {"c_ident": np.eye(P, dtype=f), "c_flip": np.eye(P, dtype=f)[::-1].copy(), "c_rel": c_rel.reshape(P, 1024), "c_t5": c_t5, "c_masks": masks,
            "c_tri": (e[None, :] < e[:, None]).astype(f).reshape(-1),
            "c_inv_freq": (f(1.0) / (f(10000.0) ** (np.arange(0, HD, 2, dtype=f) / f(HD)))).astype(f)}


def kernel(**inputs):
    import concourse.bacc as bacc
    from concourse.bass_utils import run_bass_kernel_spmd

    nc = bacc.Bacc("TRN2", target_bir_lowering=False, num_devices=1)
    arrays, aps = {}, {}
    for name, v in [(n, inputs[n]) for n in NAMES] + list(constants().items()):
        v = np.ascontiguousarray(v)
        arrays["in_" + name] = v
        aps[name] = nc.dram_tensor("in_" + name, v.shape, mybir.dt.from_np(v.dtype), kind="ExternalInput").ap()
    out = nc.dram_tensor("out", (1, S, D), F32, kind="ExternalOutput").ap()
    build(nc, aps, out)
    r = run_bass_kernel_spmd(nc, [arrays], core_ids=[0])
    return r.results[0]["out"]
```

```python
from contextlib import ExitStack
import math

import numpy as np

import concourse.bass as bass
from concourse import mybir

F32 = mybir.dt.float32
F32R = mybir.dt.float32r
BF16 = mybir.dt.bfloat16
I32 = mybir.dt.int32
ALU = mybir.AluOpType
ACT = mybir.ActivationFunctionType
AX = mybir.AxisListType

P = 128
D = 1024
KT = D // P
TB = 2
S = TB * P
HD = 64
D_FF = 2816
SELF_W = 768
IN_W = 2560
IN_ORDER = (4, 0, 1, 2, 3)
N_E = 32
TOP_K = 4
NEG = -1e30
EPS = 1e-6
LN_EPS = 1e-5
ALPHA = 2.0 ** 0.25
LAMBDA_INIT = 0.8 - 0.6 * math.exp(-0.3)
LIMIT = 7.0
SWIGLU_ALPHA = 1.702

TRIG_STEPS = 20
BIG = 3e38
MOE_LOADS = 16 * 7
MASK_W = 4 * 128 + 64 + 32 + 34
PI_BELOW = 3.1415925

CH = 2048
RAW = 6
CUT = 3
AHEAD = 2
MOE_CUT, MOE_AHEAD = 4, 3
LAP = 6

FFN_PAIRS = D_FF // 256
FFN_C = 3 * FFN_PAIRS
KV_C, IN_C, OUT_C = 2, 10, 4
LAYER_C = 2 * FFN_C + KV_C + IN_C + OUT_C
MOBA_IN_C = 12
MOE_C0 = 2 * LAYER_C + MOBA_IN_C + OUT_C
EXPERT_C = 12
SLOTS = 64
ROUNDS = S // SLOTS
EV = ROUNDS * N_E + 2
REL_W = 256


def is_key(kind, tile):
    return tile >= 8 if kind == "moba" else 6 <= tile < 12 or tile >= 14


def n_diff(groups, n):
    return sum(g["diff"] for g in groups[:n + 1])


def build(nc, a, out):
    with ExitStack() as ctx:
        sem = lambda name: ctx.enter_context(nc.semaphore(name))

        def sb(name, shape, dt=F32, stack=ctx):
            return stack.enter_context(nc.sbuf_tensor("sb_" + name, shape, dt))

        raw = sb("raw", [P, RAW, CH])
        w_hi = sb("w_hi", [P, CUT, CH], F32R)
        w_lo = sb("w_lo", [P, CUT, CH], F32R)
        x = sb("x", [P, TB, D])
        more_hi = ExitStack()
        w_hi3 = sb("w_hi3", [P, CH], F32R, more_hi)
        more_hi.close()
        nat = sb("nat", [P, TB, D])
        ident = sb("ident", [P, P])
        flip = sb("flip", [P, P])
        gcol = sb("gcol", [P, 72])
        grow = sb("grow", [P, P])
        qscale = sb("qscale", [P, 4])
        stat = sb("stat", [P, 16])
        bias_parts = sb("bias_parts", [96, 3 * D], BF16)
        bc = sb("bc", [P, 512])
        inv_row = sb("inv_row", [P, 32])
        pos_i = sb("pos_i", [P, TB], I32)
        pos_f = sb("pos_f", [P, TB])
        trig = sb("trig", [P, TB, 2, 32])
        ang = sb("ang", [P, 5, TB * 32])
        turns_i = sb("turns_i", [P, TB * 32], I32)
        lam = sb("lam", [P, 8])
        chunk_mask = sb("chunk_mask", [P, REL_W], BF16)
        flip_bf = sb("flip_bf", [P, P], BF16)
        turn_by = sb("turn_by", [P, 2, TB, 2, HD])
        row_stats = sb("row_stats", [P, TB, 2, 6])
        mean_var = sb("mean_var", [P, TB, 2])

        early = ExitStack()
        strip = sb("strip", [P, 12, REL_W], stack=early)
        early.close()
        late = ExitStack()
        m = sb("m", [P, KT, P], F32R, late)
        xs = sb("xs", [P, KT, P], F32R, late)
        y_hi = sb("y_hi", [P, D], F32R, late)
        y_lo = sb("y_lo", [P, D], F32R, late)
        late.close()
        turned_rows = ExitStack()
        xT_hi = sb("xT_hi", [P, KT, S], F32R, turned_rows)
        xT_lo = sb("xT_lo", [P, KT, S], F32R, turned_rows)
        ffn = ExitStack()
        a_hi = sb("a_hi", [P, 2, 512], F32R, ffn)
        a_lo = sb("a_lo", [P, 2, 512], F32R, ffn)
        sig = sb("sig", [P, 2, 512], stack=ffn)
        gated = sb("gated", [P, 2, 512], stack=ffn)
        act = sb("act", [P, 2, 512], stack=ffn)
        ffn.close()
        att = ExitStack()
        pr = sb("pr", [P, TB * 3 * D], stack=att)
        qkT = sb("qkT", [P, 16, S], stack=att)
        kvm = sb("kvm", [P, TB, 512], stack=att)
        prob = sb("prob", [P, 2, 4, S], stack=att)
        probT = sb("probT", [P, 4, TB, P], stack=att)
        sums = sb("sums", [P, TB, 32], stack=att)
        soft = sb("soft", [P, 2, 24], stack=att)
        att.close()
        moe, routing = ExitStack(), ExitStack()
        xn_hi = sb("xn_hi", [P, TB, D], F32R, moe)
        xn_lo = sb("xn_lo", [P, TB, D], F32R, moe)
        pick = sb("pick", [P, 2, TB, P], F32R, moe)
        pickT = sb("pickT", [P, S], F32R, moe)
        slot_gate = sb("slot_gate", [P, 2], stack=moe)
        sel = sb("sel", [96, 2, P], BF16, moe)
        gate = sb("gate", [P, TB, EV], stack=moe)
        place = sb("place", [P, TB, EV], stack=moe)
        more_lo = ExitStack()
        w_lo3 = sb("w_lo3", [P, CH], F32R, more_lo)
        more_lo.close()
        ln = sb("ln", [P, 2, 2, D], stack=moe)
        crowd_i = sb("crowd_i", [P, 2], I32, moe)
        masks = sb("masks", [P, MASK_W], stack=moe)
        iota_row, before, ones = masks[:, 0:P], masks[:, P:2 * P], masks[:, 2 * P:3 * P]
        first_slots, fold = masks[:, 3 * P:4 * P], masks[:, 4 * P:4 * P + SLOTS]
        fold_logits = masks[0:2 * N_E, 4 * P + SLOTS:4 * P + SLOTS + N_E]
        onehot96 = masks[0:96, MASK_W - 34:MASK_W]
        wr2 = sb("wr2", [P, KT, 2, N_E], F32R, routing)
        wr = sb("wr", [P, KT, N_E], stack=routing)
        lgT = sb("lgT", [2 * N_E, S], stack=routing)
        lg = sb("lg", [P, TB, N_E], stack=routing)
        lg_row = sb("lg_row", [P, N_E], stack=routing)
        top8 = sb("top8", [P, TB, 8], stack=routing)
        needles = sb("needles", [P, TB, 8], stack=routing)
        rest = sb("rest", [P, TB, N_E], stack=routing)
        share = sb("share", [P, TB, N_E], stack=routing)
        counted = sb("counted", [P, TB, N_E], stack=routing)
        share_sum = sb("share_sum", [P, TB], stack=routing)
        chosen = sb("chosen", [P, TB, N_E], stack=routing)
        crowd = sb("crowd", [P, N_E + 4], stack=routing)
        routing.close()
        h_rows = sb("h_rows", [P, 2, 2, 512], stack=moe)
        m_g = sb("m_g", [P, 256], stack=moe)
        m_sig = sb("m_sig", [P, 256], stack=moe)
        m_u = sb("m_u", [P, 256], stack=moe)
        m_gu = sb("m_gu", [P, 256], stack=moe)
        m_act = sb("m_act", [P, 2, 256], stack=moe)
        moe.close()
        turned_rows.close()

        def cut_slot(c):
            s = c % (CUT if c < MOE_C0 else MOE_CUT)
            return (w_hi[:, s, :], w_lo[:, s, :]) if s < CUT else (w_hi3[:], w_lo3[:])

        ps = ctx.enter_context(nc.psum_tensor("ps", [P, 8, 512], F32))

        qk_flat = qkT[:].rearrange("p a b -> p (a b)")
        rel_rows = probT[:].rearrange("p a b c -> p (a b c)")
        mem = prob[:].rearrange("p a b c -> p (a b c)").rearrange("p (b d) -> p b d", b=TB)
        ext = nc.dram_tensor("ext", (3, 12, 512), F32)

        raw_loaded = [sem(f"raw_loaded{i}") for i in range(RAW)]
        hi_made, lo_made, chunk_used = sem("hi_made"), sem("lo_made"), sem("chunk_used")
        x_loaded, ident_loaded, rows_loaded = sem("x_loaded"), sem("ident_loaded"), sem("rows_loaded")
        small_loaded = sem("small_loaded")
        up_limited = sem("up_limited")
        flip_loaded = sem("flip_loaded")
        bias_loaded, bias_step, bias_made = sem("bias_loaded"), sem("bias_step"), sem("bias_made")
        gcol_turned, qscale_made = sem("gcol_turned"), sem("qscale_made")
        squared, ms_made, std_made, rstd_made, normed = (sem("squared"), sem("ms_made"), sem("std_made"),
                                                         sem("rstd_made"), sem("normed"))
        turned, turn_hi, turn_lo = sem("turned"), sem("turn_hi"), sem("turn_lo")
        sig_made, gated_made, act_made = sem("sig_made"), sem("gated_made"), sem("act_made")
        act_hi, act_lo = sem("act_hi"), sem("act_lo")
        x_updated = sem("x_updated")
        mem_loaded, proj_read = sem("mem_loaded"), sem("proj_read")
        rel_loaded, ext_turned, ext_rows, ext_made, ext_copied, ext_stored, strip_loaded, strip_ready = (
            sem("rel_loaded"), sem("ext_turned"), sem("ext_rows"), sem("ext_made"), sem("ext_copied"),
            sem("ext_stored"), sem("strip_loaded"), sem("strip_ready"))
        mask_made = sem("mask_made")
        head_step, head_ms, head_std, heads_ready = (sem("head_step"), sem("head_ms"), sem("head_std"),
                                                     sem("heads_ready"))
        qk_turned, q_copied, k_copied = sem("qk_turned"), sem("q_copied"), sem("k_copied")
        scored, max_made, prob_made, total_read, mixed, probT_turned, probT_made, pv_done, o_made = (
            sem("scored"), sem("max_made"), sem("prob_made"), sem("total_read"),
            sem("mixed"), sem("probT_turned"), sem("probT_made"), sem("pv_done"), sem("o_made"))
        sub_step, sub_ms, sub_std, sub_normed = sem("sub_step"), sem("sub_ms"), sem("sub_std"), sem("sub_normed")
        lam_step, lam_exp, trig_step, trig_sin, trig_gains = (sem("lam_step"), sem("lam_exp"), sem("trig_step"),
                                                              sem("trig_sin"), sem("trig_gains"))
        ln_step, ln_var, ln_std, ln_rows = sem("ln_step"), sem("ln_var"), sem("ln_std"), sem("ln_rows")
        moe_loaded, wr_cut, wr_ready, logits_done, logits_copied, logits_folded = (
            sem("moe_loaded"), sem("wr_cut"), sem("wr_ready"), sem("logits_done"), sem("logits_copied"),
            sem("logits_folded"))
        route_step, chosen_made, shifted, route_exp, crowd_done, crowd_made = (
            sem("route_step"), sem("chosen_made"), sem("shifted"), sem("route_exp"), sem("crowd_done"),
            sem("crowd_made"))
        xn_hi_made, xn_lo_made = sem("xn_hi_made"), sem("xn_lo_made")
        m_zero = sem("m_zero")
        picked, gathered, xs_hi_made, xs_lo_made = (sem("picked"), sem("gathered"), sem("xs_hi_made"),
                                                    sem("xs_lo_made"))
        limited, m_sig_made, m_gu_made, m_act_made = (sem("limited"), sem("m_sig_made"), sem("m_gu_made"),
                                                      sem("m_act_made"))
        h_read = sem("h_read")
        folded, m_hi_made, m_lo_made, pickT_turned, pickT_made, gate_made = (
            sem("folded"), sem("m_hi_made"), sem("m_lo_made"), sem("pickT_turned"), sem("pickT_made"),
            sem("gate_made"))
        y_hi_made, y_lo_made, scattered, last_scattered = (
            sem("y_hi_made"), sem("y_lo_made"), sem("scattered"), sem("last_scattered"))
        out_stored = sem("out_stored")

        block = ctx.enter_context(nc.Block())

        c_ffn1 = lambda i: i * LAYER_C
        c_kv = lambda i: i * LAYER_C + FFN_C
        c_in = lambda i: c_kv(i) + KV_C
        c_out = lambda i: c_in(i) + IN_C
        c_ffn2 = lambda i: c_out(i) + OUT_C
        c_moba = 2 * LAYER_C
        c_moba_out = c_moba + MOBA_IN_C
        round_laps = lambda r: (N_E * EXPERT_C // LAP) * r
        g_kv, g_in, g_out = (lambda i: 8 * i), (lambda i: 8 * i + 1), (lambda i: 8 * i + 6)
        g_moba, g_moba_out = 16, 22
        u_layer, u_moba = (lambda i: 8 * i), 16
        T_FFN1, T_MEM, T_MIX, T_O, T_FFN2 = range(5)
        t_of = lambda i, which: 5 * i + which
        t_moba, t_moba_o, t_moe = 10, 11, 12
        n_of = lambda i, which: 4 * i + (which if which < 3 else 3)
        gain0 = {T_FFN1: 0, T_MEM: 16, T_MIX: 32, T_FFN2: 48}

        def attention_groups(kind):
            groups = []
            if kind != "moba":
                groups = [dict(b=b, nk=TB, qk=[(12 + h // 2, 14 + h // 2, h % 2) for h in range(4)], bias=None,
                               dv=HD, v=("kvm", 256), o=SELF_W, n=4, diff=False) for b in range(TB)]
            for b in range(TB):
                if kind == "moba":
                    for h0 in (0, 4):
                        groups.append(dict(b=b, nk=b + 1, qk=[(h, 8 + h, None) for h in range(h0, h0 + 4)],
                                           bias=(h0, 4), dv=P, v=("pr", 2 * D + h0 * P), o=h0 * P, n=4, diff=False))
                    continue
                for h0 in (0, 4, 8):
                    qk = [(h // 2, 6 + h // 2, h % 2) for h in range(h0, h0 + 4)]
                    if kind == "rel":
                        groups.append(dict(b=b, nk=b + 1, qk=qk, bias=(h0, 4), dv=HD, v=("pr", 2 * SELF_W + h0 * HD),
                                           o=h0 * HD, n=4, diff=False))
                    else:
                        groups.append(dict(b=b, nk=b + 1, qk=qk, bias=(0, 1), dv=2 * HD, v=("pr", 2 * SELF_W + h0 * HD),
                                           o=h0 * HD, n=2, diff=True))
            return groups

        def head_sums(n):
            return 24 if n == 1 else 8 * IN_ORDER[n - 1]

        def pr_width(kind):
            return 3 * D if kind == "moba" else IN_W

        def pr_view(kind):
            w = pr_width(kind)
            return pr[:, 0:TB * w].rearrange("p (b w) -> p b w", b=TB)

        def row_by_distance(heads):
            return rel_rows[0:heads, 512:1024]

        @block.sync
        def _(sp):
            def load_chunk(c, src, laps=0, shape=None):
                if c >= RAW or not isinstance(laps, int):
                    sp.wait_ge(lo_made, LAP * laps + (c - RAW + 1))
                dst = raw[:, c % RAW, :].rearrange("p (a n) -> p a n", a=shape)
                sp.dma_start(dst, src).then_inc(raw_loaded[c % RAW], 16)

            def ffn_chunks(c0, wg, wu, wd):
                gsrc = lambda w, j: w.rearrange("(k p) f -> p k f", p=P)[:, :, bass.ds(j * 256, 256)]
                dsrc = lambda j: wd.rearrange("(j k p) n -> j p k n", p=P, k=2)[j]
                dsl = lambda j: wd[bass.ds(j * 256, 256), :].rearrange("(k p) n -> p k n", p=P)
                load_chunk(c0, gsrc(wg, 0), shape=KT)
                load_chunk(c0 + 1, gsrc(wu, 0), shape=KT)
                if c0 == 0:
                    small_loads()

                def two_steps(it):
                    for jj in range(2):
                        j = 1 + jj + 2 * it
                        c = c0 + 2 + 3 * jj
                        load_chunk(c, gsrc(wg, j), it, shape=KT)
                        load_chunk(c + 1, gsrc(wu, j), it, shape=KT)
                        load_chunk(c + 2, dsl(j - 1), it, shape=2)

                two_steps(0)
                with sp.Fori(1, (FFN_PAIRS - 1) // 2) as it:
                    two_steps(it)
                load_chunk(c0 + FFN_C - 1, dsl(FFN_PAIRS - 1), shape=2)

            def product_chunks(c0, w, order):
                for n, col in enumerate(order):
                    for h in range(2):
                        src = w[h * 512:(h + 1) * 512, col * 512:(col + 1) * 512].rearrange("(k p) n -> p k n", p=P)
                        load_chunk(c0 + 2 * n + h, src, shape=4)

            def load_strips(n, heads, used):
                sp.wait_ge(ext_copied, n + 1)
                sp.dma_start(ext[n, 0:heads, :], row_by_distance(heads)).then_inc(ext_stored, 16)
                sp.wait_ge(ext_stored, 16 * (n + 1))
                sp.wait_ge(chunk_used, used)
                for h in range(heads):
                    src = bass.AP(ext, (n * 12 + h) * 512, [[1, P], [1, REL_W]])
                    sp.dma_start(strip[:, h, :], src).then_inc(strip_loaded, 16)

            tok = lambda t: t.rearrange("(b p) d -> p b d", p=P)
            rows = lambda v, n: bass.AP(v.tensor, v.offset, [[0, P], [1, n]])
            sp.dma_start(x[:], tok(a["x"][0])).then_inc(x_loaded, 16)
            sp.dma_start(ident[:], a["c_ident"]).then_inc(ident_loaded, 16)
            for n, name in enumerate(("ffn1_norm", "mem_norm", "mix_norm", "ffn2_norm")):
                sp.dma_start(grow[16 * n:16 * n + 16, :], a[name].rearrange("i (k p) -> (i k) p", p=P)).then_inc(rows_loaded, 16)
            for r, name, n in ((64, "mem_q_norm", 2), (66, "mem_k_norm", 2), (68, "a_q_norm", 1), (69, "a_k_norm", 1)):
                sp.dma_start(grow[r:r + n, :].rearrange("i (h d) -> i h d", h=2),
                             bass.AP(a[name].tensor, a[name].offset, [[HD, n], [0, 2], [1, HD]])).then_inc(rows_loaded, 16)

            def small_loads():
                sp.dma_start(mem, tok(a["mem"][0])).then_inc(mem_loaded, 16)
                for r in range(3):
                    sp.dma_start(qk_flat[32 * r:32 * r + 32, 0:2 * D], a["moe_b_gate_up_2"][0]).then_inc(bias_loaded, 16)
                    sp.dma_start(qk_flat[32 * r:32 * r + 32, 2 * D:3 * D], a["moe_b_down_2"][0]).then_inc(bias_loaded, 16)
                sp.dma_start(flip[:], a["c_flip"]).then_inc(flip_loaded, 16)
                for n, name in enumerate(("b_lambda_q1", "b_lambda_k1", "b_lambda_q2", "b_lambda_k2", "b_q_norm",
                                          "b_k_norm")):
                    sp.dma_start(bc[:, HD * n:HD * (n + 1)], rows(a[name][0], HD)).then_inc(small_loaded, 16)
                sp.dma_start(bc[:, 384:512], rows(a["b_subln"][0], P)).then_inc(small_loaded, 16)
                sp.dma_start(inv_row[:], rows(a["c_inv_freq"], 32)).then_inc(small_loaded, 16)
                with nc.allow_non_contiguous_dma(reason="256 positions, one per partition"):
                    sp.dma_start(pos_i[:], a["positions"][0].rearrange("(b p) -> p b", p=P)).then_inc(small_loaded, 16)

            for i in range(2):
                ffn_chunks(c_ffn1(i), a["ffn1_w_gate"][i], a["ffn1_w_up"][i], a["ffn1_w_down"][i])
                if i == 0:
                    sp.wait_ge(bias_made, 1)
                    sp.dma_start(qk_flat[:, 0:4 * S], a["c_rel"]).then_inc(rel_loaded, 16)
                    sp.dma_start(rel_rows[0:12, 0:257], a["a_rel_bias"][0]).then_inc(rel_loaded, 16)
                product_chunks(c_kv(i), a["w_mem_kv"][i], (0,))
                product_chunks(c_in(i), a["w_in"][i], IN_ORDER)
                product_chunks(c_out(i), a["w_out"][i], range(2))
                if i == 0:
                    load_strips(0, 12, c_out(0))
                    sp.wait_ge(o_made, u_layer(1))
                    sp.dma_start(mem, tok(a["mem"][0])).then_inc(mem_loaded, 16)
                ffn_chunks(c_ffn2(i), a["ffn2_w_gate"][i], a["ffn2_w_up"][i], a["ffn2_w_down"][i])
            sp.wait_ge(o_made, u_moba)
            sp.dma_start(qk_flat[0:32, 0:2 * S], a["c_t5"]).then_inc(rel_loaded, 16)
            sp.dma_start(rel_rows[0:32, 0:8], a["rel_bias_2"]).then_inc(rel_loaded, 16)
            product_chunks(c_moba, a["a_w_in_2"][0], range(6))
            product_chunks(c_moba_out, a["a_w_out_2"][0], range(2))
            load_strips(1, 8, c_moba_out)
            sp.wait_ge(o_made, u_moba + 4)
            sp.dma_start(masks[:], a["c_masks"]).then_inc(moe_loaded, 16)
            for n in range(2):
                sp.dma_start(ln[:, n, 0, :], rows(a["ln_g_2"][0, n], D)).then_inc(moe_loaded, 16)
                sp.dma_start(ln[:, n, 1, :], rows(a["ln_b_2"][0, n], D)).then_inc(moe_loaded, 16)
            sp.dma_start(wr[:], a["moe_w_router_2"][0].rearrange("(k p) e -> p k e", p=P)).then_inc(moe_loaded, 16)
            sp.dma_start(lg_row[:], rows(a["moe_b_router_2"][0], N_E)).then_inc(moe_loaded, 16)

            def expert_chunk(e, n, c, laps):
                if n < 8:
                    col = (n // 4) * 512 + ((n // 2) % 2) * D
                    h = n % 2
                    w = a["moe_w_gate_up_2"][0]
                else:
                    col = ((n - 8) % 2) * 512
                    h = (n - 8) // 2
                    w = a["moe_w_down_2"][0]
                src = w[bass.ds(e, 1), h * 512:(h + 1) * 512, col:col + 512].rearrange("e (k p) n -> p (e k) n", p=P)
                load_chunk(c, src, laps, shape=4)

            def expert_loads(r):
                with sp.Fori(0, N_E // 2 - 1) as it:
                    for n in range(MOE_AHEAD, MOE_AHEAD + 2 * EXPERT_C):
                        expert_chunk(2 * it + n // EXPERT_C, n % EXPERT_C, MOE_C0 + n, round_laps(r) + 4 * it)
                c = MOE_C0 + (N_E - 2) * EXPERT_C
                for n in range(MOE_AHEAD, MOE_AHEAD + 2 * EXPERT_C):
                    expert_chunk((N_E - 2 + n // EXPERT_C) % N_E, n % EXPERT_C, c + n, round_laps(r))

            for n in range(MOE_AHEAD):
                expert_chunk(0, n, MOE_C0 + n, 0)
            expert_loads(0)
            sp.wait_ge(crowd_made, 1)
            more = sp.value_load(crowd_i[0:1, 0:1], min_val=0, max_val=ROUNDS - 1)
            with sp.If(more > 0):
                with sp.Fori(1, more + 1) as r:
                    expert_loads(r)
            for b in range(TB):
                sp.wait_ge(ln_rows, TB + b + 1)
                sp.dma_start(out[0, b * P:(b + 1) * P, :], x[:, b, :]).then_inc(out_stored, 16)
            sp.wait_ge(out_stored, 16 * TB)

        @block.gpsimd
        def _(pool):
            pool.wait_ge(bias_loaded, 16 * 6)
            n = 0
            for t in range(3):
                src = qk_flat[0:96, t * D:(t + 1) * D]
                part = qk_flat[0:96, 3 * D:3 * D + 512].bitcast(BF16)
                for r in range(3):
                    if r:
                        pool.tensor_tensor(src, src, part, ALU.subtract).then_inc(bias_step, 1)
                        n += 1
                        pool.wait_ge(bias_step, n)
                    pool.tensor_copy(part, src).then_inc(bias_step, 1)
                    n += 1
                    pool.wait_ge(bias_step, n)
                    last = pool.tensor_copy(bias_parts[32 * r:32 * r + 32, t * D:(t + 1) * D],
                                            part[32 * r:32 * r + 32, :])
                    if t < 2 or r < 2:
                        last.then_inc(bias_step, 1)
                        n += 1
                        pool.wait_ge(bias_step, n)
            last.then_inc(bias_made, 1)
            pool.wait_ge(flip_loaded, 16)
            pool.wait_ge(bias_made, 1)
            pool.tensor_copy(flip_bf[:], flip[:]).then_inc(mask_made, 1)
            pool.wait_ge(mask_made, 1)
            pool.memset(chunk_mask[:], 0.0).then_inc(mask_made, 1)
            pool.wait_ge(mask_made, 2)
            pool.memset(chunk_mask[64:P, 192:REL_W], NEG).then_inc(mask_made, 1)
            pool.wait_ge(strip_loaded, 16 * 12)
            pool.wait_ge(mask_made, 3)
            pool.memset(strip[64:P, :, 192:REL_W], NEG).then_inc(strip_ready, 1)

        @block.scalar
        def _(sc):
            def cut(c, laps=0):
                sc.wait_ge(raw_loaded[c % RAW], 16 * (c // RAW + 1) + 16 * laps)
                if c >= CUT:
                    sc.wait_ge(chunk_used, c + 1 + LAP * laps - (CUT if c < MOE_C0 + MOE_AHEAD else MOE_CUT))
                sc.activation(cut_slot(c)[0], raw[:, c % RAW, :], ACT.Copy).then_inc(hi_made, 1)

            def warm(func):
                sc.activation(stat[:, 12:13], ident[:, 0:1], func)

            def norm(n, t, src, ready=None):
                warm(ACT.Sqrt)
                if t:
                    sc.wait_ge(turned, 4 * t)
                for b in range(TB):
                    if ready:
                        sc.wait_ge(x_updated, ready + b)
                    sc.activation(nat[:, b, :], src[:, b, :], ACT.Square,
                                  accum_out=stat[:, b:b + 1]).then_inc(squared, 1)
                sc.wait_ge(ms_made, n + 1)
                sc.activation(stat[:, 4:6], stat[:, 2:4], ACT.Sqrt).then_inc(std_made, 1)

            def turn(t, gain=None):
                for q in range(4):
                    sc.wait_ge(turned, 4 * t + q + 1)
                    if gain is None:
                        sc.activation(xT_hi[:, 2 * q:2 * q + 2, :].rearrange("p a b -> p (a b)"), ps[:, q, :],
                                      ACT.Copy).then_inc(turn_hi, 1)
                    else:
                        for k in (2 * q, 2 * q + 1):
                            ins = sc.activation(xT_hi[:, k, :], ps[:, q, (k % 2) * S:(k % 2 + 1) * S],
                                                ACT.Identity, scale=gcol[:, gain + k:gain + k + 1])
                        ins.then_inc(turn_hi, 1)

            def ffn_step(g, c, slot, laps=0):
                sc.wait_ge(chunk_used, c + 1 + LAP * laps)
                sc.activation(sig[:, slot, :], ps[:, 2 * slot, :], ACT.Sigmoid).then_inc(sig_made, 1)
                sc.wait_ge(act_made, g + 1)
                sc.activation(a_hi[:, slot, :], act[:, slot, :], ACT.Copy).then_inc(act_hi, 1)

            def ffn_phase(f, c0, other=None):
                cut(c0 + AHEAD)
                cut(c0 + 1 + AHEAD)
                ffn_step(FFN_PAIRS * f, c0, 0)
                if other:
                    other()
                with sc.Fori(0, (FFN_PAIRS - 1) // 2) as it:
                    for jj in range(2):
                        c = c0 + 2 + 3 * jj
                        cut(c + AHEAD, it)
                        cut(c + 1 + AHEAD, it)
                        ffn_step(2 * it + (FFN_PAIRS * f + 1 + jj), c, 1 - jj, it)
                        cut(c + 2 + AHEAD, it)
                cut(c0 + FFN_C - 1 + AHEAD)

            def project(g0, c0, order, dst, during=None, heads_of=None):
                for n, col in enumerate(order):
                    g, c = g0 + n, c0 + 2 * n
                    late = heads_of is not None and n == 4
                    if not late:
                        cut(c + AHEAD)
                    if n and heads_of is not None:
                        head_roots(heads_of, n)
                    if late:
                        cut(c + AHEAD)
                    cut(c + 1 + AHEAD)
                    if during:
                        during()
                    if dst is None:
                        continue
                    sc.wait_ge(chunk_used, c + 2)
                    bank = 4 + 2 * (g % 2)
                    sc.activation(dst[:, :, 512 * col:512 * (col + 1)], ps[:, bank:bank + 2, :],
                                  ACT.Copy).then_inc(proj_read, 1)

            def qk_copies(w, kind):
                for r in range(2):
                    for t in range(8):
                        if is_key(kind, 8 * r + t):
                            sc.wait_ge(qk_turned, 8 * w + 4 * r + t // 2 + 1)
                            sc.activation(qkT[:, 8 * r + t, :], ps[:, t // 2, (t % 2) * S:(t % 2 + 1) * S],
                                          ACT.Copy).then_inc(k_copied, 1)

            def attend(u0, groups):
                def exps(n):
                    g, u, p = groups[n], u0 + n, (u0 + n) % 2
                    sc.wait_ge(max_made, u + 1)
                    for h in range(4):
                        src = ps[:, 2 * p + h % 2, (h // 2) * S:(h // 2) * S + g["nk"] * P]
                        ins = sc.activation(prob[:, p, h, 0:g["nk"] * P], src, ACT.Exp, bias=soft[:, p, h:h + 1],
                                            accum_out=soft[:, p, 4 + h:5 + h])
                    ins.then_inc(prob_made, 1)

                exps(0)
                exps(1)
                sc.wait_ge(ext_stored, 16)
                for n in range(len(groups)):
                    g, u = groups[n], u0 + n
                    sc.wait_ge(probT_turned, u + 1)
                    if u:
                        sc.wait_ge(pv_done, u)
                    m = g["n"] * g["nk"] * P
                    sc.activation(probT[:].rearrange("p a b c -> p (a b c)")[:, 0:m],
                                  ps[:, 4:6, :].rearrange("p a b -> p (a b)")[:, 0:m],
                                  ACT.Copy).then_inc(probT_made, 1)
                    if n + 2 < len(groups):
                        exps(n + 2)

            def layer_norm(n):
                warm(ACT.Sqrt)
                sc.wait_ge(ln_var, n + 1)
                sc.activation(stat[:, 4:6], stat[:, 2:4], ACT.Sqrt).then_inc(ln_std, 1)

            def head_roots(i, n):
                s0 = head_sums(n)
                sc.wait_ge(head_ms, 4 * i + n)
                sc.activation(sums[:, :, s0:s0 + 8], sums[:, :, s0:s0 + 8], ACT.Sqrt).then_inc(head_std, 1)

            def angles():
                sc.wait_ge(lam_step, 4)
                sc.activation(lam[:, 2:4], lam[:, 0:2], ACT.Exp).then_inc(lam_exp, 1)
                sc.wait_ge(trig_step, TRIG_STEPS)
                sc.activation(trig[:, :, 0, :], ang[:, 3, :].rearrange("p (b f) -> p b f", b=TB), ACT.Sin).then_inc(trig_sin, 1)
                sc.activation(trig[:, :, 1, :], ang[:, 2, :].rearrange("p (b f) -> p b f", b=TB), ACT.Sin).then_inc(trig_sin, 1)

            def memory_norm(i):
                sc.wait_ge(mem_loaded, 16 * (i + 1))
                norm(n_of(i, T_MEM), t_of(i, T_MEM), mem)

            sc.wait_ge(ident_loaded, 16)
            for i in range(2):
                kind = ("rel", "diff")[i]
                if i == 0:
                    sc.wait_ge(x_loaded, 16)
                norm(n_of(i, T_FFN1), t_of(i, T_FFN1), x, 4 * i - 1 if i else None)
                if i == 0:
                    cut(0)
                    cut(1)
                turn(t_of(i, T_FFN1), gain0[T_FFN1] + 8 * i)
                ffn_phase(2 * i, c_ffn1(i), lambda: memory_norm(i))
                turn(t_of(i, T_MEM), gain0[T_MEM] + 8 * i)
                project(g_kv(i), c_kv(i), range(1), kvm, lambda: norm(n_of(i, T_MIX), t_of(i, T_MIX), x, 4 * i + 1))
                turn(t_of(i, T_MIX), gain0[T_MIX] + 8 * i)
                project(g_in(i), c_in(i), IN_ORDER, pr_view("rel"), heads_of=i)
                qk_copies(i, kind)
                attend(u_layer(i), attention_groups(kind))
                if i == 1:
                    warm(ACT.Sqrt)
                    sc.wait_ge(sub_ms, 1)
                    sc.activation(sums[:, :, 0:6], sums[:, :, 0:6], ACT.Sqrt).then_inc(sub_std, 1)
                turn(t_of(i, T_O))
                project(g_out(i), c_out(i), range(2), None)
                sc.wait_ge(proj_read, g_out(i) + 2)
                norm(n_of(i, T_FFN2), t_of(i, T_FFN2), x)
                turn(t_of(i, T_FFN2), gain0[T_FFN2] + 8 * i)
                ffn_phase(2 * i + 1, c_ffn2(i), angles if i == 0 else None)
            turn(t_moba)
            project(g_moba, c_moba, range(6), pr_view("moba"))
            qk_copies(2, "moba")
            attend(u_moba, attention_groups("moba"))
            turn(t_moba_o)
            project(g_moba_out, c_moba_out, range(2), None)
            sc.wait_ge(moe_loaded, MOE_LOADS)
            sc.activation(wr2[:, :, 0, :], wr[:], ACT.Copy).then_inc(wr_cut, 1)
            layer_norm(0)
            turn(t_moe)
            for b in range(TB):
                sc.activation(xn_hi[:, b, :], x[:, b, :], ACT.Copy).then_inc(xn_hi_made, 1)
            warm(ACT.Exp)
            sc.wait_ge(logits_done, 1)
            sc.activation(lgT[:], ps[0:2 * N_E, 0, 0:S], ACT.Copy).then_inc(logits_copied, 1)
            sc.wait_ge(shifted, TB)
            sc.activation(share[:], share[:], ACT.Exp).then_inc(route_exp, 1)

            def gathered_rows(e, bank):
                sc.wait_ge(gathered, e + 1)
                sc.activation(xs[:, :, 0:SLOTS], ps[:, bank, :].rearrange("p (k s) -> p k s", k=KT),
                              ACT.Copy).then_inc(xs_hi_made, 1)

            def read_rows(half, up, bank, c, laps):
                sc.wait_ge(chunk_used, c + LAP * laps)
                sc.activation(h_rows[:, half, up, :], ps[:, bank, :], ACT.Copy).then_inc(h_read, 1)

            def sigmoid(e, half):
                sc.wait_ge(limited, 2 * e + half + 1)
                sc.activation(m_sig[:], m_g[:], ACT.Sigmoid, scale=SWIGLU_ALPHA).then_inc(m_sig_made, 1)

            def activations(e, half):
                sc.wait_ge(m_act_made, 2 * e + half + 1)
                sc.activation(m[:, 4 * half:4 * half + 4, 0:SLOTS],
                              m_act[:, half, :].rearrange("p (k s) -> p k s", k=4), ACT.Copy).then_inc(m_hi_made, 1)

            def outputs(e, par, bank):
                sc.wait_ge(scattered, e + 2)
                sc.wait_ge(gate_made, e + 2)
                sc.activation(y_hi[:], ps[:, bank:bank + 2, :].rearrange("p a b -> p (a b)"), ACT.Identity,
                              scale=slot_gate[:, par:par + 1]).then_inc(y_hi_made, 1)

            def expert(e, par, c, laps):
                g0 = 2 * par
                g1 = 2 - g0
                for n in range(EXPERT_C):
                    cut(c + n + MOE_AHEAD, laps)
                    if n == 5:
                        sigmoid(e, 0)
                    if n in (1, 3, 5, 7):
                        half, up = n // 4, (n // 2) % 2
                        read_rows(half, up, (g0, g1)[half] + up, c + n + 1, laps)
                    if n == 5:
                        sc.wait_ge(pickT_turned, e + 1)
                        sc.wait_ge(scattered, e + 2)
                        sc.activation(pickT[:], ps[:, g0 + 1, 0:S], ACT.Copy).then_inc(pickT_made, 1)
                        sc.activation(slot_gate[:, par:par + 1], ps[:, g0 + 1, S:S + 1], ACT.Copy).then_inc(gate_made, 1)
                    if n == 6:
                        activations(e, 0)
                    if n == 8:
                        sigmoid(e, 1)
                        activations(e, 1)
                    if n == 10:
                        gathered_rows(e + 1, g1 + 1)
                sc.wait_ge(chunk_used, c + EXPERT_C + LAP * laps)
                outputs(e, par, g0)

            warm(ACT.Sigmoid)
            outputs(-1, 1, 2)
            gathered_rows(0, 1)
            cut(MOE_C0 + AHEAD)

            def round_of_experts(r):
                with sc.Fori(0, N_E // 2) as it:
                    for par in range(2):
                        expert(2 * it + N_E * r + par, par, MOE_C0 + par * EXPERT_C, round_laps(r) + 4 * it)

            round_of_experts(0)
            sc.wait_ge(crowd_made, 1)
            more = sc.value_load(crowd_i[0:1, 0:1], min_val=0, max_val=ROUNDS - 1)
            with sc.If(more > 0):
                with sc.Fori(1, more + 1) as r:
                    round_of_experts(r)
            layer_norm(1)

        @block.vector
        def _(ve):
            def cut(c, laps=0):
                ve.wait_ge(hi_made, c + 1 + LAP * laps)
                hi, lo = cut_slot(c)
                ve.tensor_tensor(lo, raw[:, c % RAW, :], hi.bitcast(F32),
                                 ALU.subtract).then_inc(lo_made, 1)

            def norm(n, src):
                ve.wait_ge(squared, TB * (n + 1))
                ve.tensor_scalar(stat[:, 2:4], stat[:, 0:2], 1.0 / D, EPS, ALU.mult, ALU.add).then_inc(ms_made, 1)
                ve.wait_ge(std_made, n + 1)
                ve.reciprocal(stat[:, 6:8], stat[:, 4:6]).then_inc(rstd_made, 1)
                ve.wait_ge(rstd_made, n + 1)
                for b in range(TB):
                    ve.tensor_scalar(nat[:, b, :], src[:, b, :], stat[:, 6 + b:7 + b], None, ALU.mult).then_inc(normed, 1)

            def turn(t, gain=None):
                for q in range(4):
                    ve.wait_ge(turn_hi, 4 * t + q + 1)
                    hi = xT_hi[:, 2 * q:2 * q + 2, :].bitcast(F32)
                    if gain is None:
                        ve.tensor_tensor(xT_lo[:, 2 * q:2 * q + 2, :].rearrange("p a b -> p (a b)"), ps[:, q, :],
                                         hi.rearrange("p a b -> p (a b)"), ALU.subtract).then_inc(turn_lo, 1)
                    else:
                        for k in (2 * q, 2 * q + 1):
                            ins = ve.scalar_tensor_tensor(
                                out=xT_lo[:, k, :], in0=ps[:, q, (k % 2) * S:(k % 2 + 1) * S],
                                scalar=gcol[:, gain + k:gain + k + 1], in1=xT_hi[:, k, :].bitcast(F32),
                                op0=ALU.mult, op1=ALU.subtract)
                        ins.then_inc(turn_lo, 1)

            def ffn_step(g, c, slot, laps=0):
                ve.wait_ge(sig_made, g + 1)
                ve.tensor_tensor(gated[:, slot, :], ps[:, 2 * slot, :], sig[:, slot, :], ALU.mult).then_inc(gated_made, 1)
                ve.wait_ge(gated_made, g + 1)
                ve.wait_ge(chunk_used, c + 2 + LAP * laps)
                ve.tensor_tensor(act[:, slot, :], ps[:, 2 * slot + 1, :], gated[:, slot, :], ALU.mult).then_inc(act_made, 1)
                ve.wait_ge(act_hi, g + 1)
                ve.tensor_tensor(a_lo[:, slot, :], act[:, slot, :], a_hi[:, slot, :].bitcast(F32),
                                 ALU.subtract).then_inc(act_lo, 1)

            def ffn_phase(f, c0, other=None):
                cut(c0 + AHEAD)
                cut(c0 + 1 + AHEAD)
                ffn_step(FFN_PAIRS * f, c0, 0)
                if other:
                    other()
                with ve.Fori(0, (FFN_PAIRS - 1) // 2) as it:
                    for jj in range(2):
                        c = c0 + 2 + 3 * jj
                        cut(c + AHEAD, it)
                        cut(c + 1 + AHEAD, it)
                        ffn_step(2 * it + (FFN_PAIRS * f + 1 + jj), c, 1 - jj, it)
                        cut(c + 2 + AHEAD, it)
                cut(c0 + FFN_C - 1 + AHEAD)
                ve.wait_ge(chunk_used, c0 + FFN_C)
                for b in range(TB):
                    ve.scalar_tensor_tensor(out=x[:, b, :], in0=ps[:, 4 + 2 * b:6 + 2 * b, :].rearrange("p a b -> p (a b)"),
                                            scalar=0.5, in1=x[:, b, :], op0=ALU.mult, op1=ALU.add).then_inc(x_updated, 1)

            def project(g0, c0, n_groups, add=None, heads_of=None, stats=False):
                for n in range(n_groups):
                    g, c = g0 + n, c0 + 2 * n
                    late = heads_of is not None and n == 4
                    if not late:
                        cut(c + AHEAD)
                    if n and heads_of is not None:
                        head_norms(heads_of, n)
                    if late:
                        cut(c + AHEAD)
                    cut(c + 1 + AHEAD)
                    if add is None:
                        continue
                    ve.wait_ge(chunk_used, c + 2)
                    bank = 4 + 2 * (g % 2)
                    cols = x[:, :, 512 * n:512 * (n + 1)]
                    ve.scalar_tensor_tensor(out=cols, in0=cols, scalar=add, in1=ps[:, bank:bank + 2, :],
                                            op0=ALU.mult, op1=ALU.add).then_inc(proj_read, 1)
                    if stats:
                        ve.wait_ge(proj_read, g + 1)
                        for b in range(TB):
                            ve.bn_stats(row_stats[:, b, n, :], x[:, b, 512 * n:512 * (n + 1)]).then_inc(ln_step, 1)

            def heads(t, n):
                return t.rearrange("p (h d) -> p h d", h=n)

            head_steps = [0]

            def head_norms(i, n):
                def step(ins):
                    ins.then_inc(head_step, 1)
                    head_steps[0] += 1

                def all_steps():
                    ve.wait_ge(head_step, head_steps[0])

                v = pr_view("rel")
                col = IN_ORDER[n - 1]
                s0 = head_sums(n)
                spans = [(v, 3 * SELF_W, 4, 24), (kvm, 0, 4, 28)] if n == 1 else [(v, 512 * col, 8, s0)]
                by_head = lambda t, k: t.rearrange("p b (h d) -> p b h d", h=k)
                tmp = prob[:].rearrange("p a b c -> p (a b c)").rearrange("p (a b w) -> p a b w", a=2, b=TB)
                ve.wait_ge(proj_read, g_in(i) + n)
                for m, (src, c0, k, s1) in enumerate(spans):
                    rows = src[:, :, c0:c0 + k * HD]
                    step(ve.tensor_tensor(tmp[:, m, :, 0:k * HD], rows, rows, ALU.mult))
                all_steps()
                for m, (src, c0, k, s1) in enumerate(spans):
                    step(ve.tensor_reduce(sums[:, :, s1:s1 + k], by_head(tmp[:, m, :, 0:k * HD], k), AX.X, ALU.add))
                all_steps()
                eight = sums[:, :, s0:s0 + 8]
                ve.tensor_scalar(eight, eight, 1.0 / HD, EPS, ALU.mult, ALU.add).then_inc(head_ms, 1)
                ve.wait_ge(head_std, 4 * i + n)
                step(ve.reciprocal(eight, eight))
                all_steps()
                for src, c0, k, s1 in spans:
                    rows = by_head(src[:, :, c0:c0 + k * HD], k)
                    over = sums[:, :, s1:s1 + k].unsqueeze(3).to_broadcast([P, TB, k, HD])
                    step(ve.tensor_tensor(rows, rows, over, ALU.mult))
                if i == 1 and n > 1:
                    all_steps()
                    ve.wait_ge(trig_sin, 2)
                    ve.wait_ge(trig_gains, 2 * TB)
                    spans = [(512 * col, 8, 0), (512 * col, 4, 0), (512 * col, 8, 1)][col:col + 1] + (
                        [(512 * col + 4 * HD, 4, 1)] if col == 1 else [])
                    part = lambda t, c0, k: by_head(t[:, :, c0:c0 + k * HD], k)
                    table = lambda t, w, k: turn_by[:, t, :, w, :].unsqueeze(2).to_broadcast([P, TB, k, HD])
                    for c0, k, w in spans:
                        step(ve.tensor_tensor(part(tmp[:, 1], c0 - 512 * col, k), part(v, c0, k), table(1, w, k), ALU.mult))
                    all_steps()
                    for c0, k, w in spans:
                        step(ve.tensor_tensor(part(v, c0, k), part(v, c0, k), table(0, w, k), ALU.mult))
                    all_steps()
                    both, crossed = part(v, 512 * col, 8), part(tmp[:, 1], 0, 8)
                    h0, h1 = slice(0, HD // 2), slice(HD // 2, HD)
                    step(ve.tensor_tensor(both[:, :, :, h0], both[:, :, :, h0], crossed[:, :, :, h1], ALU.subtract))
                    step(ve.tensor_tensor(both[:, :, :, h1], both[:, :, :, h1], crossed[:, :, :, h0], ALU.add))
                all_steps()
                ve.memset(stat[:, 13:14], 0.0).then_inc(heads_ready, 1)

            def qk_copies(w, kind):
                for r in range(2):
                    for t in range(8):
                        tile = 8 * r + t
                        if is_key(kind, tile):
                            continue
                        ve.wait_ge(qk_turned, 8 * w + tile // 2 + 1)
                        src = ps[:, t // 2, (t % 2) * S:(t % 2 + 1) * S]
                        if kind == "moba":
                            scale = P ** -0.5
                        elif tile >= 12:
                            scale = qscale[:, w:w + 1]
                        else:
                            scale = qscale[:, 2:3] if kind == "rel" else HD ** -0.5
                        ve.tensor_scalar(qkT[:, tile, :], src, scale, None, ALU.mult).then_inc(q_copied, 1)

            def attend(u0, groups):
                def lead(n):
                    g, u, p = groups[n], u0 + n, (u0 + n) % 2
                    ve.wait_ge(scored, u + 1)
                    s = ps[:, 2 * p:2 * p + 2, :].rearrange("p a (c k) -> p c a k", c=2)
                    if u >= 2:
                        ve.wait_ge(probT_turned, u - 1)
                    for c in range(2):
                        ins = ve.tensor_reduce(soft[:, p, 2 * c:2 * c + 2], s[:, c, :, 0:g["nk"] * P], AX.X, ALU.max, negate=True)
                    ins.then_inc(max_made, 1)

                def follow(n):
                    g, u, p = groups[n], u0 + n, (u0 + n) % 2
                    ve.wait_ge(prob_made, u + 1)
                    if n >= 2:
                        ve.wait_ge(o_made, u - 1)
                    ve.reciprocal(soft[:, p, 8:12], soft[:, p, 4:8]).then_inc(total_read, 1)
                    ve.wait_ge(total_read, u + 1)
                    if g["diff"]:
                        m, keys = n_diff(groups, n), slice(0, g["nk"] * P)
                        for h in range(2):
                            ve.tensor_scalar(soft[:, p, 12 + h:13 + h], soft[:, p, 9 + 2 * h:10 + 2 * h],
                                             lam[:, 5:6], None, ALU.mult).then_inc(mixed, 1)
                        ve.wait_ge(mixed, 6 * m - 4)
                        for h in range(2):
                            ve.tensor_scalar(prob[:, p, 2 * h + 1, keys], prob[:, p, 2 * h + 1, keys],
                                             soft[:, p, 12 + h:13 + h], None, ALU.mult).then_inc(mixed, 1)
                        ve.wait_ge(mixed, 6 * m - 2)
                        for h in range(2):
                            ve.scalar_tensor_tensor(out=prob[:, p, 2 * h, keys], in0=prob[:, p, 2 * h, keys],
                                                    scalar=soft[:, p, 8 + 2 * h:9 + 2 * h], in1=prob[:, p, 2 * h + 1, keys],
                                                    op0=ALU.mult, op1=ALU.subtract).then_inc(mixed, 1)

                def outputs(n):
                    g, u, p = groups[n], u0 + n, (u0 + n) % 2
                    ve.wait_ge(pv_done, u + 1)
                    k, dv = g["n"], g["dv"]
                    dst = nat[:, g["b"], g["o"]:g["o"] + k * dv]
                    src = ps[:, 6 + p, 0:k * dv]
                    if g["diff"]:
                        ve.tensor_copy(dst, src).then_inc(o_made, 1)
                        m, h0 = n_diff(groups, n), g["o"] // P
                        sq = ang[:].rearrange("p a b -> p (a b)")[:, 0:2 * P]
                        ve.wait_ge(o_made, u + 1)
                        ve.tensor_tensor(sq, dst, dst, ALU.mult).then_inc(sub_step, 1)
                        ve.wait_ge(sub_step, 2 * m - 1)
                        ve.tensor_reduce(sums[:, g["b"], h0:h0 + 2], heads(sq, 2), AX.X, ALU.add).then_inc(sub_step, 1)
                    else:
                        ve.tensor_tensor(heads(dst, k), heads(src, k),
                                         soft[:, p, 8:12].unsqueeze(2).to_broadcast([P, k, dv]), ALU.mult).then_inc(o_made, 1)

                lead(0)
                lead(1)
                follow(0)
                for n in range(len(groups)):
                    if n + 2 < len(groups):
                        lead(n + 2)
                    if n + 1 < len(groups):
                        follow(n + 1)
                    outputs(n)

            def layer_norm(n):
                ve.wait_ge(ln_step, 4 * (n + 1) + 2 * TB * n)
                for b in range(TB):
                    ins = ve.bn_aggr(mean_var[:, b, :], row_stats[:, b].rearrange("p a b -> p (a b)"))
                    ins.then_inc(ln_step, 1)
                ve.wait_ge(ln_step, 4 * (n + 1) + 2 * TB * n + TB)
                ve.tensor_scalar(stat[:, 2:4], mean_var[:, :, 1], LN_EPS, None, ALU.add).then_inc(ln_var, 1)
                for b in range(TB):
                    ve.scalar_tensor_tensor(out=x[:, b, :], in0=x[:, b, :], scalar=mean_var[:, b, 0:1],
                                            in1=ln[:, n, 0, :], op0=ALU.subtract, op1=ALU.mult).then_inc(ln_step, 1)
                    if b == 0:
                        ve.wait_ge(ln_std, n + 1)
                        ve.reciprocal(stat[:, 6:8], stat[:, 4:6]).then_inc(rstd_made, 1)
                        ve.wait_ge(rstd_made, 8 + n + 1)
                    ve.wait_ge(ln_step, 4 * (n + 1) + 2 * TB * n + TB + b + 1)
                    ve.scalar_tensor_tensor(out=x[:, b, :], in0=x[:, b, :], scalar=stat[:, 6 + b:7 + b],
                                            in1=ln[:, n, 1, :], op0=ALU.mult, op1=ALU.add).then_inc(ln_rows, 1)

            ve.wait_ge(gcol_turned, 1)
            ve.tensor_copy(gcol[:, 0:70], ps[:, 0, 0:70]).then_inc(qscale_made, 1)
            ve.wait_ge(qscale_made, 1)
            for n, (q, k) in enumerate(((64, 66), (65, 67), (68, 69))):
                ve.scalar_tensor_tensor(out=qscale[:, n:n + 1], in0=gcol[:, q:q + 1], scalar=HD ** -0.5,
                                        in1=gcol[:, k:k + 1], op0=ALU.mult, op1=ALU.mult).then_inc(qscale_made, 1)
            ve.wait_ge(qscale_made, 4)

            def angles():
                ve.wait_ge(small_loaded, 16 * 9)
                for n in range(2):
                    ve.tensor_tensor(ang[:, n, 0:HD], bc[:, 128 * n:128 * n + 64], bc[:, 128 * n + 64:128 * n + 128],
                                     ALU.mult).then_inc(lam_step, 1)
                    ve.wait_ge(lam_step, 2 * n + 1)
                    ve.tensor_reduce(lam[:, n:n + 1], ang[:, n, 0:HD], AX.X, ALU.add).then_inc(lam_step, 1)
                ve.wait_ge(lam_exp, 1)
                ve.tensor_tensor(lam[:, 4:5], lam[:, 2:3], lam[:, 3:4], ALU.subtract).then_inc(lam_step, 1)
                ve.wait_ge(lam_step, 5)
                ve.tensor_scalar(lam[:, 5:6], lam[:, 4:5], LAMBDA_INIT, None, ALU.add).then_inc(lam_step, 1)
                t = [0]

                def step(ins):
                    ins.then_inc(trig_step, 1)
                    t[0] += 1
                    ve.wait_ge(trig_step, t[0])

                step(ve.tensor_copy(pos_f[:], pos_i[:]))
                for b in range(TB):
                    step(ve.tensor_scalar(ang[:, 0, 32 * b:32 * b + 32], inv_row[:], pos_f[:, b:b + 1], None, ALU.mult))
                step(ve.tensor_scalar(ang[:, 1, :], ang[:, 0, :], 1.0 / (2 * math.pi), None, ALU.mult))
                step(ve.tensor_copy(turns_i[:], ang[:, 1, :]))
                step(ve.tensor_copy(ang[:, 1, :], turns_i[:]))
                c1 = 6.28125
                c2 = float(np.float32(np.round((2 * math.pi - c1) * 2 ** 21) / 2 ** 21))
                c3 = 2 * math.pi - c1 - c2
                src = 0
                for c in (c1, c2, c3):
                    step(ve.scalar_tensor_tensor(out=ang[:, 2, :], in0=ang[:, 1, :], scalar=-c, in1=ang[:, src, :],
                                                 op0=ALU.mult, op1=ALU.add))
                    src = 2
                step(ve.tensor_scalar(ang[:, 3, :], ang[:, 2, :], math.pi / 2, None, ALU.add))
                for k in (2, 3):
                    for bound, op, off in ((math.pi, ALU.is_gt, -2 * math.pi), (-math.pi, ALU.is_lt, 2 * math.pi)):
                        step(ve.tensor_scalar(ang[:, 4, :], ang[:, k, :], bound, off, op, ALU.mult))
                        step(ve.tensor_tensor(ang[:, k, :], ang[:, k, :], ang[:, 4, :], ALU.add))
                    step(ve.tensor_scalar(ang[:, k, :], ang[:, k, :], PI_BELOW, -PI_BELOW, ALU.min, ALU.max))
                assert t[0] == TRIG_STEPS
                ve.wait_ge(lam_step, 6)
                ve.tensor_scalar(bc[:, 384:512], bc[:, 384:512], 1.0 - LAMBDA_INIT, None, ALU.mult).then_inc(lam_step, 1)
                ve.wait_ge(trig_sin, 2)
                for t in range(2):
                    for b in range(TB):
                        ve.tensor_tensor(turn_by[:, t, b].rearrange("p w (h d) -> p (w h) d", h=2),
                                         bc[:, 4 * HD:6 * HD].rearrange("p (h d) -> p h d", h=4),
                                         trig[:, b, t, :].unsqueeze(1).to_broadcast([P, 4, 32]), ALU.mult).then_inc(trig_gains, 1)

            for i in range(2):
                kind = ("rel", "diff")[i]
                norm(n_of(i, T_FFN1), x)
                if i == 0:
                    cut(0)
                    cut(1)
                turn(t_of(i, T_FFN1), gain0[T_FFN1] + 8 * i)
                ffn_phase(2 * i, c_ffn1(i), lambda: norm(n_of(i, T_MEM), mem))
                turn(t_of(i, T_MEM), gain0[T_MEM] + 8 * i)
                if i == 0:
                    ve.wait_ge(ext_turned, 1)
                    ve.tensor_copy(ang[:, 0, 0:24], ps[:, 7, 0:24]).then_inc(ext_made, 1)
                project(g_kv(i), c_kv(i), 1)
                norm(n_of(i, T_MIX), x)
                if i == 0:
                    ve.wait_ge(ext_rows, 1)
                    ve.tensor_copy(row_by_distance(12), ps[0:12, 7, :]).then_inc(ext_copied, 1)
                turn(t_of(i, T_MIX), gain0[T_MIX] + 8 * i)
                project(g_in(i), c_in(i), 5, heads_of=i)
                qk_copies(i, kind)
                attend(u_layer(i), attention_groups(kind))
                if i == 1:
                    ve.wait_ge(sub_step, 2 * 6)
                    ve.tensor_scalar(sums[:, :, 0:6], sums[:, :, 0:6], 1.0 / P, EPS, ALU.mult, ALU.add).then_inc(sub_ms, 1)
                    ve.wait_ge(sub_std, 1)
                    ve.reciprocal(sums[:, :, 0:6], sums[:, :, 0:6]).then_inc(sub_step, 1)
                    ve.wait_ge(sub_step, 2 * 6 + 1)
                    for b in range(TB):
                        for h in range(6):
                            view = nat[:, b, h * P:(h + 1) * P]
                            ins = ve.scalar_tensor_tensor(out=view, in0=view, scalar=sums[:, b, h:h + 1],
                                                          in1=bc[:, 384:512], op0=ALU.mult, op1=ALU.mult)
                        ins.then_inc(sub_normed, 1)
                turn(t_of(i, T_O))
                project(g_out(i), c_out(i), 2, add=1.0)
                norm(n_of(i, T_FFN2), x)
                turn(t_of(i, T_FFN2), gain0[T_FFN2] + 8 * i)
                ffn_phase(2 * i + 1, c_ffn2(i), angles if i == 0 else None)
            turn(t_moba)
            ve.wait_ge(ext_rows, 2)
            ve.tensor_copy(row_by_distance(8), ps[0:8, 7, :]).then_inc(ext_made, 1)
            ve.wait_ge(ext_made, 2)
            ve.memset(row_by_distance(8)[:, S:512], NEG).then_inc(ext_copied, 1)
            project(g_moba, c_moba, 6)
            qk_copies(2, "moba")
            attend(u_moba, attention_groups("moba"))
            turn(t_moba_o)
            project(g_moba_out, c_moba_out, 2, add=ALPHA, stats=True)
            ve.wait_ge(moe_loaded, MOE_LOADS)
            layer_norm(0)
            ve.wait_ge(wr_cut, 1)
            ve.tensor_tensor(wr2[:, :, 1, :], wr[:], wr2[:, :, 0, :].bitcast(F32), ALU.subtract).then_inc(wr_ready, 1)
            turn(t_moe)
            for b in range(TB):
                ve.wait_ge(xn_hi_made, b + 1)
                ve.tensor_tensor(xn_lo[:, b, :], x[:, b, :], xn_hi[:, b, :].bitcast(F32), ALU.subtract).then_inc(xn_lo_made, 1)
            ve.memset(slot_gate[:], 0.0).then_inc(gate_made, 1)
            for b in range(TB):
                ve.tensor_scalar(pickT[:, b * P:(b + 1) * P], ones, 0.0, None, ALU.mult).then_inc(m_zero, 1)
            r = [0]

            def route(*steps):
                for ins in steps:
                    ins.then_inc(route_step, 1)
                r[0] += len(steps)
                ve.wait_ge(route_step, r[0])

            route(ve.memset(gate[:, :, EV - 2:EV], 0.0), ve.memset(place[:, :, EV - 2:EV], -1.0),
                  ve.memset(needles[:, :, TOP_K:8], BIG))
            ve.wait_ge(logits_folded, 1)
            route(ve.tensor_tensor(lg[:], ps[:, 0, S:S + TB * N_E].rearrange("p (b e) -> p b e", b=TB),
                                   lg_row[:].unsqueeze(1).to_broadcast([P, TB, N_E]), ALU.add))
            route(*[ve.max(top8[:, b, :], lg[:, b, :]) for b in range(TB)])
            route(ve.tensor_copy(needles[:, :, 0:TOP_K], top8[:, :, 0:TOP_K]))
            route(*[ve.match_replace(rest[:, b, :], needles[:, b, :], lg[:, b, :], -BIG) for b in range(TB)])
            ve.tensor_scalar(chosen[:], rest[:], -BIG, None, ALU.is_equal).then_inc(chosen_made, 1)
            for b in range(TB):
                ve.tensor_scalar(share[:, b, :], lg[:, b, :], top8[:, b, 0:1], None, ALU.subtract).then_inc(shifted, 1)
            ve.wait_ge(chosen_made, 1)
            ve.wait_ge(crowd_done, 1)
            counts = ps[:, 0, S + TB * N_E:S + (TB + 3) * N_E]
            route(ve.scalar_tensor_tensor(out=counted[:], in0=counts[:, 0:TB * N_E].rearrange("p (b e) -> p b e", b=TB),
                                          scalar=1.0, in1=chosen[:], op0=ALU.add, op1=ALU.mult))
            route(*[ve.tensor_scalar(place[:, :, N_E * k:N_E * (k + 1)], counted[:], float(-1 - k * SLOTS), None, ALU.add)
                    for k in range(ROUNDS)])
            def picks(e, par):
                for b in range(TB):
                    ins = ve.tensor_scalar(pick[:, par, b, :], iota_row, place[:, b, bass.ds(e, 1)], None, ALU.is_equal)
                ins.then_inc(picked, 1)

            def bias_rows(e, par):
                ve.tensor_scalar(sel[:, par, :], first_slots[0:96, :], onehot96[:, bass.ds(e, 1)], None,
                                 ALU.mult).then_inc(picked, 1)

            def gathered_rows(e, bank):
                ve.wait_ge(xs_hi_made, e + 1)
                ve.tensor_tensor(xs[:, :, SLOTS:P], ps[:, bank, :].rearrange("p (k s) -> p k s", k=KT),
                                 xs[:, :, 0:SLOTS].bitcast(F32), ALU.subtract).then_inc(xs_lo_made, 1)

            def limits(e, half, bank):
                n = 2 * e + half + 1
                ve.wait_ge(folded, n)
                ve.tensor_scalar(m_g[:], ps[:, bank, 0:256], LIMIT, None, ALU.min).then_inc(limited, 1)
                ve.tensor_scalar(m_u[:], ps[:, bank, 256:512], LIMIT, -LIMIT, ALU.min, ALU.max).then_inc(up_limited, 1)
                ve.wait_ge(limited, n)
                ve.wait_ge(up_limited, n)
                ve.scalar_tensor_tensor(out=m_gu[:], in0=m_u[:], scalar=1.0, in1=m_g[:], op0=ALU.add,
                                        op1=ALU.mult).then_inc(m_gu_made, 1)

            def activations(e, half):
                n = 2 * e + half + 1
                ve.wait_ge(m_gu_made, n)
                ve.wait_ge(m_sig_made, n)
                ve.tensor_tensor(m_act[:, half, :], m_gu[:], m_sig[:], ALU.mult).then_inc(m_act_made, 1)

            def low_activations(e, half):
                ve.wait_ge(m_hi_made, 2 * e + half + 1)
                ks = slice(4 * half, 4 * half + 4)
                ve.tensor_tensor(m[:, ks, SLOTS:P], m_act[:, half, :].rearrange("p (k s) -> p k s", k=4),
                                 m[:, ks, 0:SLOTS].bitcast(F32), ALU.subtract).then_inc(m_lo_made, 1)

            def outputs(e, par, bank):
                ve.wait_ge(y_hi_made, e + 2)
                ve.scalar_tensor_tensor(out=y_lo[:], in0=ps[:, bank:bank + 2, :].rearrange("p a b -> p (a b)"),
                                        scalar=slot_gate[:, par:par + 1], in1=y_hi[:].bitcast(F32),
                                        op0=ALU.mult, op1=ALU.subtract).then_inc(y_lo_made, 1)

            def expert(e, e_in_round, par, c, laps):
                g0 = 2 * par
                g1 = 2 - g0
                for n in range(EXPERT_C):
                    cut(c + n + MOE_AHEAD, laps)
                    if n == 1:
                        picks(e + 1, 1 - par)
                        bias_rows(e_in_round + 1, 1 - par)
                    if n == 4:
                        limits(e, 0, g0)
                    if n == 5:
                        activations(e, 0)
                    if n == 6:
                        low_activations(e, 0)
                    if n == 8:
                        limits(e, 1, g1)
                        activations(e, 1)
                        low_activations(e, 1)
                    if n == 10:
                        gathered_rows(e + 1, g1 + 1)
                outputs(e, par, g0)

            picks(0, 0)
            bias_rows(0, 0)
            ve.wait_ge(route_exp, 1)
            route(ve.tensor_tensor(share[:], share[:], chosen[:], ALU.mult))
            route(ve.tensor_reduce(share_sum[:], share[:], AX.X, ALU.add))
            route(ve.reciprocal(share_sum[:], share_sum[:]))
            route(*[ve.tensor_scalar(gate[:, b, 0:ROUNDS * N_E].rearrange("p (k e) -> p k e", k=ROUNDS),
                                     share[:, b, :].unsqueeze(1).to_broadcast([P, ROUNDS, N_E]),
                                     share_sum[:, b:b + 1], None, ALU.mult) for b in range(TB)])
            route(ve.tensor_reduce(crowd[:, N_E:N_E + 1], counts[:, TB * N_E:(TB + 1) * N_E], AX.X, ALU.max))
            route(ve.tensor_scalar(crowd[:, N_E + 1:N_E + 2], crowd[:, N_E:N_E + 1], float(SLOTS), None, ALU.is_gt))
            for k in range(2, ROUNDS):
                route(ve.scalar_tensor_tensor(out=crowd[:, N_E + k:N_E + k + 1], in0=crowd[:, N_E:N_E + 1],
                                              scalar=float(k * SLOTS), in1=crowd[:, N_E + k - 1:N_E + k],
                                              op0=ALU.is_gt, op1=ALU.add))
            ve.tensor_copy(crowd_i[:, 0:1], crowd[:, N_E + ROUNDS - 1:N_E + ROUNDS]).then_inc(crowd_made, 1)
            outputs(-1, 1, 2)
            gathered_rows(0, 1)
            cut(MOE_C0 + AHEAD)

            def round_of_experts(r):
                with ve.Fori(0, N_E // 2) as it:
                    for par in range(2):
                        expert(2 * it + N_E * r + par, 2 * it + par, par, MOE_C0 + par * EXPERT_C,
                               round_laps(r) + 4 * it)

            round_of_experts(0)
            ve.wait_ge(crowd_made, 1)
            more = ve.value_load(crowd_i[0:1, 0:1], min_val=0, max_val=ROUNDS - 1)
            with ve.If(more > 0):
                with ve.Fori(1, more + 1) as r:
                    round_of_experts(r)
            ve.wait_ge(last_scattered, 1)
            for b in range(TB):
                ve.scalar_tensor_tensor(out=x[:, b, :], in0=x[:, b, :], scalar=ALPHA,
                                        in1=ps[:, 4 + 2 * b:6 + 2 * b, :].rearrange("p a b -> p (a b)"),
                                        op0=ALU.mult, op1=ALU.add).then_inc(x_updated, 1)
                ve.wait_ge(x_updated, 8 + b + 1)
                for h in range(2):
                    ve.bn_stats(row_stats[:, b, h, :], x[:, b, 512 * h:512 * (h + 1)]).then_inc(ln_step, 1)
            layer_norm(1)

        @block.tensor
        def _(pe):
            def three(o, l_hi, l_lo, r_hi, r_lo, start, stop):
                pe.matmul(o, l_hi, r_hi, start=start, stop=False)
                pe.matmul(o, l_hi, r_lo, start=False, stop=False)
                return pe.matmul(o, l_lo, r_hi, start=False, stop=stop)

            def turn(src, ready, count):
                for b in range(TB):
                    pe.wait_ge(ready, count + b)
                    for q in range(4):
                        for k in (2 * q, 2 * q + 1):
                            o = (k % 2) * S + b * P
                            ins = pe.transpose(ps[:, q, o:o + P], src[:, b, k * P:(k + 1) * P], ident[:])
                        if b == TB - 1:
                            ins.then_inc(turned, 1)

            def turned_tile(t, k):
                if k % 2 == 0:
                    pe.wait_ge(turn_lo, 4 * t + k // 2 + 1)

            def ffn_in(c, bank, laps=0, t=None):
                pe.wait_ge(lo_made, c + 1 + LAP * laps)
                s = c % CUT
                for f in range(2):
                    for k in range(KT):
                        if t is not None and f == 0:
                            turned_tile(t, k)
                        w = slice(k * 256 + f * P, k * 256 + (f + 1) * P)
                        ins = three(ps[:, bank, f * S:(f + 1) * S], w_hi[:, s, w], w_lo[:, s, w],
                                    xT_hi[:, k, :], xT_lo[:, k, :], k == 0, k == KT - 1)
                ins.then_inc(chunk_used, 1)

            def ffn_out(c, slot, g, first=False, last=False, laps=0):
                pe.wait_ge(act_lo, g + 1)
                pe.wait_ge(lo_made, c + 1 + LAP * laps)
                s = c % CUT
                for k in range(2):
                    for b in range(TB):
                        for h in range(2):
                            l = slice(k * S + b * P, k * S + (b + 1) * P)
                            w = slice(k * D + h * 512, k * D + (h + 1) * 512)
                            ins = three(ps[:, 4 + 2 * b + h, :], a_hi[:, slot, l], a_lo[:, slot, l],
                                        w_hi[:, s, w], w_lo[:, s, w], first and k == 0, last and k == 1)
                ins.then_inc(chunk_used, 1)

            def ffn_phase(f, c0, t):
                g0 = FFN_PAIRS * f
                ffn_in(c0, 0, t=t)
                ffn_in(c0 + 1, 1)

                def step(slot, c, laps, first, g):
                    if not first:
                        pe.wait_ge(act_made, g - 1)
                    ffn_in(c, 2 * slot, laps)
                    ffn_in(c + 1, 2 * slot + 1, laps)
                    ffn_out(c + 2, 1 - slot, g - 1, first=first, laps=laps)

                step(1, c0 + 2, 0, True, g0 + 1)
                step(0, c0 + 5, 0, False, g0 + 2)
                with pe.Fori(1, (FFN_PAIRS - 1) // 2) as it:
                    for jj in range(2):
                        step(1 - jj, c0 + 2 + 3 * jj, it, False, 2 * it + (g0 + 1 + jj))
                ffn_out(c0 + FFN_C - 1, 0, g0 + FFN_PAIRS - 1, last=True)

            def project(g0, c0, n_groups, t):
                for n in range(n_groups):
                    g = g0 + n
                    if g >= 2:
                        pe.wait_ge(proj_read, g - 1)
                    for h in range(2):
                        c = c0 + 2 * n + h
                        pe.wait_ge(lo_made, c + 1)
                        s = c % CUT
                        for b in range(TB):
                            for k in range(4):
                                kk = 4 * h + k
                                if n == 0 and b == 0:
                                    turned_tile(t, kk)
                                w = slice(k * 512, (k + 1) * 512)
                                l = slice(b * P, (b + 1) * P)
                                ins = three(ps[:, 4 + 2 * (g % 2) + b, :], xT_hi[:, kk, l], xT_lo[:, kk, l],
                                            w_hi[:, s, w], w_lo[:, s, w], kk == 0, kk == KT - 1)
                        ins.then_inc(chunk_used, 1)

            def turn_qk(w, kind):
                v = pr_view(kind)
                for r in range(2):
                    for t in range(8):
                        tile = 8 * r + t
                        if r == 1 and t % 2 == 0:
                            for tt in (t, t + 1):
                                if is_key(kind, tt):
                                    pe.wait_ge(k_copied, 8 * w + 1 + sum(is_key(kind, m) for m in range(tt)))
                                else:
                                    pe.wait_ge(q_copied, 8 * w + 1 + sum(not is_key(kind, m) for m in range(tt)))
                        for b in range(TB):
                            if kind != "moba" and tile >= 14:
                                src = kvm[:, b, (tile - 14) * P:(tile - 13) * P]
                            elif kind != "moba" and tile >= 12:
                                c = 3 * SELF_W + (tile - 12) * P
                                src = v[:, b, c:c + P]
                            else:
                                src = v[:, b, tile * P:(tile + 1) * P]
                            o = (t % 2) * S + b * P
                            ins = pe.transpose(ps[:, t // 2, o:o + P], src, ident[:])
                        if t % 2:
                            ins.then_inc(qk_turned, 1)

            def attend(u0, groups, kind, w):
                def scores(n):
                    g, u, p = groups[n], u0 + n, (u0 + n) % 2
                    if n >= 2:
                        pe.wait_ge(prob_made, u - 1)
                    if g["bias"] and kind != "moba":
                        pe.wait_ge(*((strip_ready, 1), (mask_made, 3))[w])
                    for h, (qt, kt, half) in enumerate(g["qk"]):
                        rows = slice(0, P) if half is None else slice(half * HD, (half + 1) * HD)
                        q0 = g["b"] * P
                        nk = g["nk"] * P
                        o = ps[:, 2 * p + h % 2, (h // 2) * S:(h // 2) * S + nk]
                        ins = pe.matmul(o, qkT[rows, qt, q0:q0 + P], qkT[rows, kt, 0:nk], start=True, stop=not g["bias"])
                        if g["bias"]:
                            h0, _ = g["bias"]
                            m0 = P if g["b"] == 0 else 0
                            if kind == "diff":
                                ins = pe.matmul(o, flip_bf[:], chunk_mask[:, m0:m0 + nk], start=False, stop=True)
                            else:
                                ins = pe.matmul(o, flip[:], strip[:, h0 + h, m0:m0 + nk], start=False, stop=True)
                    ins.then_inc(scored, 1)

                def values(n):
                    g, u, p = groups[n], u0 + n, (u0 + n) % 2
                    if g["diff"]:
                        pe.wait_ge(mixed, 6 * n_diff(groups, n))
                    else:
                        pe.wait_ge(prob_made, u + 1)
                    if n:
                        pe.wait_ge(probT_made, u)
                    for h in range(g["n"]):
                        row = 2 * h if g["diff"] else h
                        for k in range(g["nk"]):
                            col = (h * g["nk"] + k) * P
                            ins = pe.transpose(ps[:, 4 + col // 512, col % 512:col % 512 + P],
                                               prob[:, p, row, k * P:(k + 1) * P], ident[:])
                    ins.then_inc(probT_turned, 1)

                def outputs(n):
                    g, u, p = groups[n], u0 + n, (u0 + n) % 2
                    pe.wait_ge(probT_made, u + 1)
                    if n >= 2:
                        pe.wait_ge(o_made, u - 1)
                    where, v0 = g["v"]
                    v = kvm if where == "kvm" else pr_view(kind)
                    dv = g["dv"]
                    for h in range(g["n"]):
                        for k in range(g["nk"]):
                            col = (h * g["nk"] + k) * P
                            ins = pe.matmul(ps[:, 6 + p, h * dv:(h + 1) * dv],
                                            probT[:].rearrange("p a b c -> p (a b c)")[:, col:col + P],
                                            v[:, k, v0 + h * dv:v0 + (h + 1) * dv], start=k == 0,
                                            stop=k == g["nk"] - 1)
                    ins.then_inc(pv_done, 1)

                pe.wait_ge(flip_loaded, 16)
                if kind == "moba":
                    pe.wait_ge(strip_loaded, 16 * 20)
                pe.wait_ge(proj_read, (g_in(w) + 5) if w < 2 else g_moba + 6)
                pe.wait_ge(q_copied, 8 * (w + 1))
                pe.wait_ge(k_copied, 8 * (w + 1))
                scores(0)
                scores(1)
                for n in range(len(groups)):
                    values(n)
                    if n + 2 < len(groups):
                        scores(n + 2)
                    outputs(n)

            pe.wait_ge(ident_loaded, 16)
            pe.wait_ge(rows_loaded, 16 * 8)
            pe.transpose(ps[:, 0, 0:70], grow[0:70, :], ident[0:70, 0:70]).then_inc(gcol_turned, 1)
            pe.wait_ge(qscale_made, 1)
            for i in range(2):
                kind = ("rel", "diff")[i]
                turn(nat, normed, TB * n_of(i, T_FFN1) + 1)
                ffn_phase(2 * i, c_ffn1(i), t_of(i, T_FFN1))
                turn(nat, normed, TB * n_of(i, T_MEM) + 1)
                pe.wait_ge(x_updated, 4 * i + 2)
                if i == 0:
                    pe.wait_ge(rel_loaded, 32)
                    for k in range(2):
                        ins = pe.transpose(ps[:, 7, 12 * k:12 * k + 12], rel_rows[0:12, 1 + k * P:1 + (k + 1) * P], ident[0:12, 0:12])
                    ins.then_inc(ext_turned, 1)
                project(g_kv(i), c_kv(i), 1, t_of(i, T_MEM))
                if i == 0:
                    pe.wait_ge(ext_made, 1)
                    for k in range(2):
                        ins = pe.matmul(ps[0:12, 7, :], ang[:, 0, 12 * k:12 * k + 12],
                                        qk_flat[:, 512 * k:512 * (k + 1)],
                                        start=k == 0, stop=k == 1)
                    ins.then_inc(ext_rows, 1)
                turn(nat, normed, TB * n_of(i, T_MIX) + 1)
                if i == 0:
                    pe.wait_ge(ext_copied, 1)
                project(g_in(i), c_in(i), 5, t_of(i, T_MIX))
                pe.wait_ge(heads_ready, 4 * (i + 1))
                turn_qk(i, kind)
                attend(u_layer(i), attention_groups(kind), kind, i)
                pe.wait_ge(o_made, u_layer(i) + 8)
                if i == 1:
                    turn(nat, sub_normed, 1)
                else:
                    turn(nat, o_made, u_layer(i) + 7)
                project(g_out(i), c_out(i), 2, t_of(i, T_O))
                turn(nat, normed, TB * n_of(i, T_FFN2) + 1)
                pe.wait_ge(proj_read, g_out(i) + 2)
                ffn_phase(2 * i + 1, c_ffn2(i), t_of(i, T_FFN2))
            turn(x, x_updated, 7)
            pe.wait_ge(rel_loaded, 64)
            pe.matmul(ps[0:8, 7, :], rel_rows[0:32, 0:8], qk_flat[0:32, 0:512],
                      start=True, stop=True).then_inc(ext_rows, 1)
            pe.wait_ge(ext_copied, 2)
            project(g_moba, c_moba, 6, t_moba)
            pe.wait_ge(proj_read, g_moba + 6)
            turn_qk(2, "moba")
            attend(u_moba, attention_groups("moba"), "moba", 2)
            turn(nat, o_made, u_moba + 3)
            project(g_moba_out, c_moba_out, 2, t_moba_o)
            turn(x, ln_rows, 1)
            pe.wait_ge(wr_ready, 1)
            pe.wait_ge(turn_lo, 4 * t_moe + 1)
            for k in range(KT):
                turned_tile(t_moe, k)
                w = wr2[:, k, :, :].rearrange("p a e -> p (a e)")
                pe.matmul(ps[0:2 * N_E, 0, 0:S], w, xT_hi[:, k, :], start=k == 0, stop=False)
                ins = pe.matmul(ps[0:2 * N_E, 0, 0:S], w, xT_lo[:, k, :], start=False, stop=k == KT - 1)
            ins.then_inc(logits_done, 1)
            pe.wait_ge(logits_copied, 1)
            for b in range(TB):
                o = S + b * N_E
                ins = pe.matmul(ps[:, 0, o:o + N_E], lgT[:, b * P:(b + 1) * P], fold_logits, start=True, stop=True)
            ins.then_inc(logits_folded, 1)
            pe.wait_ge(m_zero, 2)
            pe.wait_ge(xn_lo_made, 2)
            for bank in (4, 5, 6, 7, 2, 3):
                ins = pe.matmul(ps[:, bank, :], pickT[:, 0:P], xn_hi[:, 0, 0:512], start=True, stop=True)
            ins.then_inc(scattered, 1)
            pe.wait_ge(chosen_made, 1)
            counts = ps[:, 0, S + TB * N_E:S + (TB + 3) * N_E]
            pe.matmul(counts[:, 0:N_E], before, chosen[:, 0, :], start=True, stop=True)
            pe.matmul(counts[:, N_E:2 * N_E], ones, chosen[:, 0, :], start=True, stop=False)
            pe.matmul(counts[:, N_E:2 * N_E], before, chosen[:, 1, :], start=False, stop=True)
            pe.matmul(counts[:, 2 * N_E:3 * N_E], ones, chosen[:, 0, :], start=True, stop=False)
            pe.matmul(counts[:, 2 * N_E:3 * N_E], ones, chosen[:, 1, :], start=False, stop=True).then_inc(crowd_done, 1)

            def gather(bank, par):
                for k in range(KT):
                    o = ps[:, bank, k * SLOTS:(k + 1) * SLOTS]
                    for b in range(TB):
                        slots = pick[:, par, b, 0:SLOTS]
                        pe.matmul(o, xn_hi[:, b, k * P:(k + 1) * P], slots, start=b == 0, stop=False)
                        ins = pe.matmul(o, xn_lo[:, b, k * P:(k + 1) * P], slots, start=False, stop=b == 1)
                ins.then_inc(gathered, 1)

            def scatter():
                for b in range(TB):
                    for h in range(2):
                        o = ps[:, 4 + 2 * b + h, :]
                        l, r = pickT[:, b * P:(b + 1) * P], slice(h * 512, (h + 1) * 512)
                        pe.matmul(o, l, y_hi[:, r], start=False, stop=False, skip_group_check=True)
                        ins = pe.matmul(o, l, y_lo[:, r], start=False, stop=False, skip_group_check=True)
                return ins

            def bias(bank, col, par):
                pe.matmul(ps[:, bank, :], sel[:, par, :], bias_parts[:, col:col + 512], start=True, stop=False)

            def rows(src, c, bank, h, laps, stop):
                pe.wait_ge(lo_made, c + 1 + LAP * laps)
                hi, lo = cut_slot(c)
                for k in range(4):
                    w = slice(k * 512, (k + 1) * 512)
                    pe.matmul(ps[:, bank, :], src[:, 4 * h + k, :], hi[:, w], start=False, stop=False)
                    ins = pe.matmul(ps[:, bank, :], src[:, 4 * h + k, :], lo[:, w], start=False,
                                    stop=stop and k == 3)
                ins.then_inc(chunk_used, 1)

            def fold_half(e, half, bank):
                pe.wait_ge(h_read, 4 * e + 2 * half + 2)
                for up in range(2):
                    for k in range(4):
                        o = 256 * up + SLOTS * k
                        ins = pe.matmul(ps[:, bank, o:o + SLOTS], h_rows[:, half, up, k * P:(k + 1) * P], fold,
                                        start=True, stop=True)
                ins.then_inc(folded, 1)

            def expert(e, par, c, laps):
                g0 = 2 * par
                g1 = 2 - g0
                pe.wait_ge(xs_lo_made, e + 1)
                bias(g0, 0, par)
                rows(xs, c, g0, 0, laps, False)
                rows(xs, c + 1, g0, 1, laps, True)
                pe.wait_ge(y_lo_made, e + 1)
                scatter().then_inc(scattered, 1)
                bias(g0 + 1, D, par)
                rows(xs, c + 2, g0 + 1, 0, laps, False)
                rows(xs, c + 3, g0 + 1, 1, laps, True)
                bias(g1, 512, par)
                rows(xs, c + 4, g1, 0, laps, False)
                fold_half(e, 0, g0)
                for b in range(TB):
                    pe.transpose(ps[:, g0 + 1, b * P:(b + 1) * P], pick[:, par, b, :].bitcast(F32), ident[:])
                for b in range(TB):
                    ins = pe.matmul(ps[:, g0 + 1, S:S + 1], pick[:, par, b, :].bitcast(F32), gate[:, b, bass.ds(e, 1)],
                                    start=b == 0, stop=b == 1)
                ins.then_inc(pickT_turned, 1)
                rows(xs, c + 5, g1, 1, laps, True)
                bias(g1 + 1, D + 512, par)
                rows(xs, c + 6, g1 + 1, 0, laps, False)
                rows(xs, c + 7, g1 + 1, 1, laps, True)
                pe.wait_ge(m_lo_made, 2 * e + 1)
                bias(g0, 2 * D, par)
                rows(m, c + 8, g0, 0, laps, False)
                fold_half(e, 1, g1)
                pe.wait_ge(pickT_made, e + 1)
                pe.wait_ge(gate_made, e + 2)
                bias(g0 + 1, 2 * D + 512, par)
                rows(m, c + 9, g0 + 1, 0, laps, False)
                pe.wait_ge(picked, 2 * e + 4)
                gather(g1 + 1, 1 - par)
                pe.wait_ge(m_lo_made, 2 * e + 2)
                rows(m, c + 10, g0, 1, laps, True)
                rows(m, c + 11, g0 + 1, 1, laps, True)

            pe.wait_ge(picked, 2)
            gather(1, 0)

            def round_of_experts(r):
                with pe.Fori(0, N_E // 2) as it:
                    for par in range(2):
                        expert(2 * it + N_E * r + par, par, MOE_C0 + par * EXPERT_C, round_laps(r) + 4 * it)

            round_of_experts(0)
            pe.wait_ge(crowd_made, 1)
            more = pe.value_load(crowd_i[0:1, 0:1], min_val=0, max_val=ROUNDS - 1)
            with pe.If(more > 0):
                with pe.Fori(1, more + 1) as r:
                    round_of_experts(r)
            pe.wait_ge(y_lo_made, N_E * more + (N_E + 1))
            scatter().then_inc(last_scattered, 1)


NAMES = ["x", "mem", "positions", "ffn1_norm", "ffn1_w_gate", "ffn1_w_up", "ffn1_w_down", "mix_norm", "mem_norm",
         "w_in", "w_mem_kv", "mem_q_norm", "mem_k_norm", "w_out", "a_q_norm", "a_k_norm", "a_rel_bias",
         "b_q_norm", "b_k_norm", "b_lambda_q1", "b_lambda_k1", "b_lambda_q2", "b_lambda_k2", "b_subln",
         "ffn2_norm", "ffn2_w_gate", "ffn2_w_up", "ffn2_w_down", "rel_bias_2", "a_w_in_2", "a_w_out_2",
         "ln_g_2", "ln_b_2", "moe_w_router_2", "moe_b_router_2", "moe_w_gate_up_2", "moe_b_gate_up_2",
         "moe_w_down_2", "moe_b_down_2"]


def constants():
    f = np.float32
    m = np.arange(512)
    rel = np.clip(255 - m, -128, 128) + 128
    c_rel = np.zeros((P, 2, 512), f)
    for k in range(2):
        c_rel[:, k, :] = rel[None, :] == 1 + k * P + np.arange(P)[:, None]
    n = np.maximum(255 - m, 0)
    large = 16 + (np.log(np.maximum(n, 1).astype(f) / f(16)) / f(math.log(8)) * f(16)).astype(np.int32)
    bucket = np.where(n < 16, n, np.minimum(large, 31))
    c_t5 = (bucket[None, :] == np.arange(32)[:, None]).astype(f)
    masks = np.zeros((P, MASK_W), f)
    i = np.arange(P)
    masks[:, 0:P] = i[None, :] % SLOTS
    masks[:, P:2 * P] = i[:, None] < i[None, :]
    masks[:, 2 * P:3 * P] = 1
    masks[:, 3 * P:4 * P] = i[None, :] < SLOTS
    masks[:, 4 * P:4 * P + SLOTS] = i[:, None] % SLOTS == np.arange(SLOTS)[None, :]
    masks[0:2 * N_E, 4 * P + SLOTS:4 * P + SLOTS + N_E] = i[0:2 * N_E, None] % N_E == np.arange(N_E)[None, :]
    for e in range(34):
        for r in range(3):
            masks[32 * r + e % N_E, MASK_W - 34 + e] = 1
    return {"c_ident": np.eye(P, dtype=f), "c_flip": np.eye(P, dtype=f)[::-1].copy(), "c_rel": c_rel.reshape(P, 1024), "c_t5": c_t5, "c_masks": masks,
            "c_inv_freq": (f(1.0) / (f(10000.0) ** (np.arange(0, HD, 2, dtype=f) / f(HD)))).astype(f)}


def kernel(**inputs):
    import concourse.bacc as bacc
    from concourse.bass_utils import run_bass_kernel_spmd

    nc = bacc.Bacc("TRN2", target_bir_lowering=False, num_devices=1)
    arrays, aps = {}, {}
    for name, v in [(n, inputs[n]) for n in NAMES] + list(constants().items()):
        v = np.ascontiguousarray(v)
        arrays["in_" + name] = v
        aps[name] = nc.dram_tensor("in_" + name, v.shape, mybir.dt.from_np(v.dtype), kind="ExternalInput").ap()
    out = nc.dram_tensor("out", (1, S, D), F32, kind="ExternalOutput").ap()
    build(nc, aps, out)
    r = run_bass_kernel_spmd(nc, [arrays], core_ids=[0])
    return r.results[0]["out"]
```
